# Optimizing a Trainium2 kernel written in Bass

```python
import functools
import jax, jax.numpy as jnp
from jax import lax
import numpy as np

D_MODEL = 1024
BATCH = 1
SEQ = 1024
DEPTH = 1
DEC_BATCH = 8
DEC_SEQ = 4
PAST_LEN = 4096
PAGE_SIZE = 128

D_CONV = D_MODEL // 2
CONV_WIDTH = 3
N_HEADS = 8
HEAD_DIM = 64
D_ATTN = N_HEADS * HEAD_DIM
Q_BLOCK = 128
FORGET_BIAS_INIT = 3.0
N_MEM = 256
N_XHEADS = 4
XHEAD_DIM = 128
D_XATTN = N_XHEADS * XHEAD_DIM
N_GROUPS = 4
EXPERTS_PER_GROUP = 8
N_EXPERTS = N_GROUPS * EXPERTS_PER_GROUP
TOP_K = 2
D_EXPERT = D_MODEL // 2
ROW_BLOCK = 128
D_IN = 3 * D_CONV + 3 * D_ATTN + N_HEADS + 2 * D_MODEL
RMS_EPS = 1e-6

kernel_name = 'hybrid_conv_fox_hmoe_step'

def rms_norm(x, g):
    xf = x.astype(jnp.float32)
    y = xf * lax.rsqrt(jnp.mean(xf * xf, axis=-1, keepdims=True) + RMS_EPS)
    return (y * g.astype(jnp.float32)).astype(x.dtype)

def split_combined(z):
    sizes = (D_CONV, D_CONV, D_CONV, D_ATTN, D_ATTN, D_ATTN, N_HEADS, D_MODEL, D_MODEL)
    offs = [int(o) for o in np.cumsum(sizes)[:-1]]
    return jnp.split(z, offs, axis=-1)

def short_conv(u, prev, conv_w, conv_b):
    s = u.shape[1]
    ext = jnp.concatenate([prev.astype(u.dtype), u], axis=1)
    y = conv_b.astype(u.dtype)
    for j in range(CONV_WIDTH):
        y = y + conv_w[j] * ext[:, j:j + s]
    return y, ext[:, -(CONV_WIDTH - 1):]

def fox_prompt(q, k, v, logf):
    b, s = q.shape[:2]
    nb = s // Q_BLOCK
    scale = HEAD_DIM ** -0.5
    dcum = lax.cumsum(logf, axis=1)
    dk = dcum.transpose(0, 2, 1)
    kpos = jnp.arange(s)
    qb = q.reshape(b, nb, Q_BLOCK, N_HEADS, HEAD_DIM).transpose(1, 0, 2, 3, 4)
    db = dcum.reshape(b, nb, Q_BLOCK, N_HEADS).transpose(1, 0, 3, 2)

    def block(args):
        i, qi, di = args
        qpos = i * Q_BLOCK + jnp.arange(Q_BLOCK)
        sc = jnp.einsum('bqhd,bkhd->bhqk', qi, k, preferred_element_type=jnp.float32) * scale
        sc = sc + di[:, :, :, None] - dk[:, :, None, :]
        sc = jnp.where(kpos[None, :] <= qpos[:, None], sc, -jnp.inf)
        p = jax.nn.softmax(sc, axis=-1)
        return jnp.einsum('bhqk,bkhd->bqhd', p.astype(v.dtype), v)

    out = lax.map(block, (jnp.arange(nb), qb, db))
    return out.transpose(1, 0, 2, 3, 4).reshape(b, s, D_ATTN)

def fox_sample(q, k, v, logf, k_past, v_past, logf_past):
    b, s = q.shape[:2]
    scale = HEAD_DIM ** -0.5
    d_new = lax.cumsum(logf, axis=1).transpose(0, 2, 1)
    rev = (lax.cumsum(logf_past, axis=1, reverse=True) - logf_past).transpose(0, 2, 1)
    sp = jnp.einsum('bqhd,bkhd->bhqk', q, k_past, preferred_element_type=jnp.float32) * scale
    sp = sp + d_new[:, :, :, None] + rev[:, :, None, :]
    sn = jnp.einsum('bqhd,bkhd->bhqk', q, k, preferred_element_type=jnp.float32) * scale
    sn = sn + d_new[:, :, :, None] - d_new[:, :, None, :]
    causal = jnp.arange(s)[None, :] <= jnp.arange(s)[:, None]
    sn = jnp.where(causal, sn, -jnp.inf)
    p = jax.nn.softmax(jnp.concatenate([sp, sn], axis=-1), axis=-1)
    n_past = k_past.shape[1]
    out = (jnp.einsum('bhqk,bkhd->bqhd', p[..., :n_past].astype(v_past.dtype), v_past)
           + jnp.einsum('bhqk,bkhd->bqhd', p[..., n_past:].astype(v.dtype), v))
    return out.reshape(b, s, D_ATTN)

def token_mixer(xn, conv_prev, attend, w_in, b_forget, conv_w, conv_b, w_up_conv, w_up_attn, w_mix_out):
    b, s = xn.shape[:2]
    z = xn @ w_in
    cb, cc, cx, q, k, v, fz, g_conv, g_attn = split_combined(z)
    cy, conv_new = short_conv(cc * cx, conv_prev, conv_w, conv_b)
    y_conv = (cb * cy) @ w_up_conv
    logf = jax.nn.log_sigmoid(fz.astype(jnp.float32) + b_forget.astype(jnp.float32))
    kh = k.reshape(b, s, N_HEADS, HEAD_DIM)
    vh = v.reshape(b, s, N_HEADS, HEAD_DIM)
    y_attn = attend(q.reshape(b, s, N_HEADS, HEAD_DIM), kh, vh, logf) @ w_up_attn
    mixed = jax.nn.sigmoid(g_conv) * y_conv + jax.nn.sigmoid(g_attn) * y_attn
    return mixed @ w_mix_out, conv_new, kh, vh, logf

def memory_kv(mem, norm_mem, w_xk, w_xv):
    b, m = mem.shape[:2]
    mn = rms_norm(mem, norm_mem)
    return ((mn @ w_xk).reshape(b, m, N_XHEADS, XHEAD_DIM),
            (mn @ w_xv).reshape(b, m, N_XHEADS, XHEAD_DIM))

def cross_attention(xn, mem_k, mem_v, w_xq, w_xo):
    b, s = xn.shape[:2]
    q = (xn @ w_xq).reshape(b, s, N_XHEADS, XHEAD_DIM)
    sc = jnp.einsum('bqhd,bmhd->bhqm', q, mem_k, preferred_element_type=jnp.float32) * (XHEAD_DIM ** -0.5)
    p = jax.nn.softmax(sc, axis=-1).astype(mem_v.dtype)
    o = jnp.einsum('bhqm,bmhd->bqhd', p, mem_v).reshape(b, s, D_XATTN)
    return o @ w_xo

def hier_moe(x, w_rg, w_re, w_eg, w_eu, w_ed):
    shp = x.shape
    xt = x.reshape(-1, D_MODEL)
    t = xt.shape[0]
    xf = xt.astype(jnp.float32)
    p_group = jax.nn.softmax(xf @ w_rg.astype(jnp.float32), axis=-1)
    g_idx = jnp.argmax(p_group, axis=-1)
    p_g = jnp.take_along_axis(p_group, g_idx[:, None], axis=-1)
    logits_all = jnp.einsum('td,gde->tge', xf, w_re.astype(jnp.float32))
    logits_e = jnp.take_along_axis(logits_all, g_idx[:, None, None], axis=1)[:, 0]
    top_v, top_i = lax.top_k(logits_e, TOP_K)
    gate = jax.nn.softmax(top_v, axis=-1) * p_g
    eid = (g_idx[:, None] * EXPERTS_PER_GROUP + top_i).reshape(-1).astype(jnp.int32)
    tok = jnp.repeat(jnp.arange(t, dtype=jnp.int32), TOP_K)
    wt = gate.reshape(-1)
    order = jnp.argsort(eid)
    eid_s, tok_s, wt_s = eid[order], tok[order], wt[order]
    counts = jnp.bincount(eid, length=N_EXPERTS)
    padded = (counts + ROW_BLOCK - 1) // ROW_BLOCK * ROW_BLOCK
    start = jnp.cumsum(counts) - counts
    pend = jnp.cumsum(padded)
    pstart = pend - padded
    dest = pstart[eid_s] + (jnp.arange(t * TOP_K) - start[eid_s])
    n_blocks = -(-(t * TOP_K + N_EXPERTS * (ROW_BLOCK - 1)) // ROW_BLOCK)
    n_rows = n_blocks * ROW_BLOCK
    row_tok = jnp.full((n_rows,), t, jnp.int32).at[dest].set(tok_s)
    row_w = jnp.zeros((n_rows,), jnp.float32).at[dest].set(wt_s)
    blk_e = jnp.minimum(jnp.searchsorted(pend, jnp.arange(n_blocks) * ROW_BLOCK, side='right'), N_EXPERTS - 1)
    x_pad = jnp.concatenate([xt, jnp.zeros((1, D_MODEL), xt.dtype)], axis=0)
    xb = x_pad[row_tok].reshape(n_blocks, ROW_BLOCK, D_MODEL)

    def expert_block(args):
        xi, e = args
        h = jax.nn.silu(xi @ w_eg[e]) * (xi @ w_eu[e])
        return h @ w_ed[e]

    yb = lax.map(expert_block, (xb, blk_e)).reshape(n_rows, D_MODEL)
    yb = yb * row_w[:, None].astype(yb.dtype)
    out = jnp.zeros((t + 1, D_MODEL), yb.dtype).at[row_tok].add(yb)[:t]
    return out.reshape(shp).astype(x.dtype)

def trunk_layer(h, conv_prev, attend, mem_k, mem_v, norm_mix, w_in, b_forget, conv_w, conv_b,
                w_up_conv, w_up_attn, w_mix_out, norm_xattn, w_xq, w_xo, norm_ffn,
                w_rg, w_re, w_eg, w_eu, w_ed):
    mix, conv_new, k, v, logf = token_mixer(rms_norm(h, norm_mix), conv_prev, attend, w_in, b_forget,
                                            conv_w, conv_b, w_up_conv, w_up_attn, w_mix_out)
    h = h + mix
    h = h + cross_attention(rms_norm(h, norm_xattn), mem_k, mem_v, w_xq, w_xo)
    h = h + hier_moe(rms_norm(h, norm_ffn), w_rg, w_re, w_eg, w_eu, w_ed)
    return h, conv_new, k, v, logf

def _dense(key, shape, fan_in):
    return jax.random.normal(key, shape, jnp.float32) * (fan_in ** -0.5)

def setup_inputs(seed: int = 0) -> dict:
    key = jax.random.key(seed)
    ks = jax.random.split(key, 32)
    n_pages = PAST_LEN // PAGE_SIZE
    n_used = DEC_BATCH * n_pages
    n_pool = n_used + (n_used + 3) // 4
    page_table = jax.random.permutation(ks[0], n_pool)[:n_used].reshape(DEC_BATCH, n_pages).astype(jnp.int32)
    nrm = lambda k, shp: jax.random.normal(k, shp, jnp.float32)
    gain = lambda k: 1.0 + 0.02 * nrm(k, (DEPTH, D_MODEL))
    return {
        'x_prompt': nrm(ks[1], (BATCH, SEQ, D_MODEL)),
        'x_sample': nrm(ks[2], (DEC_BATCH, DEC_SEQ, D_MODEL)),
        'cache_k': nrm(ks[3], (DEPTH, n_pool, PAGE_SIZE, N_HEADS, HEAD_DIM)),
        'cache_v': nrm(ks[4], (DEPTH, n_pool, PAGE_SIZE, N_HEADS, HEAD_DIM)),
        'cache_logf': jax.nn.log_sigmoid(FORGET_BIAS_INIT + 0.5 * nrm(ks[5], (DEPTH, n_pool, PAGE_SIZE, N_HEADS))),
        'cache_mem_k': nrm(ks[6], (DEPTH, DEC_BATCH, N_MEM, N_XHEADS, XHEAD_DIM)),
        'cache_mem_v': nrm(ks[7], (DEPTH, DEC_BATCH, N_MEM, N_XHEADS, XHEAD_DIM)),
        'state_conv': nrm(ks[8], (DEPTH, DEC_BATCH, CONV_WIDTH - 1, D_CONV)),
        'page_table': page_table,
        'mem_prompt': nrm(ks[9], (BATCH, N_MEM, D_MODEL)),
        'norm_mix': gain(ks[10]),
        'w_in': _dense(ks[11], (DEPTH, D_MODEL, D_IN), D_MODEL),
        'b_forget': FORGET_BIAS_INIT + 0.1 * nrm(ks[12], (DEPTH, N_HEADS)),
        'conv_w': _dense(ks[13], (DEPTH, CONV_WIDTH, D_CONV), CONV_WIDTH),
        'conv_b': 0.01 * nrm(ks[14], (DEPTH, D_CONV)),
        'w_up_conv': _dense(ks[15], (DEPTH, D_CONV, D_MODEL), D_CONV),
        'w_up_attn': _dense(ks[16], (DEPTH, D_ATTN, D_MODEL), D_ATTN),
        'w_mix_out': _dense(ks[17], (DEPTH, D_MODEL, D_MODEL), D_MODEL),
        'norm_xattn': gain(ks[18]),
        'norm_mem': gain(ks[19]),
        'w_xq': _dense(ks[20], (DEPTH, D_MODEL, D_XATTN), D_MODEL),
        'w_xk': _dense(ks[21], (DEPTH, D_MODEL, D_XATTN), D_MODEL),
        'w_xv': _dense(ks[22], (DEPTH, D_MODEL, D_XATTN), D_MODEL),
        'w_xo': _dense(ks[23], (DEPTH, D_XATTN, D_MODEL), D_XATTN),
        'norm_ffn': gain(ks[24]),
        'w_router_group': _dense(ks[25], (DEPTH, D_MODEL, N_GROUPS), D_MODEL),
        'w_router_expert': _dense(ks[26], (DEPTH, N_GROUPS, D_MODEL, EXPERTS_PER_GROUP), D_MODEL),
        'w_expert_gate': _dense(ks[27], (DEPTH, N_EXPERTS, D_MODEL, D_EXPERT), D_MODEL),
        'w_expert_up': _dense(ks[28], (DEPTH, N_EXPERTS, D_MODEL, D_EXPERT), D_MODEL),
        'w_expert_down': _dense(ks[29], (DEPTH, N_EXPERTS, D_EXPERT, D_MODEL), D_EXPERT),
        'norm_final': 1.0 + 0.02 * nrm(ks[30], (D_MODEL,)),
    }

def reference(x_prompt, x_sample, cache_k, cache_v, cache_logf, cache_mem_k, cache_mem_v, state_conv,
              page_table, mem_prompt, norm_mix, w_in, b_forget, conv_w, conv_b, w_up_conv, w_up_attn,
              w_mix_out, norm_xattn, norm_mem, w_xq, w_xk, w_xv, w_xo, norm_ffn, w_router_group,
              w_router_expert, w_expert_gate, w_expert_up, w_expert_down, norm_final):
    db = x_sample.shape[0]
    past_len = page_table.shape[1] * PAGE_SIZE
    hp, hs = x_prompt, x_sample
    conv_p, k_p, v_p, lf_p, mk_p, mv_p = [], [], [], [], [], []
    conv_s, k_s, v_s, lf_s = [], [], [], []
    for l in range(DEPTH):
        shared = (norm_mix[l], w_in[l], b_forget[l], conv_w[l], conv_b[l], w_up_conv[l], w_up_attn[l],
                  w_mix_out[l], norm_xattn[l], w_xq[l], w_xo[l], norm_ffn[l], w_router_group[l],
                  w_router_expert[l], w_expert_gate[l], w_expert_up[l], w_expert_down[l])
        mem_k, mem_v = memory_kv(mem_prompt, norm_mem[l], w_xk[l], w_xv[l])
        conv0 = jnp.zeros((hp.shape[0], CONV_WIDTH - 1, D_CONV), hp.dtype)
        hp, c, k, v, lf = trunk_layer(hp, conv0, fox_prompt, mem_k, mem_v, *shared)
        conv_p.append(c); k_p.append(k); v_p.append(v); lf_p.append(lf); mk_p.append(mem_k); mv_p.append(mem_v)
        k_past = cache_k[l][page_table].reshape(db, past_len, N_HEADS, HEAD_DIM)
        v_past = cache_v[l][page_table].reshape(db, past_len, N_HEADS, HEAD_DIM)
        lf_past = cache_logf[l][page_table].reshape(db, past_len, N_HEADS).astype(jnp.float32)
        attend_s = functools.partial(fox_sample, k_past=k_past, v_past=v_past, logf_past=lf_past)
        hs, c, k, v, lf = trunk_layer(hs, state_conv[l], attend_s, cache_mem_k[l], cache_mem_v[l], *shared)
        conv_s.append(c); k_s.append(k); v_s.append(v); lf_s.append(lf)
    y_prompt = rms_norm(hp, norm_final)
    y_sample = rms_norm(hs, norm_final)
    return (y_prompt, y_sample,
            jnp.stack(conv_p), jnp.stack(k_p), jnp.stack(v_p), jnp.stack(lf_p), jnp.stack(mk_p), jnp.stack(mv_p),
            jnp.stack(conv_s), jnp.stack(k_s), jnp.stack(v_s), jnp.stack(lf_s))


_drawn_inputs = setup_inputs


def setup_inputs(seed=0):
    import zlib

    import numpy as np

    out = dict(_drawn_inputs(seed))
    spreads = {}
    factors = {'norm_xattn': 7.596,
     'norm_mem': 2.837,
     'norm_final': 7.585,
     'cache_logf': 3.511,
     'conv_b': 2.735}
    for name, (base, spread) in spreads.items():
        noise = np.random.default_rng([zlib.crc32(name.encode()), seed]).standard_normal(out[name].shape)
        drawn = base * np.exp(spread * noise) if base else spread * noise
        out[name] = __import__('jax').numpy.asarray(drawn.astype(out[name].dtype))
    for name, factor in factors.items():
        out[name] = (out[name] * factor).astype(out[name].dtype)
    return out
```

```python
from contextlib import ExitStack

import numpy as np

import concourse.bass as bass
from concourse import mybir

F32 = mybir.dt.float32
BF16 = mybir.dt.bfloat16
I32 = mybir.dt.int32
U32 = mybir.dt.uint32
ALU = mybir.AluOpType
ACT = mybir.ActivationFunctionType
AX = mybir.AxisListType.X
ds = bass.ds

P = 128
D = 1024
KD = D // P
SEQ = 1024
DB, DS = 8, 4
NS = DB * DS
NT = SEQ + NS
PT = SEQ // P
TILES = PT + 1
DC = D // 2
KC = DC // P
H, HD = 8, 64
DA = H * HD
QH = DS * H
PAST, PAGE = 4096, 128
PAGES = PAST // PAGE
NMEM = 256
XH, XD = 4, 128
NG, EG = 4, 8
NE = NG * EG
DE = D // 2
BLK = 128
MAXB = -(-(NT * 2 + NE * (BLK - 1)) // BLK)
EPS = 1e-6
NEG = -1e30
COLS = 3
NC_ = NT // COLS
HALO = 2
UW = HALO + SEQ + DB * (HALO + DS)
O_CB, O_CC, O_CX, O_Q, O_K, O_V = (n * 512 for n in range(6))
O_FZ = 6 * 512
O_GA = O_FZ + H
O_GB = O_GA + D
RING_ORDER = ["cc", "cx", "cb", "q", "k", "v", "xk", "xv", "ga0", "gb0", "ga1", "gb1", "mo0", "mo1", "xq", "xo"]


def rows_of(i):
    return P if i < PT else NS


def cols_of(n):
    return slice(n * NC_, (n + 1) * NC_)


C_ID, C_CAUSAL, C_BEFORE, C_PAGES, C_MASK = 0, P, 2 * P, 3 * P, 4 * P
C_DIAG = C_MASK + DB * NS
C_SELQ = C_DIAG + DA
C_GRP = C_SELQ + DS
C_EXP = C_GRP + NE
C_BLK = C_EXP + NE
C_TOK = C_BLK + MAXB
CW = C_TOK + TILES


def constants():
    c = np.zeros((P, CW), np.float32)
    r = np.arange(P)
    c[:, C_ID:C_ID + P] = np.eye(P)
    c[:, C_CAUSAL:C_CAUSAL + P] = np.where(r[None, :] <= r[:, None], 0.0, NEG)
    c[:, C_BEFORE:C_BEFORE + P] = r[:, None] < r[None, :]
    g, j = r // PAGES, r % PAGES
    c[:, C_PAGES:C_PAGES + P] = (g[:, None] == g[None, :]) & (j[:, None] > j[None, :])
    qh, s = np.arange(DS * H), np.arange(NS)
    own = (s[None, None, :] // DS == np.arange(DB)[None, :, None]) & (s[None, None, :] % DS <= (qh // H)[:, None, None])
    c[:QH, C_MASK:C_MASK + DB * NS] = np.where(own, 0.0, NEG).reshape(QH, -1)
    c[:QH, C_DIAG:C_DIAG + DA] = (qh % H)[:, None] == (np.arange(DA) // HD)[None, :]
    c[:QH, C_SELQ:C_SELQ + DS] = (qh // H)[:, None] == np.arange(DS)[None, :]
    c[:, C_GRP:C_GRP + NE] = np.arange(NE) // EG
    c[:, C_EXP:C_EXP + NE] = np.arange(NE)
    c[:, C_BLK:C_BLK + MAXB] = np.arange(MAXB)
    c[:, C_TOK:C_TOK + TILES] = r[:, None] + P * np.arange(TILES)[None, :]
    return c


class Results:

    def __init__(self, full, by_act, by_dve):
        self.full, self.by = full, {"act": by_act, "dve": by_dve}
        self.order, self.index, self.count = [], {}, {"act": 0, "dve": 0}

    def add(self, reader, *tag):
        self.count[reader] += 1
        self.index[tag] = len(self.order)
        self.order.append((reader, self.count[reader]))

    def bank(self, *tag):
        return self.index[tag] % 8

    def pe_free(self, pe, *tag):
        e = self.index[tag] - 8
        if e >= 0:
            reader, n = self.order[e]
            pe.wait_ge(self.by[reader], n)

    def made(self, eng, *tag):
        eng.wait_ge(self.full, self.index[tag] + 1)

    def read(self, eng, *tag):
        reader, n = self.order[self.index[tag]]
        eng.wait_ge(self.by[reader], n)


def build_program(nc, t):
    ctx = ExitStack()
    with ctx:
        top = [16512]

        def area(nbytes):
            at = top[0]
            top[0] += -(-nbytes // 32) * 32
            assert top[0] <= 229344, top[0]
            return at

        def at(name, shape, offset, dt=F32):
            return nc.alloc_sbuf_tensor_at(name, shape, dt, offset=offset).ap()

        def new(name, shape, dt=F32):
            n = 4 if dt != BF16 else 2
            for s in shape[1:]:
                n *= s
            return at(name, shape, area(n), dt)

        def sem(name):
            return ctx.enter_context(nc.semaphore(name))

        consts = new("consts", [P, CW])
        ident = consts[:, C_ID:C_ID + P]
        identb = new("identb", [P, P], BF16)
        causalb = new("causalb", [P, P], BF16)
        gain = new("gain", [P, D])
        ss = new("ss", [P, 6, TILES])
        convp = new("convp", [P, 4 * KC + 1])
        ones = new("ones", [P, 1])
        pages = new("pages", [1, DB * PAGES], I32)
        beforeb = new("beforeb", [P, P], BF16)
        onesb = new("onesb", [P, P], BF16)
        wgt = new("wgt", [P, 2, TILES])
        dest = new("dest", [P, 2, TILES], I32)
        pairs = new("pairs", [P, 2, TILES, 2], I32)
        blke = new("blke", [1, MAXB + 1], I32)
        nblk = new("nblk", [1, 1], I32)
        rowi = new("rowi", [P, 1], I32)
        outi = new("outi", [P, 1], I32)
        memKT = new("memKT", [P, XH, NMEM])
        memV = new("memV", [P, 2, XH * XD])
        qs = new("qs", [P, KC, NS])
        ks = new("ks", [P, KC, NS])
        a_norm = area(KD * NT * 4)
        xnT = at("xnT", [P, KD, NT], a_norm)
        a_ring = area(2 * KD * 512 * 4)
        ring = [at(f"ring{s}", [P, KD, 512], a_ring + s * KD * 512 * 4) for s in range(2)]
        a_v = area(TILES * DA * 4)
        a_u = area(KC * UW * 4)
        a_o = area(KC * NT * 4)
        vtok = at("vtok", [P, TILES, DA], a_v)
        uT = at("uT", [P, KC, UW], a_u)
        cyT = at("cyT", [P, KC, NT], a_o)
        oT = at("oT", [P, KC, NT], a_u)
        resid = at("resid", [P, TILES, D], a_v)
        a_qk = area(2 * KC * NT * 4)
        qT = at("qT", [P, KC, NT], a_qk)
        kT = at("kT", [P, KC, NT], a_qk + KC * NT * 4)
        mixT = at("mixT", [P, KD, NT], a_qk)
        w = top[0]
        xs = [at(f"xs{p}", [P, D], w + p * 4096) for p in range(2)]
        junk = at("junk", [P, D], w + 2 * 4096)
        mem = at("mem", [P, 2, D], w + 3 * 4096)
        memT = at("memT", [P, KD, NMEM], w + 5 * 4096)
        stage = [at(f"stage{p}", [P, 512], w + 7 * 4096 + p * 2048) for p in range(2)]
        wfz = at("wfz", [P, KD, H], w + 8 * 4096)
        halo = at("halo", [2 * DB, DC], w + 8 * 4096 + 256)
        tailT = at("tailT", [P, KC, 2 + 2 * DB], w + 8 * 4096 + 2304)
        tail = at("tail", [2 + 2 * DB, DC], w + 8 * 4096 + 2656)
        lfo = at("lfo", [P, TILES, H], w + 8 * 4096 + 4704)
        lf = at("lf", [H, 4, NT], a_u)
        assert w + 8 * 4096 + 4992 <= 229376

        ps = [ctx.enter_context(nc.psum_tensor(f"ps{n}", [P, 1024], F32)) for n in range(4)]

        def bank(n):
            return ps[n // 2][:, (n % 2) * 512:(n % 2) * 512 + 512]

        prob = [at(f"prob{p}", [P, SEQ], w + p * 4096) for p in range(2)]
        probT = [at(f"probT{p}", [P, PT, P], w + (2 + p) * 4096) for p in range(2)]
        qz = [at(f"qz{p}", [P, SEQ], w + (4 + p) * 4096) for p in range(2)]
        negk = [at(f"negk{p}", [P, SEQ], w + (6 + p) * 4096) for p in range(2)]
        pair = at("pair", [P, PT, P], w + 8 * 4096)
        fstat = at("fstat", [P, 4, 4], w + 9 * 4096)
        past = at("past", [P, 2, PAGE * H], a_qk)
        after = at("after", [P, 2, H, PAGE], a_qk + 8192)
        ptot = at("ptot", [P, 2, H], a_qk + 16384)
        pgi = at("pgi", [P, 2], a_qk + 16384 + 64, I32)
        kpage = [at(f"kpage{s}", [P, 4, DA], a_qk + s * 8192) for s in range(2)]
        kpT = [at(f"kpT{s}", [P, KC, 512], a_qk + 16384 + s * 8192) for s in range(2)]
        vpage = [at(f"vpage{s}", [P, 4, DA], a_ring + s * 8192) for s in range(4)]
        rev = at("rev", [QH, PAST], a_v)
        sprob = at("sprob", [QH, PAST + NS], w)
        w2 = w + (PAST + NS) * 4
        sprobT = at("sprobT", [P, PAGES, QH], w2)
        snewT = at("snewT", [NS, QH], w2 + 4096)
        own = at("own", [QH, DA], w2 + 4224)
        qb = at("qb", [P, KC * (QH + 2)], w2 + 6272)
        nbias = at("nbias", [QH, DB, NS], w2 + 6848)
        nd = at("nd", [QH, NS], w2 + 7872)
        nb = at("nb", [QH, NS], w2 + 8128)
        sstat = at("sstat", [QH, 24], w2 + 8000)

        upc = at("upc", [P, KC, D], a_v)
        upa = at("upa", [P, KC, D], w)
        gate = [[at(f"gate{m}{p}", [P, NC_], w2 + (2 * m + p) * NC_ * 4) for p in range(2)] for m in range(2)]
        xr = [at(f"xr{p}", [P, D], w2 + 8448 + p * 4096) for p in range(2)]
        a_x = a_v + TILES * D * 4
        assert a_x + 15600 <= a_qk
        q2T = at("q2T", [P, XH, NT], a_qk)
        o2T = at("o2T", [P, XH, NT], a_qk + XH * NT * 4)
        xp = [at(f"xp{p}", [P, XH, NMEM], w + p * 4096) for p in range(2)]
        xpT = [at(f"xpT{p}", [P, 2 * XH, P], w + (2 + p) * 4096) for p in range(2)]
        ck = [at(f"ck{p}", [P, 2, XH * XD], w + (4 + p) * 4096) for p in range(2)]
        ckT = [at(f"ckT{p}", [P, XH, NMEM], w + (6 + p) * 4096) for p in range(2)]
        cv = at("cv", [P, DB, 2, XH * XD], a_norm)
        qp = at("qp", [P, DB * XH * 32], a_x)
        sp_ = at("sp_", [P, NMEM], a_x + 4096)
        spT = at("spT", [P, 2, P], a_x + 5120)
        xstat = at("xstat", [P, 2, 16], a_x + 6144)
        sxstat = at("sxstat", [P, 4], a_x + 6272)
        wr = at("wr", [P, KD, NG + NE], a_x + 6304)
        a_r = a_x + 6304 + 1152
        lgT = at("lgT", [NG + NE, NT], a_r)
        lg = at("lg", [P, TILES, NG + NE], a_r + 4224)
        t4 = [at(f"t4_{n}", [P, TILES, NG], w + 8 * 4096 + n * 160) for n in range(3)]
        t32 = [at(f"t32_{n}", [P, TILES, NE], w + 2 * 4096 + n * 1152) for n in range(7)]
        t1 = at("t1", [P, 16, TILES], w + 8 * 4096 + 512)
        cnt = at("cnt", [P, 4, NE], w + 8 * 4096 + 1120)
        cnti = at("cnti", [P, NE], w + 8 * 4096 + 1632, I32)
        hot = at("hot", [P, TILES, NE], w + 8 * 4096 + 1760, BF16)
        empty = at("empty", [P, MAXB + 1, 2], w + 8 * 4096 + 2336, I32)
        bcmp = at("bcmp", [1, MAXB, NE], w)
        bsum = at("bsum", [1, MAXB], w + MAXB * NE * 4)
        wg, wu = ring
        wd = at("wd", [P, DE // P, D], a_qk)
        xg = at("xg", [P, D], w)
        xgT = at("xgT", [P, KD, BLK], w + 4096)
        sg = at("sg", [P, DE], w + 8192)
        hh = at("hh", [P, DE], w + 8192 + 2048)
        hT = at("hT", [P, DE // P, BLK], w + 8192 + 4096)
        yb = at("yb", [P, D], w + 8192 + 6144)
        yy = [[at(f"yy{k}{p}", [P, D], a_norm + (2 * k + p) * 4096) for p in range(2)] for k in range(2)]

        x3_d = nc.dram_tensor("x3_d", (NT, D), F32, kind="Internal").ap()
        row_d = nc.dram_tensor("row_d", ((MAXB + 1) * BLK, 2), I32, kind="Internal").ap()
        y_d = nc.dram_tensor("y_d", (2 * NT + 1, D), F32, kind="Internal").ap()
        rev_d = nc.dram_tensor("rev_d", (DB, H, PAST), F32, kind="Internal").ap()
        neg_d = nc.dram_tensor("neg_d", (H, NT), F32, kind="Internal").ap()

        consts_in, gain_in, gain_used = sem("consts_in"), sem("gain_in"), sem("gain_used")
        x_in = [sem(f"x_in{i}") for i in range(TILES)]
        mem_in, halo_in, wfz_in = sem("mem_in"), sem("halo_in"), sem("wfz_in")
        ring_in = [sem(f"ring_in{s}") for s in range(2)]
        passed = sem("passed")
        made_up = sem("made_up")
        tail_got, abs_ready, ln_ready, lf_ready, neg_ready = (
            sem(n) for n in ("tail_got", "abs_ready", "ln_ready", "lf_ready", "neg_ready"))
        stage_stored = [sem(f"stage_stored{p}") for p in range(2)]
        neg_stored, stored = sem("neg_stored"), sem("stored")
        past_in, pgi_in, totals_ready, after_ready, rev_stored = (
            sem(n) for n in ("past_in", "pgi_in", "totals_ready", "after_ready", "rev_stored"))
        negk_in = [sem(f"negk_in{p}") for p in range(2)]
        qz_cleared = sem("qz_cleared")
        qz_ready = sem("qz_ready")
        fs_full, fs_max, fs_exp = sem("fs_full"), sem("fs_max"), sem("fs_exp")
        ft_full, ft_act, ft_dve = sem("ft_full"), sem("ft_act"), sem("ft_dve")
        fo_full, fo_read = sem("fo_full"), sem("fo_read")
        fp_full, fp_read = sem("fp_full"), sem("fp_read")
        k_in = [sem(f"k_in{s}") for s in range(2)]
        v_in = [sem(f"v_in{s}") for s in range(4)]
        rev_in, nd_in, nbias_ready, qb_ready = sem("rev_in"), sem("nd_in"), sem("nbias_ready"), sem("qb_ready")
        v_used = sem("v_used")
        kt_full, kt_act, kt_dve = sem("kt_full"), sem("kt_act"), sem("kt_dve")
        sc_full, sc_read = sem("sc_full"), sem("sc_read")
        s_max, s_exp = sem("s_max"), sem("s_exp")
        t2_full, t2_act, t2_dve = sem("t2_full"), sem("t2_act"), sem("t2_dve")
        so_full, so_read, sx_full, sx_read = sem("so_full"), sem("so_read"), sem("sx_full"), sem("sx_read")
        upc_in, upa_in, mixed = sem("upc_in"), sem("upa_in"), sem("mixed")
        xr_in = [sem(f"xr_in{p}") for p in range(2)]
        ck_in = [sem(f"ck_in{p}") for p in range(2)]
        cv_in, qp_ready = sem("cv_in"), sem("qp_ready")
        x_max, x_exp, x_norm = sem("x_max"), sem("x_exp"), sem("x_norm")
        sx_max, sx_exp, sx_norm = sem("sx_max"), sem("sx_exp"), sem("sx_norm")
        wr_in, empty_ready, empty_stored, g_sub, g_exp, e_sub, e_exp, hot_ready = (
            sem(n) for n in ("wr_in", "empty_ready", "empty_stored", "g_sub", "g_exp", "e_sub", "e_exp", "hot_ready"))
        x3_stored = [sem(f"x3_stored{p}") for p in range(2)]
        routed, rows_stored = sem("routed"), sem("rows_stored")
        wg_in, wu_in, wd_in, rowi_in, outi_in, xg_in, y_stored = (
            sem(n) for n in ("wg_in", "wu_in", "wd_in", "rowi_in", "outi_in", "xg_in", "y_stored"))
        y_free = sem("y_free")
        xt_full, xt_read, g_full, sg_ready, u_full, h_ready, ht_full, ht_read, d_full, d_read = (
            sem(n) for n in ("xt_full", "xt_read", "g_full", "sg_ready", "u_full", "h_ready", "ht_full", "ht_read",
                             "d_full", "d_read"))
        y_in = [sem(f"y_in{p}") for p in range(2)]
        summed = sem("summed")
        y_out = [sem(f"y_out{p}") for p in range(2)]
        R = Results(sem("result_full"), sem("read_by_act"), sem("read_by_dve"))

        FN = [(f, n) for f in range(KC) for n in range(COLS)]
        for i in range(TILES):
            R.add("act", "nmix", i, 0), R.add("act", "nmix", i, 1)
        R.add("dve", "later", 0), R.add("dve", "later", 1)
        R.add("dve", "halo")
        for name, reader in (("cc", "act"), ("cx", "dve"), ("cb", "dve")):
            for f, n in FN:
                R.add(reader, name, f, n)
        R.add("dve", "tail")
        for name in "qk":
            for f, n in FN:
                R.add("act", name, f, n)
        for n in range(COLS):
            R.add("dve", "fz", n)
        for i in range(TILES):
            R.add("act", "v", i)
        for i in range(TILES):
            R.add("act", "kout", i)
        R.add("dve", "lf")
        for i in range(2):
            R.add("act", "nmem", i, 0), R.add("act", "nmem", i, 1)
        for name in ("mk", "mkT", "mv"):
            for i in range(2):
                R.add("act", name, i)

        FN8 = [(f, n) for f in range(KD) for n in range(COLS)]
        for f, n in FN8:
            R.add("act", "ga", f, n), R.add("dve", "yc", f, n), R.add("act", "gb", f, n), R.add("dve", "ya", f, n)
        for i in range(TILES):
            R.add("dve", "mo", i, 0), R.add("dve", "mo", i, 1)
        for i in range(TILES):
            R.add("act", "nxat", i, 0), R.add("act", "nxat", i, 1)
        for f, n in FN:
            R.add("act", "xq", f, n)
        R.add("act", "xs", 0, 0), R.add("act", "xs", 0, 1)
        for i in range(PT):
            if i + 1 < PT:
                R.add("act", "xs", i + 1, 0), R.add("act", "xs", i + 1, 1)
            R.add("act", "xt", i, 0), R.add("dve", "xt", i, 1)
            if i:
                R.add("dve", "xo", i - 1)
        R.add("dve", "xo", PT - 1)
        for b in range(DB):
            R.add("act", "ckT", b, 0), R.add("dve", "ckT", b, 1)
            if b % 2:
                R.add("dve", "ss", b // 2)
        R.add("act", "spT")
        R.add("act", "so")
        for i in range(TILES):
            R.add("dve", "h2", i, 0), R.add("dve", "h2", i, 1)
        for i in range(TILES):
            R.add("act", "nffn", i, 0), R.add("act", "nffn", i, 1)
        for n in range(COLS):
            R.add("act", "lgT", n)
        R.add("dve", "lg")
        R.add("dve", "rank")

        class Norm:

            def __init__(self, name, slot, n):
                self.name, self.stat, self.n = name, ss[:, slot, 0:n], n
                self.rows = (lambda i: P) if n < TILES else rows_of
                self.squared = sem(name + "_squared")
                self.mean = sem(name + "_mean")
                self.root = sem(name + "_root")
                self.scaled = sem(name + "_scaled")

            def act_stats(self, act, src, wait_src):
                for i in range(self.n):
                    r = self.rows(i)
                    wait_src(i)
                    if i:
                        act.drain()
                    nc.scalar.activation(junk[0:r, :], src(i)[0:r, :], ACT.Square,
                                         accum_out=self.stat[0:r, i:i + 1]).then_inc(self.squared, 1)
                act.wait_ge(self.mean, 1)
                nc.scalar.activation(self.stat, self.stat, ACT.Sqrt).then_inc(self.root, 1)

            def dve_scale(self, dve, src, gain_load, free=None):
                free = free or (lambda i: R.made(dve, self.name, i, 1))
                dve.wait_ge(self.squared, self.n)
                nc.vector.tensor_scalar(self.stat, self.stat, 1.0 / D, EPS, ALU.mult, ALU.add).then_inc(self.mean, 1)
                dve.wait_ge(self.root, 1)
                nc.vector.reciprocal(self.stat, self.stat)
                dve.drain()
                dve.wait_ge(gain_in, 16 * gain_load)
                for i in range(self.n):
                    r = self.rows(i)
                    if i >= 2:
                        free(i - 2)
                    nc.vector.scalar_tensor_tensor(xs[i % 2][0:r, :], src(i)[0:r, :], self.stat[0:r, i:i + 1],
                                                   gain[0:r, :], ALU.mult, ALU.mult).then_inc(self.scaled, 1)
                dve.drain()
                dve.sem_inc(gain_used, 1)

            def pe_turn(self, pe):
                for i in range(self.n):
                    r = self.rows(i)
                    pe.wait_ge(self.scaled, i + 1)
                    for half in range(2):
                        R.pe_free(pe, self.name, i, half)
                        out = bank(R.bank(self.name, i, half))
                        for c in range(4):
                            f = (half * 4 + c) * P
                            last = nc.tensor.transpose(out[:, c * P:c * P + r], xs[i % 2][0:r, f:f + P], ident[0:r, 0:r])
                        last.then_inc(R.full, 1)

            def act_copy(self, act, dst):
                for i in range(self.n):
                    r = self.rows(i)
                    for half in range(2):
                        R.made(act, self.name, i, half)
                        src = bank(R.bank(self.name, i, half)).rearrange("p (c x) -> p c x", c=4)[:, :, 0:r]
                        nc.scalar.activation(dst[:, half * 4:half * 4 + 4, i * P:i * P + r], src,
                                             ACT.Copy).then_inc(R.by["act"], 1)

        n_mix, n_mem = Norm("nmix", 0, TILES), Norm("nmem", 1, 2)
        n_xat, n_ffn, n_fin = Norm("nxat", 2, TILES), Norm("nffn", 3, TILES), Norm("nfin", 4, TILES)

        ring_xo = ring[1].rearrange("p k n -> p (k n)").rearrange("p (k n) -> p k n", k=KC)
        N_POOL = t["cache_k"].shape[0]

        def units():
            return [(u, u // PT, u % PT) for u in range(2 * PT)]

        def groups(u):
            i, first = u % PT, (u // PT) * 12 + (u % PT if u % PT < 4 else 2 * (u % PT) - 4)
            return [(first + g, 4 * g, min(4, i + 1 - 4 * g)) for g in range(1 if i < 4 else 2)]

        def w3(ap, c0, width=512):
            return ap.rearrange("(k p) n -> p k n", p=P)[:, :, c0:c0 + width]

        LOADS = {"cc": (w3(t["w_in"], O_CC), None), "cx": (w3(t["w_in"], O_CX), None),
                 "cb": (w3(t["w_in"], O_CB), ("cc", KC - 1, COLS - 1)), "q": (w3(t["w_in"], O_Q), ("cx", KC - 1, COLS - 1)),
                 "k": (w3(t["w_in"], O_K), ("cb", KC - 1, COLS - 1)), "v": (w3(t["w_in"], O_V), ("q", KC - 1, COLS - 1)),
                 "xk": (w3(t["w_xk"], 0), ("k", KC - 1, COLS - 1)), "xv": (w3(t["w_xv"], 0), ("v", TILES - 1)),
                 "ga0": (w3(t["w_in"], O_GA), None), "gb0": (w3(t["w_in"], O_GB), None),
                 "ga1": (w3(t["w_in"], O_GA + 512), ("ga", 3, COLS - 1)), "gb1": (w3(t["w_in"], O_GB + 512), ("gb", 3, COLS - 1)),
                 "mo0": (w3(t["w_mix_out"], 0), ("ga", 7, COLS - 1)), "mo1": (w3(t["w_mix_out"], 512), ("gb", 7, COLS - 1)),
                 "xq": (w3(t["w_xq"], 0), ("mo", TILES - 1, 0)), "xo": (w3(t["w_xo"], 0, D), ("mo", TILES - 1, 1))}

        def ring_load(sp, name):
            n = RING_ORDER.index(name)
            src, after = LOADS[name]
            if after is not None:
                R.made(sp, *after)
            dst = ring[n % 2] if src.shape[1] == KD else ring_xo
            sp.dma_start(dst, src).then_inc(ring_in[n % 2], 16)

        def ring_slot(pe, name):
            n = RING_ORDER.index(name)
            pe.wait_ge(ring_in[n % 2], 16 * (n // 2 + 1))
            return ring[n % 2]

        def samples(row):
            return row[:, HALO + SEQ:UW].rearrange("p (b s) -> p b s", b=DB)

        def apart(eng):
            eng.sem_inc(passed, 1)

        block = ctx.enter_context(nc.Block())

        @block.sync
        def _(sp):
            sp.dma_start(consts, t["consts"]).then_inc(consts_in, 16)
            sp.dma_start(convp, t["convp"]).then_inc(consts_in, 16)
            sp.dma_start(pages, t["pages"]).then_inc(consts_in, 16)
            with nc.allow_non_contiguous_dma("page numbers, one per partition"):
                sp.dma_start(pgi, t["pages"].rearrange("a (g p) -> p (a g)", g=2)).then_inc(pgi_in, 16)
            sp.dma_start(gain, t["norm_mix"].to_broadcast([P, D])).then_inc(gain_in, 16)
            for i in range(TILES):
                sp.dma_start(resid[0:rows_of(i), i, :], t["x"][i * P:i * P + rows_of(i), :]).then_inc(x_in[i], 16)
            for name in ("cc", "cx"):
                ring_load(sp, name)
            sp.dma_start(halo, t["state_conv"]).then_inc(halo_in, 16)
            with nc.allow_non_contiguous_dma("8 columns of w_in"):
                sp.dma_start(wfz, w3(t["w_in"], O_FZ, H)).then_inc(wfz_in, 16)
            sp.dma_start(mem, t["mem_prompt"].rearrange("(i p) d -> p i d", p=P)).then_inc(mem_in, 16)
            sp.wait_ge(gain_used, 1)
            sp.dma_start(gain, t["norm_mem"].to_broadcast([P, D])).then_inc(gain_in, 16)
            for name in ("cb", "q", "k", "v", "xk", "xv"):
                ring_load(sp, name)
            sp.wait_ge(neg_stored, 16)
            R.read(sp, "mv", 1)
            sp.wait_ge(stage_stored[0], 16 * 6), sp.wait_ge(stage_stored[1], 16 * 5)
            for p in range(2):
                sp.dma_start(negk[p], neg_d[p:p + 1, 0:SEQ].to_broadcast([P, SEQ])).then_inc(negk_in[p], 16)
            with sp.Fori(1, H // 2) as hp:
                for p in range(2):
                    sp.wait_ge(fs_max, hp * 16 - 8 + 8 * p)
                    sp.dma_start(negk[p], neg_d[ds(hp * 2 + p, 1), 0:SEQ].to_broadcast([P, SEQ])
                                 ).then_inc(negk_in[p], 16)
            sp.wait_ge(fp_full, 1 + H // 2)
            sp.wait_ge(rev_stored, 16 * DB)
            for q in range(DS):
                sp.dma_start(nd[q * H:(q + 1) * H, :], neg_d[:, SEQ:NT]).then_inc(nd_in, 16)
            with sp.Fori(0, DB) as b:
                sp.wait_ge(s_max, b + 1)
                for q in range(DS):
                    sp.dma_start(rev[q * H:(q + 1) * H, :], rev_d[ds(b, 1)].rearrange("a h s -> (a h) s")
                                 ).then_inc(rev_in, 16)
                for g in range(PAGES // 4):
                    sp.wait_ge(kt_full, b * 32 + g * 4 + 4)
                    for p in range(4):
                        page = sp.value_load(pages[0:1, ds(b * PAGES + (g * 4 + p), 1)], min_val=0, max_val=N_POOL - 1)
                        sp.dma_start(kpage[g % 2][:, p, :], t["cache_k"][ds(page, 1)].rearrange("a s d -> (a s) d")
                                     ).then_inc(k_in[g % 2], 16)

            sp.wait_ge(so_full, DB)
            for name in ("ga0", "gb0"):
                ring_load(sp, name)
            sp.dma_start(upc, t["w_up_conv"].rearrange("(k p) n -> p k n", p=P)).then_inc(upc_in, 16)
            sp.dma_start(upa, t["w_up_attn"].rearrange("(k p) n -> p k n", p=P)).then_inc(upa_in, 16)
            for i in range(2):
                sp.dma_start(xr[i], t["x"][i * P:(i + 1) * P, :]).then_inc(xr_in[i], 16)
            sp.wait_ge(gain_used, 2)
            sp.dma_start(gain, t["norm_xattn"].to_broadcast([P, D])).then_inc(gain_in, 16)
            for name in ("ga1", "gb1", "mo0", "mo1"):
                ring_load(sp, name)
            for i in range(2, TILES):
                R.read(sp, "mo", i - 2, 1)
                sp.dma_start(xr[i % 2][0:rows_of(i), :], t["x"][i * P:i * P + rows_of(i), :]).then_inc(xr_in[i % 2], 16)
            for name in ("xq", "xo"):
                ring_load(sp, name)
            for b in range(2):
                sp.dma_start(ck[b], t["cache_mem_k"][b].rearrange("(i p) d -> p i d", p=P)).then_inc(ck_in[b], 16)
            sp.dma_start(wr, t["w_router"].rearrange("(k p) n -> p k n", p=P)).then_inc(wr_in, 16)
            R.made(sp, "xq", KC - 1, COLS - 1)
            sp.dma_start(cv, t["cache_mem_v"].rearrange("b (i p) d -> p b i d", p=P)).then_inc(cv_in, 16)
            sp.wait_ge(gain_used, 3)
            sp.dma_start(gain, t["norm_ffn"].to_broadcast([P, D])).then_inc(gain_in, 16)
            for b in range(2, DB):
                R.made(sp, "ckT", b - 2, 1)
                sp.dma_start(ck[b % 2], t["cache_mem_k"][b].rearrange("(i p) d -> p i d", p=P)).then_inc(ck_in[b % 2], 16)
            sp.wait_ge(gain_used, 4)
            sp.dma_start(gain, t["norm_final"].to_broadcast([P, D])).then_inc(gain_in, 16)
            R.made(sp, "h2", TILES - 1, 1)
            sp.wait_ge(routed, 1)
            n = sp.value_load(nblk[0:1, 0:1], min_val=2, max_val=MAXB)

            def expert_load(b, which):
                src = t[which][ds(sp.value_load(blke[0:1, ds(b, 1)], min_val=0, max_val=NE - 1), 1)]
                return src.rearrange("a (k p) n -> p (a k) n", p=P)

            sp.dma_start(wg, expert_load(0, "w_expert_gate")).then_inc(wg_in, 16)
            sp.dma_start(wu, expert_load(0, "w_expert_up")).then_inc(wu_in, 16)
            sp.dma_start(wd, expert_load(0, "w_expert_down")).then_inc(wd_in, 16)
            with sp.Fori(1, n) as b:
                sp.wait_ge(g_full, b)
                apart(sp)
                sp.dma_start(wg, expert_load(b, "w_expert_gate")).then_inc(wg_in, 16)
                sp.wait_ge(u_full, b)
                apart(sp)
                sp.dma_start(wu, expert_load(b, "w_expert_up")).then_inc(wu_in, 16)
                sp.wait_ge(d_full, b * 2)
                apart(sp)
                sp.dma_start(wd, expert_load(b, "w_expert_down")).then_inc(wd_in, 16)
            for i in range(TILES):
                sp.wait_ge(n_fin.scaled, i + 1)
                dst = t["y_prompt"][i * P:(i + 1) * P, :] if i < PT else t["y_sample"]
                sp.dma_start(dst, xs[i % 2][0:rows_of(i), :]).then_inc(y_out[i % 2], 16)
            sp.wait_ge(y_out[0], 16 * 5), sp.wait_ge(y_out[1], 16 * 4)

        @block.tensor
        def _(pe):
            def product(tag, name, f, n):
                slot = ring_slot(pe, name)
                R.pe_free(pe, *tag)
                for k in range(KD):
                    last = nc.tensor.matmul(bank(R.bank(*tag))[:, 0:NC_], slot[:, k, f * P:(f + 1) * P],
                                            xnT[:, k, cols_of(n)], start=k == 0, stop=k == KD - 1)
                last.then_inc(R.full, 1)

            def rows_product(tag, name, src, i, r):
                slot = ring_slot(pe, name)
                R.pe_free(pe, *tag)
                for k in range(KD):
                    last = nc.tensor.matmul(bank(R.bank(*tag))[0:r, :], src[:, k, i * P:i * P + r], slot[:, k, :],
                                            start=k == 0, stop=k == KD - 1)
                last.then_inc(R.full, 1)

            def turn(tag, pieces):
                R.pe_free(pe, *tag)
                for dst, src in pieces(bank(R.bank(*tag))):
                    r = src.shape[0]
                    last = nc.tensor.transpose(dst, src, ident[0:r, 0:r])
                last.then_inc(R.full, 1)

            pe.wait_ge(consts_in, 48)
            n_mix.pe_turn(pe)
            pe.wait_ge(totals_ready, 1)
            for g in range(2):
                R.pe_free(pe, "later", g)
                nc.tensor.matmul(bank(R.bank("later", g))[:, 0:H], consts[:, C_PAGES:C_PAGES + P], ptot[:, g, :],
                                 start=True, stop=True).then_inc(R.full, 1)
            pe.wait_ge(halo_in, 16)
            turn(("halo",), lambda b: [(b[:, c * 2 * DB:(c + 1) * 2 * DB], halo[:, c * P:(c + 1) * P]) for c in range(KC)])
            R.read(pe, "nmix", TILES - 1, 1)
            for name in ("cc", "cx", "cb"):
                for f, n in FN:
                    product((name, f, n), name, f, n)
            pe.wait_ge(tail_got, 1)
            turn(("tail",), lambda b: [(b[0:2 + 2 * DB, c * P:(c + 1) * P], tailT[:, c, :]) for c in range(KC)])
            for name in "qk":
                for f, n in FN:
                    product((name, f, n), name, f, n)
            pe.wait_ge(wfz_in, 16)
            for n in range(COLS):
                R.pe_free(pe, "fz", n)
                for k in range(KD):
                    last = nc.tensor.matmul(bank(R.bank("fz", n))[0:H, 0:NC_], wfz[:, k, :], xnT[:, k, cols_of(n)],
                                            start=k == 0, stop=k == KD - 1)
                last.then_inc(R.full, 1)
            for i in range(TILES):
                rows_product(("v", i), "v", xnT, i, rows_of(i))
            for i in range(TILES):
                R.read(pe, "k", KC - 1, COLS - 1)
                turn(("kout", i), lambda b: [(b[0:rows_of(i), c * P:(c + 1) * P], kT[:, c, i * P:i * P + rows_of(i)])
                                             for c in range(KC)])
            pe.wait_ge(lf_ready, 1)
            turn(("lf",), lambda b: [(b[0:rows_of(i), i * H:(i + 1) * H], lf[:, 2, i * P:i * P + rows_of(i)])
                                     for i in range(TILES)])
            n_mem.pe_turn(pe)
            R.read(pe, "nmem", 1, 1)
            for i in range(2):
                rows_product(("mk", i), "xk", memT, i, P)
            for i in range(2):
                R.read(pe, "mk", i)
                turn(("mkT", i), lambda b: [(b[:, h * XD:(h + 1) * XD], stage[i][:, h * XD:(h + 1) * XD])
                                            for h in range(XH)])
            for i in range(2):
                rows_product(("mv", i), "xv", memT, i, P)

            R.read(pe, "mv", 1), R.read(pe, "lf")
            pe.sem_inc(fp_full, 1)
            with pe.Fori(0, H // 2) as hp:
                def scores(u, p, i):
                    n = (i + 1) * P
                    if i == 0:
                        pe.wait_ge(qz_ready, hp * 2 + p + 1)
                    if u >= 2:
                        pe.wait_ge(fs_max, hp * 16 + u - 1)
                    for c0 in range(0, n, 512):
                        c1 = min(n, c0 + 512)
                        nc.tensor.matmul(ps[u % 2][:, c0:c1], qz[p][:, i * P:(i + 1) * P],
                                         kT.rearrange("p c n -> p (c n)")[:, ds(hp * NT + c0, c1 - c0)],
                                         start=True, stop=c1 < n)
                    nc.tensor.matmul(ps[u % 2][:, n - P:n], identb, causalb, start=False, stop=True).then_inc(fs_full, 1)

                def turn_probs(u):
                    pe.wait_ge(fs_exp, hp * 16 + u + 1)
                    for g, j0, nj in groups(u):
                        if g >= 2:
                            pe.wait_ge(ft_act if g % 2 == 0 else ft_dve, hp * 12 + g // 2)
                        for j in range(nj):
                            last = nc.tensor.transpose(bank(4 + g % 2)[:, j * P:(j + 1) * P],
                                                       prob[u % 2][:, (j0 + j) * P:(j0 + j + 1) * P], ident)
                        last.then_inc(ft_full, 1)

                def weigh(u, i):
                    done = groups(u)[-1][0] + 1
                    pe.wait_ge(ft_act, hp * 12 + (done + 1) // 2)
                    if done // 2:
                        pe.wait_ge(ft_dve, hp * 12 + done // 2)
                    if u >= 2:
                        pe.wait_ge(fo_read, hp * 16 + u - 1)
                    for j in range(i + 1):
                        last = nc.tensor.matmul(bank(6 + u % 2)[:, 0:P], probT[u % 2][:, j, :], vtok[:, j, ds(hp * P, P)],
                                                start=j == 0, stop=j == i)
                    last.then_inc(fo_full, 1)

                scores(*units()[0])
                for u, p, i in units():
                    if u + 1 < 2 * PT:
                        scores(*units()[u + 1])
                    turn_probs(u)
                    if u:
                        weigh(u - 1, (u - 1) % PT)
                weigh(2 * PT - 1, PT - 1)
                pe.wait_ge(fo_read, hp * 16 + 16)
                for i in range(PT):
                    last = nc.tensor.transpose(ps[0][:, i * P:(i + 1) * P], pair[:, i, :], ident)
                last.then_inc(fp_full, 1)

            pe.wait_ge(fp_read, H // 2)
            pe.sem_inc(kt_full, 8), pe.sem_inc(v_used, 4)
            with pe.Fori(0, DB) as b:
                def turn_keys(g):
                    pe.wait_ge(k_in[g % 2], b * 256 + 64 * (g // 2 + 1))
                    for c in range(KC):
                        if g:
                            pe.wait_ge(kt_dve if c % 2 else kt_act, b * 16 + 2 * (g - 1) + c // 2 + 1)
                        for p in range(4):
                            last = nc.tensor.transpose(bank(c)[:, p * PAGE:(p + 1) * PAGE],
                                                       kpage[g % 2][:, p, c * P:(c + 1) * P], ident)
                        last.then_inc(kt_full, 1)

                def sample_scores(g):
                    pe.wait_ge(kt_act, b * 16 + 2 * g + 2)
                    pe.wait_ge(kt_dve, b * 16 + 2 * g + 2)
                    if g >= 2:
                        pe.wait_ge(sc_read, b * 9 + g - 1)
                    for c in range(KC):
                        last = nc.tensor.matmul(bank(4 + g % 2)[0:QH, :], qb[:, c * QH:(c + 1) * QH], kpT[g % 2][:, c, :],
                                                start=c == 0, stop=c == KC - 1)
                    last.then_inc(sc_full, 1)

                def turn_sample_probs(r):
                    pe.wait_ge(s_exp, b * 5 + r + 1)
                    if r >= 2:
                        pe.wait_ge(t2_dve if r % 2 else t2_act, b * (3 if r % 2 else 2) + 1)
                    apart(pe)
                    for j in range(8):
                        last = nc.tensor.transpose(bank(4 + r % 2)[:, j * QH:(j + 1) * QH],
                                                   sprob[:, (r * 8 + j) * PAGE:(r * 8 + j + 1) * PAGE], ident[0:QH, 0:QH])
                    last.then_inc(t2_full, 1)

                def weigh_pages(r):
                    pe.wait_ge(t2_dve if r % 2 else t2_act, b * (3 if r % 2 else 2) + r // 2 + 1)
                    for g in (2 * r, 2 * r + 1):
                        pe.wait_ge(v_in[g % 4], b * 128 + 64 * (g // 4 + 1))
                        for p in range(4):
                            j = g * 4 + p
                            last = nc.tensor.matmul(bank(7)[0:QH, :], sprobT[:, j, :], vpage[g % 4][:, p, :],
                                                    start=j == 0, stop=False)
                        last.then_inc(v_used, 1)

                pe.wait_ge(qb_ready, b + 1)
                turn_keys(0)
                for g in range(8):
                    if g < 7:
                        turn_keys(g + 1)
                    sample_scores(g)
                pe.wait_ge(sx_read, b + 1)
                for c in range(KC):
                    last = nc.tensor.matmul(bank(6)[0:QH, 0:NS], qb[:, c * QH:(c + 1) * QH], ks[:, c, :],
                                            start=c == 0, stop=c == KC - 1)
                last.then_inc(sc_full, 1)
                turn_sample_probs(0), turn_sample_probs(1), weigh_pages(0)
                turn_sample_probs(2), weigh_pages(1), turn_sample_probs(3), weigh_pages(2)
                pe.wait_ge(s_exp, b * 5 + 5)
                apart(pe)
                nc.tensor.transpose(bank(6)[0:NS, 64:64 + QH], sprob[:, PAST:PAST + NS], ident[0:QH, 0:QH]
                                    ).then_inc(t2_full, 1)
                weigh_pages(3)
                pe.wait_ge(t2_dve, b * 3 + 3)
                apart(pe)
                nc.tensor.matmul(bank(7)[0:QH, :], snewT, vtok[0:NS, PT, :], start=False, stop=True).then_inc(so_full, 1)
                pe.wait_ge(so_read, b + 1)
                apart(pe)
                for c in range(KC):
                    last = nc.tensor.matmul(bank(6)[:, 128 + c * DS:128 + (c + 1) * DS], own[:, c * P:(c + 1) * P],
                                            consts[0:QH, C_SELQ:C_SELQ + DS], start=True, stop=True)
                last.then_inc(sx_full, 1)

            pe.wait_ge(sx_read, DB + 1)
            pe.wait_ge(upc_in, 16), pe.wait_ge(upa_in, 16)

            def up(tag, weight, src, f, n):
                R.pe_free(pe, *tag)
                for k in range(KC):
                    last = nc.tensor.matmul(bank(R.bank(*tag))[:, 0:NC_], weight[:, k, f * P:(f + 1) * P],
                                            src[:, k, cols_of(n)], start=k == 0, stop=k == KC - 1)
                last.then_inc(R.full, 1)

            for f, n in FN8:
                product(("ga", f, n), f"ga{f // 4}", f % 4, n)
                up(("yc", f, n), upc, cyT, f, n)
                product(("gb", f, n), f"gb{f // 4}", f % 4, n)
                up(("ya", f, n), upa, oT, f, n)
            pe.wait_ge(mixed, KD * COLS)
            for i in range(TILES):
                for half in range(2):
                    rows_product(("mo", i, half), f"mo{half}", mixT, i, rows_of(i))
            n_xat.pe_turn(pe)
            R.read(pe, "nxat", TILES - 1, 1)
            for f, n in FN:
                product(("xq", f, n), "xq", f, n)
            R.read(pe, "xq", KC - 1, COLS - 1)

            def cross_scores(i):
                for half in range(2):
                    R.pe_free(pe, "xs", i, half)
                    for h in (2 * half, 2 * half + 1):
                        last = nc.tensor.matmul(bank(R.bank("xs", i, half))[:, (h % 2) * NMEM:(h % 2 + 1) * NMEM],
                                                q2T[:, h, i * P:(i + 1) * P], memKT[:, h, :], start=True, stop=True)
                    last.then_inc(R.full, 1)

            def cross_weigh(i):
                R.read(pe, "xt", i, 0), R.read(pe, "xt", i, 1)
                R.pe_free(pe, "xo", i)
                for h in range(XH):
                    for m in range(2):
                        last = nc.tensor.matmul(bank(R.bank("xo", i))[:, h * P:(h + 1) * P], memV[:, m, h * XD:(h + 1) * XD],
                                                xpT[i % 2][:, 2 * h + m, :], start=m == 0, stop=m == 1)
                last.then_inc(R.full, 1)

            cross_scores(0)
            for i in range(PT):
                if i + 1 < PT:
                    cross_scores(i + 1)
                pe.wait_ge(x_norm, i + 1)
                for half in range(2):
                    turn(("xt", i, half), lambda b: [(b[:, j * P:(j + 1) * P], xp[i % 2][
                        :, (4 * half + j) // 2, (j % 2) * P:(j % 2 + 1) * P]) for j in range(4)])
                if i:
                    cross_weigh(i - 1)
            cross_weigh(PT - 1)
            pe.wait_ge(qp_ready, 1)
            for b in range(DB):
                pe.wait_ge(ck_in[b % 2], 16 * (b // 2 + 1))
                for m in range(2):
                    turn(("ckT", b, m), lambda x: [(x[:, h * P:(h + 1) * P], ck[b % 2][:, m, h * XD:(h + 1) * XD])
                                                   for h in range(XH)])
                if b % 2:
                    R.pe_free(pe, "ss", b // 2)
                    rows = slice(b // 2 * 32, b // 2 * 32 + 32)
                    for bb in (b - 1, b):
                        R.read(pe, "ckT", bb, 0), R.read(pe, "ckT", bb, 1)
                        for h in range(XH):
                            n = bb * XH + h
                            last = nc.tensor.matmul(bank(R.bank("ss", b // 2))[rows, 0:NMEM], qp[:, n * 32:(n + 1) * 32],
                                                    ckT[bb % 2][:, h, :], start=n % 8 == 0, stop=n % 8 == 7)
                    last.then_inc(R.full, 1)
            pe.wait_ge(sx_norm, 1)
            turn(("spT",), lambda b: [(b[:, m * P:(m + 1) * P], sp_[:, m * P:(m + 1) * P]) for m in range(2)])
            R.read(pe, "spT")
            pe.wait_ge(cv_in, 16)
            R.pe_free(pe, "so")
            for n in range(DB * XH):
                for m in range(2):
                    last = nc.tensor.matmul(bank(R.bank("so"))[:, n * DS:(n + 1) * DS], cv[:, n // XH, m, n % XH * XD:(n % XH + 1) * XD],
                                            spT[:, m, n * DS:(n + 1) * DS], start=m == 0, stop=m == 1)
            last.then_inc(R.full, 1)
            R.read(pe, "so")
            R.read(pe, "xo", PT - 1)
            ring_slot(pe, "xo")
            for i in range(TILES):
                for half in range(2):
                    r = rows_of(i)
                    R.pe_free(pe, "h2", i, half)
                    for k in range(XH):
                        last = nc.tensor.matmul(bank(R.bank("h2", i, half))[0:r, :], o2T[:, k, i * P:i * P + r],
                                                ring_xo[:, k, half * 512:(half + 1) * 512], start=k == 0, stop=k == XH - 1)
                    last.then_inc(R.full, 1)
            n_ffn.pe_turn(pe)
            R.read(pe, "nffn", TILES - 1, 1)
            pe.wait_ge(wr_in, 16)
            for n in range(COLS):
                R.pe_free(pe, "lgT", n)
                for k in range(KD):
                    last = nc.tensor.matmul(bank(R.bank("lgT", n))[0:NG + NE, 0:NC_], wr[:, k, :], xnT[:, k, cols_of(n)],
                                            start=k == 0, stop=k == KD - 1)
                last.then_inc(R.full, 1)
            R.read(pe, "lgT", COLS - 1)
            turn(("lg",), lambda b: [(b[0:rows_of(i), i * 36:(i + 1) * 36], lgT[:, i * P:i * P + rows_of(i)])
                                     for i in range(TILES)])
            pe.wait_ge(hot_ready, 1)
            R.pe_free(pe, "rank")
            b = bank(R.bank("rank"))
            for i in range(TILES + 1):
                for j in range(min(i, TILES - 1) + 1):
                    last = nc.tensor.matmul(b[:, i * NE:(i + 1) * NE], beforeb if j == i else onesb, hot[:, j, :],
                                            start=j == 0, stop=j == min(i, TILES - 1))
            last.then_inc(R.full, 1)
            pe.wait_ge(routed, 1)
            n = pe.value_load(nblk[0:1, 0:1], min_val=2, max_val=MAXB)

            def turn_rows():
                for c in range(KD):
                    last = nc.tensor.transpose(ps[1][:, c * P:(c + 1) * P], xg[:, c * P:(c + 1) * P], ident)
                last.then_inc(xt_full, 1)

            pe.sem_inc(ht_full, 1)
            pe.wait_ge(xg_in, 16)
            turn_rows()
            with pe.Fori(0, n) as b:
                pe.wait_ge(xt_read, b + 1)
                pe.wait_ge(wg_in, b * 16 + 16)
                pe.wait_ge(h_ready, b + 1)
                for k in range(KD):
                    last = nc.tensor.matmul(bank(0), xgT[:, k, :], wg[:, k, :], start=k == 0, stop=k == KD - 1)
                last.then_inc(g_full, 1)
                pe.wait_ge(wu_in, b * 16 + 16)
                for k in range(KD):
                    last = nc.tensor.matmul(bank(1), xgT[:, k, :], wu[:, k, :], start=k == 0, stop=k == KD - 1)
                last.then_inc(u_full, 1)
                pe.wait_ge(xg_in, b * 16 + 32)
                turn_rows()
                pe.wait_ge(h_ready, b + 2)
                for c in range(DE // P):
                    last = nc.tensor.transpose(bank(4)[:, c * P:(c + 1) * P], hh[:, c * P:(c + 1) * P], ident)
                last.then_inc(ht_full, 1)
                pe.wait_ge(ht_read, b + 1)
                pe.wait_ge(wd_in, b * 16 + 16)
                pe.wait_ge(d_read, b + 1)
                for half in range(2):
                    for k in range(DE // P):
                        last = nc.tensor.matmul(bank(6 + half), hT[:, k, :], wd[:, k, half * 512:(half + 1) * 512],
                                                start=k == 0, stop=k == DE // P - 1)
                    last.then_inc(d_full, 1)

        @block.scalar
        def _(act):
            def copy(tag, dst, src, scale=1.0, last=True):
                R.made(act, *tag)
                ins = nc.scalar.activation(dst, src(bank(R.bank(*tag))), ACT.Copy, scale=scale)
                if last:
                    ins.then_inc(R.by["act"], 1)

            act.wait_ge(made_up, 1)
            n_mix.act_stats(act, lambda i: resid[:, i, :], lambda i: act.wait_ge(x_in[i], 16))
            n_mix.act_copy(act, xnT)
            for f, n in FN:
                if n < COLS - 1:
                    copy(("cc", f, n), uT[:, f, HALO + n * NC_:HALO + (n + 1) * NC_], lambda b: b[:, 0:NC_])
                else:
                    copy(("cc", f, n), uT[:, f, HALO + n * NC_:HALO + SEQ], lambda b: b[:, 0:NC_ - NS], last=False)
                    copy(("cc", f, n), samples(uT[:, f, :])[:, :, HALO:], lambda b: b[:, NC_ - NS:NC_].rearrange(
                        "p (b s) -> p b s", b=DB))
            act.wait_ge(rev_stored, 16 * DB)
            for f, n in FN:
                copy(("q", f, n), qT[:, f, cols_of(n)], lambda b: b[:, 0:NC_], scale=HD ** -0.5)
            for f, n in FN:
                copy(("k", f, n), kT[:, f, cols_of(n)], lambda b: b[:, 0:NC_])
            act.drain()
            nc.scalar.activation(qs, qT[:, :, SEQ:NT], ACT.Copy)
            nc.scalar.activation(ks, kT[:, :, SEQ:NT], ACT.Copy)
            act.wait_ge(abs_ready, 1)
            nc.scalar.activation(lf[:, 1, :], lf[:, 1, :], ACT.Exp, scale=-1.0)
            act.drain()
            nc.scalar.activation(lf[:, 1, :], lf[:, 1, :], ACT.Ln, bias=1.0).then_inc(ln_ready, 1)
            for i in range(TILES):
                copy(("v", i), vtok[0:rows_of(i), i, :], lambda b: b[0:rows_of(i), :])
            for i in range(TILES):
                if i >= 2:
                    act.wait_ge(stage_stored[i % 2], 16 * (i // 2))
                copy(("kout", i), stage[i % 2][0:rows_of(i), :], lambda b: b[0:rows_of(i), :])
            act.wait_ge(gain_used, 1)
            n_mem.act_stats(act, lambda i: mem[:, i, :], lambda i: act.wait_ge(mem_in, 16))
            n_mem.act_copy(act, memT)
            for i in range(2):
                act.wait_ge(stage_stored[i], 16 * (5 if i == 0 else 4))
                copy(("mk", i), stage[i], lambda b: b)
            for i in range(2):
                copy(("mkT", i), memKT[:, :, i * P:(i + 1) * P], lambda b: b.rearrange("p (h m) -> p h m", h=XH))
            for i in range(2):
                copy(("mv", i), memV[:, i, :], lambda b: b)

            act.wait_ge(qz_cleared, 2)
            with act.Fori(0, H // 2) as hp:
                def exp(u):
                    act.wait_ge(fs_max, hp * 16 + u + 1)
                    n = (u % PT + 1) * P
                    nc.scalar.activation(prob[u % 2][:, 0:n], prob[u % 2][:, 0:n], ACT.Exp, bias=fstat[:, 1, u % 4:u % 4 + 1],
                                         accum_out=fstat[:, 2, u % 4:u % 4 + 1]).then_inc(fs_exp, 1)

                for p in range(2):
                    nc.scalar.activation(qz[p][p * HD:(p + 1) * HD, :],
                                         qT.rearrange("p c n -> p (c n)")[p * HD:(p + 1) * HD, ds(hp * NT, SEQ)],
                                         ACT.Copy).then_inc(qz_ready, 1)
                exp(0)
                for u, p, i in units():
                    for g, j0, nj in groups(u):
                        if g % 2 == 0:
                            act.wait_ge(ft_full, hp * 24 + g + 1)
                            if u >= 2:
                                act.wait_ge(fo_full, hp * 16 + u - 1)
                            nc.scalar.activation(probT[u % 2][:, j0:j0 + nj, :], bank(4)[:, 0:nj * P].rearrange(
                                "p (j x) -> p j x", j=nj), ACT.Copy).then_inc(ft_act, 1)
                    if u + 1 < 2 * PT:
                        exp(u + 1)
                act.wait_ge(fp_full, hp + 2)
                nc.scalar.activation(oT.rearrange("p c n -> p (c n)")[:, ds(hp * NT, SEQ)], ps[0][:, :], ACT.Copy
                                     ).then_inc(fp_read, 1)
            with act.Fori(0, DB) as b:
                def copy_keys(g):
                    if g >= 2:
                        act.wait_ge(sc_full, b * 9 + g - 1)
                    for c in (0, 2):
                        act.wait_ge(kt_full, b * 32 + g * 4 + c + 9)
                        nc.scalar.activation(kpT[g % 2][:, c, :], bank(c), ACT.Copy).then_inc(kt_act, 1)

                def exp_pages(r):
                    x = sprob[:, r * 1024:(r + 1) * 1024] if r < 4 else sprob[:, PAST:PAST + NS]
                    nc.scalar.activation(x, x, ACT.Exp, bias=sstat[:, 10:11], accum_out=sstat[:, 12 + r:13 + r]
                                         ).then_inc(s_exp, 1)

                def copy_probs(r):
                    act.wait_ge(t2_full, b * 5 + r + 1)
                    nc.scalar.activation(sprobT[:, r * 8:(r + 1) * 8, :], bank(4)[:, 0:8 * QH].rearrange(
                        "p (j x) -> p j x", j=8), ACT.Copy).then_inc(t2_act, 1)

                for g in range(8):
                    copy_keys(g)
                act.wait_ge(s_max, b + 2)
                exp_pages(0), exp_pages(1), copy_probs(0), exp_pages(2), exp_pages(3), exp_pages(4), copy_probs(2)

            for x, (f, n) in enumerate(FN8):
                for m, name in enumerate(("ga", "gb")):
                    if x >= 2:
                        act.wait_ge(mixed, x - 1)
                    R.made(act, name, f, n)
                    nc.scalar.activation(gate[m][x % 2], bank(R.bank(name, f, n))[:, 0:NC_], ACT.Sigmoid
                                         ).then_inc(R.by["act"], 1)
            act.wait_ge(gain_used, 2)
            n_xat.act_stats(act, lambda i: resid[:, i, :], lambda i: R.read(act, "mo", i, 1))
            n_xat.act_copy(act, xnT)
            for f, n in FN:
                copy(("xq", f, n), q2T[:, f, cols_of(n)], lambda b: b[:, 0:NC_])
            XSCALE = XD ** -0.5

            def cross_exp(i):
                act.wait_ge(x_max, i + 1)
                for half in range(2):
                    for h in (2 * half, 2 * half + 1):
                        last = nc.scalar.activation(xp[i % 2][:, h, :], bank(R.bank("xs", i, half))[
                            :, (h % 2) * NMEM:(h % 2 + 1) * NMEM], ACT.Exp, bias=xstat[:, i % 2, 4 + h:5 + h],
                            scale=XSCALE, accum_out=xstat[:, i % 2, 8 + h:9 + h])
                    last.then_inc(R.by["act"], 1)
                act.drain()
                act.sem_inc(x_exp, 1)

            cross_exp(0)
            for i in range(PT):
                if i + 1 < PT:
                    if i + 1 >= 2:
                        R.made(act, "xt", i - 1, 1)
                    cross_exp(i + 1)
                R.made(act, "xt", i, 0)
                if i >= 2:
                    R.made(act, "xo", i - 2)
                copy(("xt", i, 0), xpT[i % 2][:, 0:4, :], lambda b: b.rearrange("p (j x) -> p j x", j=4))
            for b in range(DB):
                if b >= 2:
                    R.made(act, "ss", b // 2 - 1)
                copy(("ckT", b, 0), ckT[b % 2][:, :, 0:P], lambda x: x.rearrange("p (h m) -> p h m", h=XH))
            act.wait_ge(sx_max, 1)
            nc.scalar.activation(sp_, sp_, ACT.Exp, bias=sxstat[:, 1:2], scale=XSCALE, accum_out=sxstat[:, 2:3]
                                 ).then_inc(sx_exp, 1)
            copy(("spT",), spT, lambda b: b[:, 0:2 * P].rearrange("p (m x) -> p m x", m=2))
            R.made(act, "so")
            for b in range(DB):
                last = nc.scalar.activation(o2T[:, :, SEQ + b * DS:SEQ + (b + 1) * DS], bank(R.bank("so"))[
                    :, b * XH * DS:(b + 1) * XH * DS].rearrange("p (h s) -> p h s", h=XH), ACT.Copy)
            last.then_inc(R.by["act"], 1)
            n_ffn.act_stats(act, lambda i: resid[:, i, :], lambda i: R.read(act, "h2", i, 1))
            n_ffn.act_copy(act, xnT)
            for n in range(COLS):
                copy(("lgT", n), lgT[:, cols_of(n)], lambda b: b[0:NG + NE, 0:NC_])
            act.wait_ge(g_sub, 1)
            nc.scalar.activation(t4[1], t4[1], ACT.Exp).then_inc(g_exp, 1)
            act.wait_ge(e_sub, 1)
            nc.scalar.activation(t1[:, 5, :], t1[:, 5, :], ACT.Exp).then_inc(e_exp, 1)
            act.wait_ge(routed, 1)
            n = act.value_load(nblk[0:1, 0:1], min_val=2, max_val=MAXB)

            def copy_rows():
                nc.scalar.activation(xgT, ps[1][:, :].rearrange("p (c x) -> p c x", c=KD), ACT.Copy).then_inc(xt_read, 1)

            act.wait_ge(xt_full, 1)
            copy_rows()
            act.sem_inc(d_read, 1)
            with act.Fori(0, n) as b:
                act.wait_ge(g_full, b + 1)
                nc.scalar.activation(sg, bank(0), ACT.Sigmoid).then_inc(sg_ready, 1)
                act.wait_ge(u_full, b + 1)
                act.wait_ge(xt_full, b + 2)
                copy_rows()
                act.wait_ge(ht_full, b + 2)
                nc.scalar.activation(hT, bank(4).rearrange("p (c x) -> p c x", c=DE // P), ACT.Copy).then_inc(ht_read, 1)
                act.wait_ge(y_free, b + 1)
                act.wait_ge(d_full, b * 2 + 2)
                nc.scalar.activation(yb, ps[3][:, :], ACT.Copy).then_inc(d_read, 1)
            n_fin.act_stats(act, lambda i: resid[:, i, :], lambda i: act.wait_ge(summed, i + 1))

        @block.vector
        def _(dve):
            nc.vector.memset(ss, 1.0)
            nc.vector.memset(ones, 1.0)
            dve.drain()
            dve.sem_inc(made_up, 1)
            n_mix.dve_scale(dve, lambda i: resid[:, i, :], 1)
            dve.wait_ge(consts_in, 48)
            nc.vector.tensor_copy(identb, ident)
            nc.vector.tensor_copy(causalb, consts[:, C_CAUSAL:C_CAUSAL + P])
            nc.vector.tensor_copy(beforeb, consts[:, C_BEFORE:C_BEFORE + P])
            nc.vector.memset(onesb, 1.0)
            dve.wait_ge(past_in, 32)
            for g in range(2):
                nc.vector.tensor_reduce(ptot[:, g, :], past[:, g, :].rearrange("p (s h) -> p h s", h=H), AX, ALU.add)
            dve.drain()
            dve.sem_inc(totals_ready, 1)
            nc.vector.memset(after[:, :, :, PAGE - 1:PAGE], 0.0)
            for g in range(2):
                for h in range(H):
                    gates = past[:, g, :].rearrange("p (s h) -> p h s", h=H)[:, h, :]
                    nc.vector.tensor_tensor_scan(after[:, g, h, 0:PAGE - 1][:, ::-1],
                                                 ones[:, 0:1].to_broadcast([P, PAGE - 1]), gates[:, 1:PAGE][:, ::-1],
                                                 0.0, ALU.mult, ALU.add)
            dve.drain()
            for g in range(2):
                R.made(dve, "later", g)
                nc.vector.tensor_tensor(after[:, g], after[:, g], bank(R.bank("later", g))[:, 0:H].unsqueeze(2)
                                        .to_broadcast([P, H, PAGE]), ALU.add).then_inc(after_ready, 1)
            dve.drain()
            dve.sem_inc(R.by["dve"], 2)
            R.made(dve, "halo")
            nc.vector.memset(uT[:, :, 0:HALO], 0.0)
            for c in range(KC):
                last = nc.vector.tensor_copy(samples(uT[:, c, :])[:, :, 0:HALO], bank(R.bank("halo"))[
                    :, c * 2 * DB:(c + 1) * 2 * DB].rearrange("p (b s) -> p b s", b=DB))
            last.then_inc(R.by["dve"], 1)
            for f, n in FN:
                R.made(dve, "cx", f, n)
                R.read(dve, "cc", f, n)
                b = bank(R.bank("cx", f, n))
                if n < COLS - 1:
                    u = uT[:, f, HALO + n * NC_:HALO + (n + 1) * NC_]
                    nc.vector.tensor_tensor(u, b[:, 0:NC_], u, ALU.mult).then_inc(R.by["dve"], 1)
                else:
                    u = uT[:, f, HALO + n * NC_:HALO + SEQ]
                    nc.vector.tensor_tensor(u, b[:, 0:NC_ - NS], u, ALU.mult)
                    u = samples(uT[:, f, :])[:, :, HALO:]
                    nc.vector.tensor_tensor(u, b[:, NC_ - NS:NC_].rearrange("p (b s) -> p b s", b=DB), u,
                                            ALU.mult).then_inc(R.by["dve"], 1)
            dve.drain()
            nc.vector.tensor_copy(tailT[:, :, 0:2], uT[:, :, HALO + SEQ - 2:HALO + SEQ])
            for c in range(KC):
                last = nc.vector.tensor_copy(tailT[:, c, 2:].rearrange("p (b s) -> p b s", b=DB),
                                             samples(uT[:, c, :])[:, :, DS:])
            last.then_inc(tail_got, 1)
            for j in range(3):
                for c in range(KC):
                    tap = convp[:, j * KC + c:j * KC + c + 1]
                    for u, y in ((uT[:, c, j:j + SEQ], cyT[:, c, 0:SEQ]),
                                 (samples(uT[:, c, :])[:, :, j:j + DS],
                                  cyT[:, c, SEQ:NT].rearrange("p (b s) -> p b s", b=DB))):
                        if j == 0:
                            nc.vector.tensor_scalar(y, u, tap, convp[:, 3 * KC + c:3 * KC + c + 1], ALU.mult, ALU.add)
                        else:
                            nc.vector.scalar_tensor_tensor(y, u, tap, y, ALU.mult, ALU.add)
                dve.drain()
            for f, n in FN:
                R.made(dve, "cb", f, n)
                y = cyT[:, f, cols_of(n)]
                nc.vector.tensor_tensor(y, bank(R.bank("cb", f, n))[:, 0:NC_], y, ALU.mult).then_inc(R.by["dve"], 1)
            R.made(dve, "tail")
            nc.vector.tensor_copy(tail, bank(R.bank("tail"))[0:2 + 2 * DB, :]).then_inc(R.by["dve"], 1)
            for n in range(COLS):
                R.made(dve, "fz", n)
                nc.vector.tensor_scalar(lf[:, 0, cols_of(n)], bank(R.bank("fz", n))[0:H, 0:NC_], convp[0:H, 4 * KC:4 * KC + 1],
                                        None, ALU.add).then_inc(R.by["dve"], 1)
            dve.drain()
            nc.vector.scalar_tensor_tensor(lf[:, 1, :], lf[:, 0, :], -1.0, lf[:, 0, :], ALU.mult, ALU.max
                                           ).then_inc(abs_ready, 1)
            dve.wait_ge(ln_ready, 1)
            nc.vector.scalar_tensor_tensor(lf[:, 2, :], lf[:, 0, :], 0.0, lf[:, 1, :], ALU.min, ALU.subtract
                                           ).then_inc(lf_ready, 1)
            dve.drain()
            nc.vector.tensor_tensor_scan(lf[:, 1, 0:SEQ], ones[0:H, 0:1].to_broadcast([H, SEQ]), lf[:, 2, 0:SEQ], 0.0,
                                         ALU.mult, ALU.add)
            nc.vector.tensor_copy(lf[:, 1, SEQ:NT], lf[:, 2, SEQ:NT])
            dve.drain()
            new_sum = lf[:, 1, SEQ:NT].rearrange("p (b s) -> p b s", b=DB)
            for s in range(1, DS):
                nc.vector.tensor_tensor(new_sum[:, :, s:s + 1], new_sum[:, :, s:s + 1], new_sum[:, :, s - 1:s], ALU.add)
                dve.drain()
            nc.vector.tensor_scalar(lf[:, 3, :], lf[:, 1, :], -1.0, None, ALU.mult).then_inc(neg_ready, 1)
            R.made(dve, "lf")
            b = bank(R.bank("lf"))
            nc.vector.tensor_copy(lfo[:, 0:PT, :], b[:, 0:PT * H].rearrange("p (i h) -> p i h", i=PT))
            nc.vector.tensor_copy(lfo[0:NS, PT, :], b[0:NS, PT * H:TILES * H]).then_inc(R.by["dve"], 1)
            n_mem.dve_scale(dve, lambda i: mem[:, i, :], 2)

            R.read(dve, "mv", 1)
            for p in range(2):
                nc.vector.memset(qz[p][(1 - p) * HD:(2 - p) * HD, :], 0.0).then_inc(qz_cleared, 1)
            with dve.Fori(0, H // 2) as hp:
                def biased(u, p, i):
                    n = (i + 1) * P
                    if i == 0:
                        dve.wait_ge(negk_in[p], hp * 16 + 16)
                    dve.wait_ge(fs_full, hp * 16 + u + 1)
                    if u >= 2:
                        dve.wait_ge(ft_full, hp * 24 + groups(u - 2)[-1][0] + 1)
                    apart(dve)
                    nc.vector.tensor_tensor_reduce(out=prob[u % 2][:, 0:n], in0=ps[u % 2][:, 0:n], in1=negk[p][:, 0:n],
                                                   scale=1.0, scalar=-3e38, op0=ALU.add, op1=ALU.max,
                                                   accum_out=fstat[:, 0, u % 4:u % 4 + 1])
                    dve.drain()
                    nc.vector.tensor_scalar(fstat[:, 1, u % 4:u % 4 + 1], fstat[:, 0, u % 4:u % 4 + 1], -1.0, None, ALU.mult
                                            ).then_inc(fs_max, 1)

                def divide(u, p, i):
                    dve.wait_ge(fo_full, hp * 16 + u + 1)
                    if u == 0:
                        dve.wait_ge(fp_full, hp + 1)
                    nc.vector.reciprocal(fstat[:, 3, u % 4:u % 4 + 1], fstat[:, 2, u % 4:u % 4 + 1])
                    dve.drain()
                    nc.vector.tensor_scalar(pair[:, i, p * HD:(p + 1) * HD], bank(6 + u % 2)[:, p * HD:(p + 1) * HD],
                                            fstat[:, 3, u % 4:u % 4 + 1], None, ALU.mult).then_inc(fo_read, 1)

                biased(*units()[0])
                for u, p, i in units():
                    if u + 1 < 2 * PT:
                        biased(*units()[u + 1])
                    for g, j0, nj in groups(u):
                        if g % 2:
                            dve.wait_ge(ft_full, hp * 24 + g + 1)
                            if u >= 2:
                                dve.wait_ge(fo_full, hp * 16 + u - 1)
                            nc.vector.tensor_copy(probT[u % 2][:, j0:j0 + nj, :], bank(5)[:, 0:nj * P].rearrange(
                                "p (j x) -> p j x", j=nj)).then_inc(ft_dve, 1)
                    if u:
                        divide(*units()[u - 1])
                divide(*units()[2 * PT - 1])
            dve.wait_ge(fp_full, 1 + H // 2)
            nc.vector.memset(qb, 0.0)
            dve.wait_ge(nd_in, 16 * DS)
            nc.vector.tensor_tensor(nbias, consts[0:QH, C_MASK:C_MASK + DB * NS].rearrange("p (b s) -> p b s", b=DB),
                                    nd.unsqueeze(1).to_broadcast([QH, DB, NS]), ALU.add)
            dve.drain()
            dve.sem_inc(s_max, 1), dve.sem_inc(sx_read, 1)
            with dve.Fori(0, DB) as b:
                def copy_keys(g):
                    if g >= 2:
                        dve.wait_ge(sc_full, b * 9 + g - 1)
                    for c in (1, 3):
                        dve.wait_ge(kt_full, b * 32 + g * 4 + c + 9)
                        nc.vector.tensor_copy(kpT[g % 2][:, c, :], bank(c)).then_inc(kt_dve, 1)

                def bias_scores(g):
                    dve.wait_ge(sc_full, b * 9 + g + 1)
                    apart(dve)
                    if g < 8:
                        out, scores, bias = sprob[:, g * 512:(g + 1) * 512], bank(4 + g % 2)[0:QH, :], rev[:, g * 512:(g + 1) * 512]
                    else:
                        out, scores = sprob[:, PAST:PAST + NS], bank(6)[0:QH, 0:NS]
                        bias = nb
                    nc.vector.tensor_tensor_reduce(out=out, in0=scores, in1=bias, scale=1.0, scalar=-3e38, op0=ALU.add,
                                                   op1=ALU.max, accum_out=sstat[:, g:g + 1]).then_inc(sc_read, 1)

                def copy_probs(r):
                    dve.wait_ge(t2_full, b * 5 + r + 1)
                    nc.vector.tensor_copy(sprobT[:, r * 8:(r + 1) * 8, :], bank(5)[:, 0:8 * QH].rearrange(
                        "p (j x) -> p j x", j=8)).then_inc(t2_dve, 1)

                for half in range(2):
                    r = slice(half * HD, (half + 1) * HD)
                    last = nc.vector.tensor_copy(qb[r, :].rearrange("p (c x) -> p c x", c=KC)[:, :, half:half + 25:H],
                                                 qs[r, :, ds(b * DS, DS)])
                dve.drain()
                dve.sem_inc(qb_ready, 1)
                copy_keys(0)
                dve.wait_ge(rev_in, b * 64 + 64)
                for g in range(8):
                    if g < 7:
                        copy_keys(g + 1)
                    bias_scores(g)
                nc.vector.tensor_copy(nb, nbias.rearrange("p b s -> p (b s)")[:, ds(b * NS, NS)])
                dve.drain()
                bias_scores(8)
                dve.drain()
                nc.vector.tensor_reduce(sstat[:, 9:10], sstat[:, 0:9], AX, ALU.max)
                dve.drain()
                nc.vector.tensor_scalar(sstat[:, 10:11], sstat[:, 9:10], -1.0, None, ALU.mult).then_inc(s_max, 1)
                copy_probs(1), copy_probs(3)
                dve.wait_ge(t2_full, b * 5 + 5)
                nc.vector.tensor_copy(snewT, bank(6)[0:NS, 64:64 + QH]).then_inc(t2_dve, 1)
                nc.vector.tensor_reduce(sstat[:, 17:18], sstat[:, 12:17], AX, ALU.add)
                dve.drain()
                nc.vector.reciprocal(sstat[:, 18:19], sstat[:, 17:18])
                dve.drain()
                dve.wait_ge(so_full, b + 1)
                nc.vector.scalar_tensor_tensor(own, bank(7)[0:QH, :], sstat[:, 18:19], consts[0:QH, C_DIAG:C_DIAG + DA],
                                               ALU.mult, ALU.mult).then_inc(so_read, 1)
                dve.wait_ge(sx_full, b + 1)
                nc.vector.tensor_copy(oT[:, :, ds(b * DS + SEQ, DS)], bank(6)[:, 128:128 + KC * DS].rearrange(
                    "p (c s) -> p c s", c=KC)).then_inc(sx_read, 1)

            for x, (f, n) in enumerate(FN8):
                for m, (name, y) in enumerate((("ga", "yc"), ("gb", "ya"))):
                    R.read(dve, name, f, n)
                    R.made(dve, y, f, n)
                    nc.vector.tensor_tensor(gate[m][x % 2], bank(R.bank(y, f, n))[:, 0:NC_], gate[m][x % 2], ALU.mult
                                            ).then_inc(R.by["dve"], 1)
                dve.drain()
                nc.vector.tensor_tensor(mixT[:, f, cols_of(n)], gate[0][x % 2], gate[1][x % 2], ALU.add).then_inc(mixed, 1)
            for i in range(TILES):
                r = rows_of(i)
                dve.wait_ge(xr_in[i % 2], 16 * (i // 2 + 1))
                for half in range(2):
                    R.made(dve, "mo", i, half)
                    c = slice(half * 512, (half + 1) * 512)
                    nc.vector.tensor_tensor(resid[0:r, i, c], bank(R.bank("mo", i, half))[0:r, :], xr[i % 2][0:r, c],
                                            ALU.add).then_inc(R.by["dve"], 1)
            n_xat.dve_scale(dve, lambda i: resid[:, i, :], 3)
            nc.vector.memset(qp, 0.0)
            R.read(dve, "xq", KC - 1, COLS - 1)
            dve.drain()
            for b in range(DB):
                cols = qp[:, b * 128:(b + 1) * 128].rearrange("p (h x) -> p h x", h=XH)
                for h in range(XH):
                    at_ = (b % 2) * 16 + h * DS
                    last = nc.vector.tensor_copy(cols[:, h, at_:at_ + DS], q2T[:, h, SEQ + b * DS:SEQ + (b + 1) * DS])
            last.then_inc(qp_ready, 1)

            def cross_max(i):
                st = xstat[:, i % 2, :]
                for half in range(2):
                    R.made(dve, "xs", i, half)
                    nc.vector.tensor_reduce(st[:, 2 * half:2 * half + 2], bank(R.bank("xs", i, half)).rearrange(
                        "p (h m) -> p h m", h=2), AX, ALU.max)
                dve.drain()
                nc.vector.tensor_scalar(st[:, 4:8], st[:, 0:4], -(XD ** -0.5), None, ALU.mult).then_inc(x_max, 1)

            def cross_out(i):
                R.made(dve, "xo", i)
                nc.vector.tensor_copy(o2T[:, :, i * P:(i + 1) * P], bank(R.bank("xo", i)).rearrange("p (h x) -> p h x", h=XH)
                                      ).then_inc(R.by["dve"], 1)

            cross_max(0)
            for i in range(PT):
                if i + 1 < PT:
                    cross_max(i + 1)
                dve.wait_ge(x_exp, i + 1)
                st = xstat[:, i % 2, :]
                nc.vector.reciprocal(st[:, 12:16], st[:, 8:12])
                dve.drain()
                nc.vector.tensor_tensor(xp[i % 2], xp[i % 2], st[:, 12:16].unsqueeze(2).to_broadcast([P, XH, NMEM]),
                                        ALU.mult).then_inc(x_norm, 1)
                R.made(dve, "xt", i, 1)
                nc.vector.tensor_copy(xpT[i % 2][:, 4:8, :], bank(R.bank("xt", i, 1)).rearrange("p (j x) -> p j x", j=4)
                                      ).then_inc(R.by["dve"], 1)
                if i:
                    cross_out(i - 1)
            cross_out(PT - 1)
            for b in range(DB):
                R.made(dve, "ckT", b, 1)
                nc.vector.tensor_copy(ckT[b % 2][:, :, P:2 * P], bank(R.bank("ckT", b, 1)).rearrange("p (h m) -> p h m", h=XH)
                                      ).then_inc(R.by["dve"], 1)
                if b % 2:
                    R.made(dve, "ss", b // 2)
                    rows = slice(b // 2 * 32, b // 2 * 32 + 32)
                    nc.vector.tensor_copy(sp_[rows, :], bank(R.bank("ss", b // 2))[rows, 0:NMEM]).then_inc(R.by["dve"], 1)
            dve.drain()
            nc.vector.tensor_reduce(sxstat[:, 0:1], sp_, AX, ALU.max)
            dve.drain()
            nc.vector.tensor_scalar(sxstat[:, 1:2], sxstat[:, 0:1], -(XD ** -0.5), None, ALU.mult).then_inc(sx_max, 1)
            dve.wait_ge(sx_exp, 1)
            nc.vector.reciprocal(sxstat[:, 3:4], sxstat[:, 2:3])
            dve.drain()
            nc.vector.tensor_scalar(sp_, sp_, sxstat[:, 3:4], None, ALU.mult).then_inc(sx_norm, 1)
            for i in range(TILES):
                r = rows_of(i)
                for half in range(2):
                    R.made(dve, "h2", i, half)
                    c = slice(half * 512, (half + 1) * 512)
                    nc.vector.tensor_tensor(resid[0:r, i, c], bank(R.bank("h2", i, half))[0:r, :], resid[0:r, i, c],
                                            ALU.add).then_inc(R.by["dve"], 1)

            def ffn_free(i):
                R.made(dve, "nffn", i, 1)
                dve.wait_ge(x3_stored[i % 2], 16 * (i // 2 + 1))

            n_ffn.dve_scale(dve, lambda i: resid[:, i, :], 4, ffn_free)
            nc.vector.memset(lg, 0.0)
            for k in range(2):
                for a in range(2):
                    nc.vector.tensor_scalar(pairs[:, k, :, a], consts[:, C_TOK:C_TOK + TILES], float(k * a * NT), None, ALU.add)
            nc.vector.memset(empty[:, :, 0:1], 0)
            nc.vector.memset(empty[:, :, 1:2], 2 * NT)
            dve.drain()
            dve.sem_inc(empty_ready, 1)
            R.made(dve, "lg")
            b = bank(R.bank("lg"))
            nc.vector.tensor_copy(lg[:, 0:PT, :], b[:, 0:PT * 36].rearrange("p (i e) -> p i e", i=PT))
            nc.vector.tensor_copy(lg[0:NS, PT, :], b[0:NS, PT * 36:TILES * 36]).then_inc(R.by["dve"], 1)
            dve.drain()
            dve.wait_ge(x3_stored[0], 16 * 5), dve.wait_ge(x3_stored[1], 16 * 4)
            TT, TS_, RED = nc.vector.tensor_tensor, nc.vector.tensor_scalar, nc.vector.tensor_reduce
            gl, el = lg[:, :, 0:NG], lg[:, :, NG:]

            def over(col, width):
                return t1[:, col, :].unsqueeze(2).to_broadcast([P, TILES, width])

            def row(c0, width):
                return consts[:, c0:c0 + width].unsqueeze(1).to_broadcast([P, TILES, width])

            RED(t1[:, 0, :], gl, AX, ALU.max)
            dve.drain()
            TT(t4[1], gl, over(0, NG), ALU.subtract).then_inc(g_sub, 1)
            TT(t4[0], gl, over(0, NG), ALU.is_lt)
            dve.drain()
            nc.vector.scalar_tensor_tensor(t4[2], t4[0], 1000.0, row(C_EXP, NG), ALU.mult, ALU.add)
            dve.drain()
            RED(t1[:, 1, :], t4[2], AX, ALU.min)
            dve.drain()
            m, le, hot1, hot2, le2, tmp, tmp2 = t32
            TT(m, row(C_GRP, NE), over(1, NE), ALU.is_equal)
            dve.drain()
            TS_(tmp, m, -NEG, NEG, ALU.mult, ALU.add)
            TT(le, el, m, ALU.mult)
            dve.drain()
            TT(le, le, tmp, ALU.add)
            dve.drain()
            for k, (src, one) in enumerate(((le, hot1), (le2, hot2))):
                if k:
                    nc.vector.scalar_tensor_tensor(le2, hot1, 2 * NEG, le, ALU.mult, ALU.add)
                    dve.drain()
                RED(t1[:, 2 + k, :], src, AX, ALU.max)
                dve.drain()
                TT(tmp, src, over(2 + k, NE), ALU.is_lt)
                dve.drain()
                nc.vector.scalar_tensor_tensor(tmp2, tmp, 1000.0, row(C_EXP, NE), ALU.mult, ALU.add)
                dve.drain()
                RED(t1[:, 4, :], tmp2, AX, ALU.min)
                dve.drain()
                TT(one, row(C_EXP, NE), over(4, NE), ALU.is_equal)
                dve.drain()
            TT(tmp, hot1, hot2, ALU.add)
            TS_(t1[:, 6, :], consts[:, C_TOK:C_TOK + TILES], float(NT), None, ALU.is_lt)
            TT(t1[:, 5, :], t1[:, 3, :], t1[:, 2, :], ALU.subtract).then_inc(e_sub, 1)
            dve.drain()
            TT(hot, tmp, over(6, NE), ALU.mult)
            dve.drain()
            dve.sem_inc(hot_ready, 1)
            dve.wait_ge(g_exp, 1)
            RED(t1[:, 7, :], t4[1], AX, ALU.add)
            dve.wait_ge(e_exp, 1)
            TS_(t1[:, 8, :], t1[:, 5, :], 1.0, None, ALU.add)
            dve.drain()
            TT(t1[:, 9, :], t1[:, 7, :], t1[:, 8, :], ALU.mult)
            dve.drain()
            nc.vector.reciprocal(wgt[:, 0, :], t1[:, 9, :])
            dve.drain()
            TT(wgt[:, 1, :], wgt[:, 0, :], t1[:, 5, :], ALU.mult)
            R.made(dve, "rank")
            b = bank(R.bank("rank"))
            TS_(cnti, b[:, TILES * NE:(TILES + 1) * NE], float(BLK - 1), None, ALU.add)
            dve.drain()
            TS_(cnti, cnti, BLK.bit_length() - 1, None, ALU.logical_shift_right)
            dve.drain()
            nc.vector.tensor_copy(cnt[:, 0, :], cnti)
            dve.drain()
            nc.vector.tensor_tensor_scan(cnt[:, 1, :], ones[:, 0:1].to_broadcast([P, NE]), cnt[:, 0, :], 0.0, ALU.mult, ALU.add)
            dve.drain()
            TT(cnt[:, 2, :], cnt[:, 1, :], cnt[:, 0, :], ALU.subtract)
            dve.drain()
            TS_(cnt[:, 3, :], cnt[:, 2, :], float(BLK), None, ALU.mult)
            dve.drain()
            TT(tmp, b[:, 0:TILES * NE].rearrange("p (i e) -> p i e", i=TILES), cnt[:, 3, :].unsqueeze(1).to_broadcast(
                [P, TILES, NE]), ALU.add).then_inc(R.by["dve"], 1)
            dve.drain()
            TT(le, tmp, hot1, ALU.mult)
            TT(le2, tmp, hot2, ALU.mult)
            dve.drain()
            RED(t1[:, 10, :], le, AX, ALU.add)
            RED(t1[:, 11, :], le2, AX, ALU.add)
            dve.drain()
            nc.vector.tensor_copy(dest, t1[:, 10:12, :])
            TT(bcmp, cnt[0:1, 1, :].unsqueeze(1).to_broadcast([1, MAXB, NE]),
               consts[0:1, C_BLK:C_BLK + MAXB].unsqueeze(2).to_broadcast([1, MAXB, NE]), ALU.is_le)
            dve.drain()
            RED(bsum, bcmp, AX, ALU.add)
            dve.drain()
            TS_(blke[0:1, 0:MAXB], bsum, float(NE - 1), None, ALU.min)
            nc.vector.tensor_copy(nblk, cnt[0:1, 1, NE - 1:NE])
            dve.drain()
            dve.sem_inc(routed, 1)
            dve.sem_inc(h_ready, 1)
            n = dve.value_load(nblk[0:1, 0:1], min_val=2, max_val=MAXB)
            with dve.Fori(0, n) as b:
                dve.wait_ge(sg_ready, b + 1)
                dve.wait_ge(ht_full, b + 1)
                TT(sg, bank(0), sg, ALU.mult)
                dve.wait_ge(u_full, b + 1)
                apart(dve)
                dve.drain()
                TT(hh, bank(1), sg, ALU.mult).then_inc(h_ready, 1)
            for i in range(TILES):
                r = rows_of(i)
                dve.wait_ge(y_in[i % 2], 32 * (i // 2 + 1))
                for k in range(2):
                    last = nc.vector.scalar_tensor_tensor(resid[0:r, i, :], yy[k][i % 2][0:r, :], wgt[0:r, k, i:i + 1],
                                                          resid[0:r, i, :], ALU.mult, ALU.add)
                    if k == 0:
                        dve.drain()
                last.then_inc(summed, 1)
            n_fin.dve_scale(dve, lambda i: resid[:, i, :], 5, lambda i: dve.wait_ge(y_out[i % 2], 16 * (i // 2 + 1)))

        @block.gpsimd
        def _(pool):
            n_stored = 0

            def store(dst, src):
                nonlocal n_stored
                n_stored += 1
                pool.dma_start(dst, src).then_inc(stored, 16)

            pool.wait_ge(pgi_in, 16)
            for g in range(2):
                pool.indirect_dma_start(past[:, g, :], None, t["cache_logf"],
                                        bass.IndirectOffsetOnAxis(ap=pgi[:, g:g + 1].bitcast(U32), axis=0)).then_inc(past_in, 16)
            pool.wait_ge(after_ready, 2)
            for b in range(DB):
                pool.dma_start(rev_d[b].rearrange("h (j s) -> j h s", j=PAGES),
                               after[b % 4 * PAGES:(b % 4 + 1) * PAGES, b // 4]).then_inc(rev_stored, 16)
            R.read(pool, "tail")
            store(t["conv_prompt"], tail[0:2, :])
            store(t["conv_sample"], tail[2:2 + 2 * DB, :])
            R.read(pool, "v", TILES - 1)
            store(t["v_prompt"].rearrange("(i p) d -> p i d", p=P), vtok[:, 0:PT, :])
            store(t["v_sample"], vtok[0:NS, PT, :])
            for i in range(TILES):
                R.read(pool, "kout", i)
                dst = t["k_prompt"][i * P:(i + 1) * P, :] if i < PT else t["k_sample"]
                pool.dma_start(dst, stage[i % 2][0:rows_of(i), :]).then_inc(stage_stored[i % 2], 16)
            pool.wait_ge(neg_ready, 1)
            pool.dma_start(neg_d, lf[:, 3, :]).then_inc(neg_stored, 16)
            R.read(pool, "lf")
            store(t["lf_prompt"].rearrange("(i p) h -> p i h", p=P), lfo[:, 0:PT, :])
            store(t["lf_sample"], lfo[0:NS, PT, :])
            for i in range(2):
                R.read(pool, "mk", i)
                pool.dma_start(t["mk_prompt"][i * P:(i + 1) * P, :], stage[i]).then_inc(stage_stored[i], 16)
            R.read(pool, "mv", 1)
            store(t["mv_prompt"].rearrange("(i p) d -> p i d", p=P), memV)
            pool.wait_ge(consts_in, 48)
            with pool.Fori(0, DB) as b:
                for g in range(PAGES // 4):
                    pool.wait_ge(v_used, b * 8 + g + 1)
                    for p in range(4):
                        page = pool.value_load(pages[0:1, ds(b * PAGES + (g * 4 + p), 1)], min_val=0, max_val=N_POOL - 1)
                        pool.dma_start(vpage[g % 4][:, p, :], t["cache_v"][ds(page, 1)].rearrange("a s d -> (a s) d")
                                       ).then_inc(v_in[g % 4], 16)
            pool.wait_ge(sx_read, DB + 1)
            for i in range(TILES):
                pool.wait_ge(n_ffn.scaled, i + 1)
                pool.dma_start(x3_d[i * P:i * P + rows_of(i), :], xs[i % 2][0:rows_of(i), :]).then_inc(x3_stored[i % 2], 16)
            pool.wait_ge(empty_ready, 1)
            pool.dma_start(row_d.rearrange("(p n) a -> p (n a)", p=P), empty.rearrange("p n a -> p (n a)")
                           ).then_inc(empty_stored, 16)
            pool.wait_ge(routed, 1)
            pool.wait_ge(empty_stored, 16)
            for i in range(TILES):
                for k in range(2):
                    r = rows_of(i)
                    pool.indirect_dma_start(row_d, bass.IndirectOffsetOnAxis(ap=dest[0:r, k, i:i + 1].bitcast(U32), axis=0),
                                            pairs[0:r, k, i, :], None).then_inc(rows_stored, 16)
            pool.wait_ge(rows_stored, 16 * 2 * TILES)
            pool.wait_ge(x3_stored[0], 16 * 5), pool.wait_ge(x3_stored[1], 16 * 4)
            n = pool.value_load(nblk[0:1, 0:1], min_val=2, max_val=MAXB)
            R.read(pool, "rank")

            def row_column(b, a):
                return row_d[ds(b * BLK, BLK), a:a + 1]

            with nc.allow_non_contiguous_dma("one number of a row for each partition"):
                pool.sem_inc(y_free, 1)
                pool.dma_start(rowi, row_column(0, 0)).then_inc(rowi_in, 16)
                pool.wait_ge(rowi_in, 16)
                pool.indirect_dma_start(xg, None, x3_d, bass.IndirectOffsetOnAxis(ap=rowi[:, 0:1].bitcast(U32), axis=0)
                                        ).then_inc(xg_in, 16)
                with pool.Fori(0, n) as b:
                    pool.dma_start(outi, row_column(b, 1)).then_inc(outi_in, 16)
                    pool.wait_ge(xt_full, b + 1)
                    pool.dma_start(rowi, row_column(b + 1, 0)).then_inc(rowi_in, 16)
                    pool.wait_ge(rowi_in, b * 16 + 32)
                    apart(pool)
                    pool.indirect_dma_start(xg, None, x3_d, bass.IndirectOffsetOnAxis(ap=rowi[:, 0:1].bitcast(U32), axis=0)
                                            ).then_inc(xg_in, 16)
                    pool.wait_ge(outi_in, b * 16 + 16)
                    pool.wait_ge(d_read, b + 2)
                    apart(pool)
                    pool.indirect_dma_start(y_d, bass.IndirectOffsetOnAxis(ap=outi[:, 0:1].bitcast(U32), axis=0), yb, None
                                            ).then_inc(y_stored, 16)
                    pool.wait_ge(y_stored, b * 16 + 16)
                    pool.sem_inc(y_free, 1)
            for i in range(TILES):
                r = rows_of(i)
                if i >= 2:
                    pool.wait_ge(summed, i - 1)
                for k in range(2):
                    pool.dma_start(yy[k][i % 2][0:r, :], y_d[k * NT + i * P:k * NT + i * P + r, :]).then_inc(y_in[i % 2], 16)
            pool.wait_ge(stored, 16 * n_stored)
            pool.wait_ge(neg_stored, 16)
            for i in range(2):
                pool.wait_ge(stage_stored[i], 16 * (6 - i))


_OUTS = [("y_prompt", (SEQ, D), (1, SEQ, D)), ("y_sample", (NS, D), (DB, DS, D)),
         ("conv_prompt", (2, DC), (1, 1, 2, DC)), ("k_prompt", (SEQ, DA), (1, 1, SEQ, H, HD)),
         ("v_prompt", (SEQ, DA), (1, 1, SEQ, H, HD)), ("lf_prompt", (SEQ, H), (1, 1, SEQ, H)),
         ("mk_prompt", (NMEM, XH * XD), (1, 1, NMEM, XH, XD)), ("mv_prompt", (NMEM, XH * XD), (1, 1, NMEM, XH, XD)),
         ("conv_sample", (DB * 2, DC), (1, DB, 2, DC)), ("k_sample", (NS, DA), (1, DB, DS, H, HD)),
         ("v_sample", (NS, DA), (1, DB, DS, H, HD)), ("lf_sample", (NS, H), (1, DB, DS, H))]


def lay_out(a):
    a = {k: np.asarray(v) for k, v in a.items()}
    out = {"consts": constants()}
    out["x"] = np.concatenate([a["x_prompt"].reshape(SEQ, D), a["x_sample"].reshape(NS, D)])
    for k in ("cache_k", "cache_v"):
        out[k] = a[k].reshape(-1, PAGE, H * HD)
    out["cache_logf"] = a["cache_logf"].reshape(-1, PAGE * H)
    for k in ("cache_mem_k", "cache_mem_v"):
        out[k] = a[k].reshape(DB, NMEM, XH * XD)
    out["state_conv"] = a["state_conv"].reshape(DB * 2, DC)
    out["pages"] = a["page_table"].reshape(1, DB * PAGES)
    out["mem_prompt"] = a["mem_prompt"].reshape(NMEM, D)
    for k in ("norm_mix", "norm_xattn", "norm_mem", "norm_ffn", "norm_final"):
        out[k] = a[k].reshape(1, D)
    for k in ("w_in", "w_up_conv", "w_up_attn", "w_mix_out", "w_xq", "w_xk", "w_xv", "w_xo"):
        out[k] = a[k][0]
    for k in ("w_expert_gate", "w_expert_up", "w_expert_down"):
        out[k] = a[k][0]
    convp = np.zeros((P, 4 * KC + 1), np.float32)
    convp[:, :3 * KC] = a["conv_w"][0].reshape(3, KC, P).transpose(2, 0, 1).reshape(P, 3 * KC)
    convp[:, 3 * KC:4 * KC] = a["conv_b"][0].reshape(KC, P).T
    convp[:H, 4 * KC] = a["b_forget"][0]
    out["convp"] = convp
    out["w_router"] = np.concatenate([a["w_router_group"][0], a["w_router_expert"][0].transpose(1, 0, 2).reshape(D, NE)], 1)
    return {k: np.ascontiguousarray(v) for k, v in out.items()}


def kernel(**inputs):
    import concourse.bacc as bacc
    from concourse.bass_utils import run_bass_kernel_spmd

    nc = bacc.Bacc("TRN2", target_bir_lowering=False, num_devices=1)
    arrays = lay_out(inputs)
    t = {k: nc.dram_tensor("in_" + k, v.shape, mybir.dt.from_np(v.dtype), kind="ExternalInput").ap()
         for k, v in arrays.items()}
    for name, shape, _ in _OUTS:
        t[name] = nc.dram_tensor("out_" + name, shape, F32, kind="ExternalOutput").ap()
    build_program(nc, t)
    r = run_bass_kernel_spmd(nc, [{"in_" + k: v for k, v in arrays.items()}], core_ids=[0])
    return tuple(r.results[0]["out_" + name].reshape(shape) for name, _, shape in _OUTS)
```

```python
from contextlib import ExitStack

import numpy as np

import concourse.bass as bass
from concourse import mybir

F32 = mybir.dt.float32
F32R = mybir.dt.float32r
BF16 = mybir.dt.bfloat16
I32 = mybir.dt.int32
U32 = mybir.dt.uint32
ALU = mybir.AluOpType
ACT = mybir.ActivationFunctionType
AX = mybir.AxisListType.X
ds = bass.ds

P = 128
D = 1024
KD = D // P
SEQ = 1024
DB, DS = 8, 4
NS = DB * DS
NT = SEQ + NS
PT = SEQ // P
TILES = PT + 1
DC = D // 2
KC = DC // P
H, HD = 8, 64
DA = H * HD
QH = DS * H
PAST, PAGE = 4096, 128
PAGES = PAST // PAGE
NMEM = 256
XH, XD = 4, 128
NG, EG = 4, 8
NE = NG * EG
DE = D // 2
BLK = 128
MAXB = -(-(NT * 2 + NE * (BLK - 1)) // BLK)
EPS = 1e-6
NEG = -1e30
COLS = 3
NC_ = NT // COLS
HALO = 2
UW = HALO + SEQ + DB * (HALO + DS)
O_CB, O_CC, O_CX, O_Q, O_K, O_V = (n * 512 for n in range(6))
O_FZ = 6 * 512
O_GA = O_FZ + H
O_GB = O_GA + D
RING_ORDER = ["cc", "cx", "cb", "q", "k", "v", "xk", "xv", "ga0", "gb0", "ga1", "gb1", "mo0", "mo1", "xq", "xo"]


def rows_of(i):
    return P if i < PT else NS


def cols_of(n):
    return slice(n * NC_, (n + 1) * NC_)


C_ID, C_CAUSAL, C_BEFORE, C_PAGES, C_MASK = 0, P, 2 * P, 3 * P, 4 * P
C_DIAG = C_MASK + DB * NS
C_SELQ = C_DIAG + DA
C_GRP = C_SELQ + DS
C_EXP = C_GRP + NE
C_BLK = C_EXP + NE
C_TOK = C_BLK + MAXB
CW = C_TOK + TILES


def constants():
    c = np.zeros((P, CW), np.float32)
    r = np.arange(P)
    c[:, C_ID:C_ID + P] = np.eye(P)
    c[:, C_CAUSAL:C_CAUSAL + P] = np.where(r[None, :] <= r[:, None], 0.0, NEG)
    c[:, C_BEFORE:C_BEFORE + P] = r[:, None] < r[None, :]
    g, j = r // PAGES, r % PAGES
    c[:, C_PAGES:C_PAGES + P] = (g[:, None] == g[None, :]) & (j[:, None] > j[None, :])
    qh, s = np.arange(DS * H), np.arange(NS)
    own = (s[None, None, :] // DS == np.arange(DB)[None, :, None]) & (s[None, None, :] % DS <= (qh // H)[:, None, None])
    c[:QH, C_MASK:C_MASK + DB * NS] = np.where(own, 0.0, NEG).reshape(QH, -1)
    for part in range(2):
        rows = slice(part * QH, (part + 1) * QH)
        c[rows, C_DIAG:C_DIAG + DA] = (qh % H)[:, None] == (np.arange(DA) // HD)[None, :]
        c[rows, C_SELQ:C_SELQ + DS] = (qh // H)[:, None] == np.arange(DS)[None, :]
    c[:, C_GRP:C_GRP + NE] = np.arange(NE) // EG
    c[:, C_EXP:C_EXP + NE] = np.arange(NE)
    c[:, C_BLK:C_BLK + MAXB] = np.arange(MAXB)
    c[:, C_TOK:C_TOK + TILES] = r[:, None] + P * np.arange(TILES)[None, :]
    return c


def rev_selectors():
    r, qh = np.arange(P), np.arange(QH)
    sel = [(r[:, None] % 8 == g) & (r[:, None] // 8 % H == qh[None, :] % H) for g in range(8)]
    return np.stack(sel, 1).reshape(P, 8 * QH).astype(np.float32)


class Results:

    def __init__(self, full, by_act, by_dve):
        self.full, self.by = full, {"act": by_act, "dve": by_dve}
        self.order, self.index, self.count = [], {}, {"act": 0, "dve": 0}

    def add(self, reader, *tag):
        self.count[reader] += 1
        self.index[tag] = len(self.order)
        self.order.append((reader, self.count[reader]))

    def bank(self, *tag):
        return self.index[tag] % 8

    def pe_free(self, pe, *tag):
        e = self.index[tag] - 8
        if e >= 0:
            reader, n = self.order[e]
            pe.wait_ge(self.by[reader], n)

    def made(self, eng, *tag):
        eng.wait_ge(self.full, self.index[tag] + 1)

    def read(self, eng, *tag):
        reader, n = self.order[self.index[tag]]
        eng.wait_ge(self.by[reader], n)


def build_program(nc, t):
    ctx = ExitStack()
    with ctx:
        top = [16512]

        def area(nbytes):
            at = top[0]
            top[0] += -(-nbytes // 32) * 32
            assert top[0] <= 229344, top[0]
            return at

        def at(name, shape, offset, dt=F32):
            return nc.alloc_sbuf_tensor_at(name, shape, dt, offset=offset).ap()

        def new(name, shape, dt=F32):
            n = 4 if dt != BF16 else 2
            for s in shape[1:]:
                n *= s
            return at(name, shape, area(n), dt)

        def sem(name):
            return ctx.enter_context(nc.semaphore(name))

        consts = new("consts", [P, CW])
        ident = consts[:, C_ID:C_ID + P]
        identb = new("identb", [P, P], BF16)
        causalb = new("causalb", [P, P], BF16)
        a_gain = area(D * 4)
        gain = at("gain", [P, D], a_gain)
        ss = new("ss", [P, 6, TILES])
        convp = new("convp", [P, 4 * KC + 1])
        ones = new("ones", [P, 1])
        pages = new("pages", [1, DB * PAGES], I32)
        wgt = new("wgt", [P, 2, TILES])
        dest = new("dest", [P, 2, TILES], I32)
        pairs = new("pairs", [P, 2, TILES, 2], I32)
        blke = new("blke", [1, MAXB + 1], I32)
        nblk = new("nblk", [1, 1], I32)
        rowi = new("rowi", [P, 1], I32)
        outi = new("outi", [P, 1], I32)
        memKT = new("memKT", [P, XH, NMEM])
        memV = new("memV", [P, 2, XH * XD])
        qs = new("qs", [P, KC, NS])
        ks = new("ks", [P, KC, NS])
        a_norm = area(KD * NT * 4)
        xnT = at("xnT", [P, KD, NT], a_norm)
        a_ring = area(2 * KD * 512 * 4)
        ring = [at(f"ring{s}", [P, KD, 512], a_ring + s * KD * 512 * 4) for s in range(2)]
        a_v = area(TILES * DA * 4)
        a_u = area(KC * UW * 4)
        a_o = area(KC * NT * 4)
        vtok = at("vtok", [P, TILES, DA], a_v)
        uT = at("uT", [P, KC, UW], a_u)
        cyT = at("cyT", [P, KC, NT], a_o)
        oT = at("oT", [P, KC, NT], a_u)
        resid = at("resid", [P, TILES, D], a_v)
        a_qk = area(2 * KC * NT * 4)
        qT = at("qT", [P, KC, NT], a_qk)
        kT = at("kT", [P, KC, NT], a_qk + KC * NT * 4)
        mixT = at("mixT", [P, KD, NT], a_qk)
        w = top[0]
        xs = [at(f"xs{p}", [P, D], w + p * 4096) for p in range(2)]
        xf = xs + [at(f"xf{p}", [P, D], w + p * 4096) for p in (3, 4)]
        junk = at("junk", [P, D], w + 2 * 4096)
        mem = at("mem", [P, 2, D], w + 3 * 4096)
        memT = at("memT", [P, KD, NMEM], w + 5 * 4096)
        stage = [at(f"stage{p}", [P, 512], w + 7 * 4096 + p * 2048) for p in range(2)]
        wfz = at("wfz", [P, KD, H], w + 8 * 4096)
        halo = at("halo", [2 * DB, DC], w + 8 * 4096 + 256)
        tailT = at("tailT", [P, KC, 2 + 2 * DB], w + 8 * 4096 + 2304)
        tail = at("tail", [2 + 2 * DB, DC], w + 8 * 4096 + 2656)
        lfo = at("lfo", [P, TILES, H], w + 8 * 4096 + 4704)
        lf = at("lf", [H, 4, NT], a_u)
        assert w + 8 * 4096 + 4992 <= 229376

        ps = [ctx.enter_context(nc.psum_tensor(f"ps{n}", [P, 1024], F32)) for n in range(4)]

        def bank(n):
            return ps[n // 2][:, (n % 2) * 512:(n % 2) * 512 + 512]

        prob = [at(f"prob{p}", [P, SEQ], w + p * 4096) for p in range(2)]
        probT = [at(f"probT{p}", [P, PT, P], w + (2 + p) * 4096) for p in range(2)]
        qz = [at(f"qz{p}", [P, SEQ], w + (4 + p) * 4096) for p in range(2)]
        negk = [at(f"negk{p}", [P, SEQ], w + (6 + p) * 4096) for p in range(2)]
        pair = at("pair", [P, PT, P], w + 8 * 4096)
        fstat = at("fstat", [P, 4, 4], w + 9 * 4096)
        past = at("past", [P, 2, PAGE * H], a_qk)
        after = at("after", [P, 2, H, PAGE], a_qk + 8192)
        ptot = at("ptot", [P, 2, H], a_qk + 16384)
        pgi = at("pgi", [P, 2], a_qk + 16384 + 64, I32)
        after_hi = at("after_hi", [P, 2, H, PAGE], a_qk)
        kpT_hi = [at(f"kpT_hi{s}", [P, KC, 512], a_qk + s * 8192, F32R) for s in range(2)]
        kpT_lo = [at(f"kpT_lo{s}", [P, KC, 512], a_qk + 16384 + s * 8192, F32R) for s in range(2)]
        vpage = [at(f"vpage{s}", [P, 4, DA], a_ring + s * 8192) for s in range(4)]
        v_lo = [at(f"v_lo{s}", [P, 4, DA], a_ring + s * 8192, F32R) for s in range(4)]
        kpage = [at(f"kpage{s}", [P, 4, DA], a_v + s * 8192) for s in range(2)]
        rev_f = gain[:, 0:512]
        rev = at("rev", [P, 512], a_gain + 2048, F32R)
        sprob = at("sprob", [QH, PAST + NS], w)
        w2 = w + (PAST + NS) * 4
        sprobT = at("sprobT", [P, PAGES, 2 * QH], w2, F32R)
        snewT_f = at("snewT", [NS, 2 * QH], w2 + 8192)
        snewT = snewT_f.bitcast(F32R)
        own = at("own", [2 * QH, DA], w2 + 8448)
        qb = at("qb", [P, KC * (2 * QH + 2)], w2 + 10496, F32R)
        qb_f = qb.bitcast(F32)
        nbias = at("nbias", [QH, DB, NS], w2 + 11552)
        nd = at("nd", [QH, NS], w2 + 12576)
        nb = at("nb", [QH, 2, NS], w2 + 12704)
        sstat = at("sstat", [QH, 24], w2 + 12960)
        srecip = at("srecip", [2 * QH, 1], w2 + 13056)
        v_hi = [at(f"v_hi{s}", [P, 2, DA], w2 + 13088 + s * 4096, F32R) for s in range(2)]
        revsel = at("revsel", [P, 8 * QH], a_qk + 32768, F32R)

        upc = at("upc", [P, KC, D], a_v)
        upa = at("upa", [P, KC, D], w)
        gate = [[at(f"gate{m}{p}", [P, NC_], w2 + (2 * m + p) * NC_ * 4) for p in range(2)] for m in range(2)]
        xr = [at(f"xr{p}", [P, D], w2 + 8448 + p * 4096) for p in range(2)]
        a_x = a_v + TILES * D * 4
        assert a_x + 15600 <= a_qk
        q2T = at("q2T", [P, XH, NT], a_qk)
        o2T = at("o2T", [P, XH, NT], a_qk + XH * NT * 4)
        xp = [at(f"xp{p}", [P, XH, NMEM], w + p * 4096) for p in range(2)]
        xpT = [at(f"xpT{p}", [P, 2 * XH, P], w + (2 + p) * 4096) for p in range(2)]
        CKS = 6
        ck = [at(f"ck{p}", [P, 2, XH * XD], a_ring + p * 4096 if p < 4 else w + p * 4096) for p in range(CKS)]
        ckT = [at(f"ckT{p}", [P, XH, NMEM], w + (6 + p) * 4096) for p in range(2)]
        cv = at("cv", [P, DB, 2, XH * XD], a_norm)
        qp = at("qp", [P, DB * XH * 32], a_x)
        sp_ = at("sp_", [P, NMEM], a_x + 4096)
        spT = at("spT", [P, 2, P], a_x + 5120)
        xstat = at("xstat", [P, 2, 16], a_x + 6144)
        sxstat = at("sxstat", [P, 4], a_x + 6272)
        wr = at("wr", [P, KD, NG + NE], a_x + 6304)
        a_r = a_x + 6304 + 1152
        lgT = at("lgT", [NG + NE, NT], a_r)
        lg = at("lg", [P, TILES, NG + NE], a_r + 4224)
        t4 = [at(f"t4_{n}", [P, TILES, NG], w + 8 * 4096 + n * 160) for n in range(3)]
        t32 = [at(f"t32_{n}", [P, TILES, NE], w + 2 * 4096 + n * 1152) for n in range(7)]
        t1 = at("t1", [P, 16, TILES], w + 8 * 4096 + 512)
        cnt = at("cnt", [P, 4, NE], w + 8 * 4096 + 1120)
        cnti = at("cnti", [P, NE], w + 8 * 4096 + 1632, I32)
        hot = at("hot", [P, TILES, NE], w + 8 * 4096 + 1760, BF16)
        empty = at("empty", [P, MAXB + 3, 2], w + 8 * 4096 + 2336, I32)
        beforeb = at("beforeb", [P, P], w + 8 * 4096 + 2784, BF16)
        onesb = at("onesb", [P, P], w + 8 * 4096 + 3040, BF16)
        bcmp = at("bcmp", [1, MAXB, NE], w)
        bsum = at("bsum", [1, MAXB], w + MAXB * NE * 4)
        wg, wu = ring
        wd = at("wd", [P, DE // P, D], a_qk)
        xg = at("xg", [P, D], w)
        xgT = at("xgT", [P, KD, BLK], w + 4096)
        sg = at("sg", [P, DE], w + 8192)
        hh = at("hh", [P, DE], w + 8192 + 2048)
        hT = at("hT", [P, DE // P, BLK], w + 8192 + 4096)
        yb = at("yb", [P, D], w + 8192 + 6144)
        yy = [at(f"yy{i}", [P, 2, D], (a_norm if i < 4 else a_ring) + i % 4 * 8192) for i in range(PT)]

        x3_d = nc.dram_tensor("x3_d", (NT, D), F32, kind="Internal").ap()
        row_d = nc.dram_tensor("row_d", ((MAXB + 3) * BLK, 2), I32, kind="Internal").ap()
        y_d = nc.dram_tensor("y_d", (2 * NT + 1, D), F32, kind="Internal").ap()
        rev_d = nc.dram_tensor("rev_d", (DB, 2, H, PAST), F32, kind="Internal").ap()
        neg_d = nc.dram_tensor("neg_d", (H, NT), F32, kind="Internal").ap()

        consts_in, gain_in, gain_used = sem("consts_in"), sem("gain_in"), sem("gain_used")
        x_in = [sem(f"x_in{i}") for i in range(TILES)]
        mem_in, halo_in, wfz_in = sem("mem_in"), sem("halo_in"), sem("wfz_in")
        ring_in = [sem(f"ring_in{s}") for s in range(2)]
        passed = sem("passed")
        made_up = sem("made_up")
        tail_got, abs_ready, ln_ready, lf_ready, neg_ready = (
            sem(n) for n in ("tail_got", "abs_ready", "ln_ready", "lf_ready", "neg_ready"))
        stage_stored = [sem(f"stage_stored{p}") for p in range(2)]
        neg_stored, stored = sem("neg_stored"), sem("stored")
        past_in, pgi_in, totals_ready, after_ready, rev_stored = (
            sem(n) for n in ("past_in", "pgi_in", "totals_ready", "after_ready", "rev_stored"))
        negk_in = [sem(f"negk_in{p}") for p in range(2)]
        qz_cleared = sem("qz_cleared")
        qz_ready = sem("qz_ready")
        fs_full, fs_max, fs_exp = sem("fs_full"), sem("fs_max"), sem("fs_exp")
        ft_full, ft_act, ft_dve = sem("ft_full"), sem("ft_act"), sem("ft_dve")
        fo_full, fo_read = sem("fo_full"), sem("fo_read")
        fp_full, fp_read = sem("fp_full"), sem("fp_read")
        k_in = [sem(f"k_in{s}") for s in range(2)]
        v_in = [sem(f"v_in{s}") for s in range(4)]
        rev_in, revsel_in, nd_in, qb_ready = sem("rev_in"), sem("revsel_in"), sem("nd_in"), sem("qb_ready")
        rev_used = sem("rev_used")
        v_used = sem("v_used")
        v_rounded, v_split = sem("v_rounded"), sem("v_split")
        kt_full = sem("kt_full")
        kt_hi, kt_lo = sem("kt_hi"), sem("kt_lo")
        sc_full, sc_low, sc_read = sem("sc_full"), sem("sc_low"), sem("sc_read")
        s_max, s_exp = sem("s_max"), sem("s_exp")
        t2_full, t2_hi, t2_lo = sem("t2_full"), sem("t2_hi"), sem("t2_lo")
        so_full, so_read, sx_full, sx_read = sem("so_full"), sem("so_read"), sem("sx_full"), sem("sx_read")
        upc_in, upa_in, mixed = sem("upc_in"), sem("upa_in"), sem("mixed")
        xr_in = [sem(f"xr_in{p}") for p in range(2)]
        ck_in = [sem(f"ck_in{p}") for p in range(CKS)]
        cv_in, qp_ready = sem("cv_in"), sem("qp_ready")
        x_max, x_exp, x_norm = sem("x_max"), sem("x_exp"), sem("x_norm")
        sx_max, sx_exp, sx_norm = sem("sx_max"), sem("sx_exp"), sem("sx_norm")
        wr_in, empty_ready, empty_stored, g_sub, g_exp, e_sub, e_exp, hot_ready = (
            sem(n) for n in ("wr_in", "empty_ready", "empty_stored", "g_sub", "g_exp", "e_sub", "e_exp", "hot_ready"))
        dest_ready = sem("dest_ready")
        x3_stored = [sem(f"x3_stored{p}") for p in range(4)]
        routed, rows_stored = sem("routed"), sem("rows_stored")
        wg_in, wu_in, wd_in, rowi_in, outi_in, xg_in, y_stored = (
            sem(n) for n in ("wg_in", "wu_in", "wd_in", "rowi_in", "outi_in", "xg_in", "y_stored"))
        y_free = sem("y_free")
        xt_full, xt_read, g_full, sg_ready, u_full, h_ready, ht_full, ht_read, d_full, d_read = (
            sem(n) for n in ("xt_full", "xt_read", "g_full", "sg_ready", "u_full", "h_ready", "ht_full", "ht_read",
                             "d_full", "d_read"))
        summed = sem("summed")
        y_out = [sem(f"y_out{p}") for p in range(4)]
        R = Results(sem("result_full"), sem("read_by_act"), sem("read_by_dve"))

        FN = [(f, n) for f in range(KC) for n in range(COLS)]
        for i in range(TILES):
            R.add("act", "nmix", i, 0), R.add("act", "nmix", i, 1)
        R.add("dve", "later", 0), R.add("dve", "later", 1)
        R.add("dve", "halo")
        for name, reader in (("cc", "act"), ("cx", "dve"), ("cb", "dve")):
            for f, n in FN:
                R.add(reader, name, f, n)
        R.add("dve", "tail")
        for i in range(2):
            R.add("act", "nmem", i, 0), R.add("act", "nmem", i, 1)
        for name in "qk":
            for f, n in FN:
                R.add("act", name, f, n)
        for n in range(COLS):
            R.add("dve", "fz", n)
        for i in range(TILES):
            R.add("act", "v", i)
        for i in range(TILES):
            R.add("act", "kout", i)
        R.add("dve", "lf")
        for name in ("mk", "mkT", "mv"):
            for i in range(2):
                R.add("act", name, i)

        FN8 = [(f, n) for f in range(KD) for n in range(COLS)]
        for f, n in FN8:
            R.add("act", "ga", f, n), R.add("dve", "yc", f, n), R.add("act", "gb", f, n), R.add("dve", "ya", f, n)
        for i in range(TILES):
            R.add("dve", "mo", i, 0), R.add("dve", "mo", i, 1)
        for i in range(TILES):
            R.add("act", "nxat", i, 0), R.add("act", "nxat", i, 1)
        for f, n in FN:
            R.add("act", "xq", f, n)
        R.add("act", "xs", 0, 0), R.add("act", "xs", 0, 1)
        for i in range(PT):
            if i + 1 < PT:
                R.add("act", "xs", i + 1, 0), R.add("act", "xs", i + 1, 1)
            R.add("act", "xt", i, 0), R.add("dve", "xt", i, 1)
            if i:
                R.add("dve", "xo", i - 1)
        R.add("dve", "xo", PT - 1)
        for b in range(DB):
            R.add("act", "ckT", b, 0), R.add("dve", "ckT", b, 1)
            if b % 2:
                R.add("dve", "ss", b // 2)
        for i in range(PT):
            R.add("dve", "h2", i, 0), R.add("dve", "h2", i, 1)
        R.add("act", "spT")
        R.add("act", "so")
        R.add("dve", "h2", PT, 0), R.add("dve", "h2", PT, 1)
        for i in range(TILES):
            R.add("act", "nffn", i, 0), R.add("act", "nffn", i, 1)
        for n in range(COLS):
            R.add("act", "lgT", n)
        R.add("dve", "lg")
        R.add("dve", "rank")

        class Norm:

            def __init__(self, name, slot, n, parts=None, bufs=None):
                self.bufs = bufs or xs
                self.parts = parts or [(0, n)]
                self.name, self.stat, self.n = name, ss[:, slot, 0:n], n
                self.rows = (lambda i: P) if n < TILES else rows_of
                self.squared = sem(name + "_squared")
                self.mean = sem(name + "_mean")
                self.root = sem(name + "_root")
                self.scaled = sem(name + "_scaled")

            def act_stats(self, act, src, wait_src):
                for k, (i0, i1) in enumerate(self.parts):
                    for i in range(i0, i1):
                        r = self.rows(i)
                        wait_src(i)
                        if i:
                            act.drain()
                        nc.scalar.activation(junk[0:r, :], src(i)[0:r, :], ACT.Square,
                                             accum_out=self.stat[0:r, i:i + 1]).then_inc(self.squared, 1)
                    act.wait_ge(self.mean, k + 1)
                    nc.scalar.activation(self.stat[:, i0:i1], self.stat[:, i0:i1], ACT.Sqrt).then_inc(self.root, 1)

            def dve_scale(self, dve, src, gain_load, free=None):
                free = free or (lambda i: R.made(dve, self.name, i, 1))
                for k, (i0, i1) in enumerate(self.parts):
                    stat = self.stat[:, i0:i1]
                    dve.wait_ge(self.squared, i1)
                    nc.vector.tensor_scalar(stat, stat, 1.0 / D, EPS, ALU.mult, ALU.add).then_inc(self.mean, 1)
                    dve.wait_ge(self.root, k + 1)
                    nc.vector.reciprocal(stat, stat)
                    dve.drain()
                    dve.wait_ge(gain_in, 16 * gain_load)
                    for i in range(i0, i1):
                        r = self.rows(i)
                        if i >= len(self.bufs):
                            free(i - len(self.bufs))
                        nc.vector.scalar_tensor_tensor(self.bufs[i % len(self.bufs)][0:r, :], src(i)[0:r, :], self.stat[0:r, i:i + 1],
                                                       gain[0:r, :], ALU.mult, ALU.mult).then_inc(self.scaled, 1)
                dve.drain()
                dve.sem_inc(gain_used, 1)

            def pe_turn(self, pe):
                for i in range(self.n):
                    r = self.rows(i)
                    pe.wait_ge(self.scaled, i + 1)
                    for half in range(2):
                        R.pe_free(pe, self.name, i, half)
                        out = bank(R.bank(self.name, i, half))
                        for c in range(4):
                            f = (half * 4 + c) * P
                            last = nc.tensor.transpose(out[:, c * P:c * P + r], self.bufs[i % len(self.bufs)][0:r, f:f + P], ident[0:r, 0:r])
                        last.then_inc(R.full, 1)

            def act_copy(self, act, dst):
                for i in range(self.n):
                    r = self.rows(i)
                    for half in range(2):
                        R.made(act, self.name, i, half)
                        src = bank(R.bank(self.name, i, half)).rearrange("p (c x) -> p c x", c=4)[:, :, 0:r]
                        nc.scalar.activation(dst[:, half * 4:half * 4 + 4, i * P:i * P + r], src,
                                             ACT.Copy).then_inc(R.by["act"], 1)

        n_mix, n_mem = Norm("nmix", 0, TILES, [(0, 2), (2, 5), (5, TILES)]), Norm("nmem", 1, 2)
        n_xat, n_ffn, n_fin = Norm("nxat", 2, TILES, bufs=xf), Norm("nffn", 3, TILES, bufs=xf), Norm("nfin", 4, TILES, [(0, PT), (PT, TILES)], xf)

        ring_xo = ring[1].rearrange("p k n -> p (k n)").rearrange("p (k n) -> p k n", k=KC)
        N_POOL = t["cache_k"].shape[0]

        def units():
            return [(u, u // PT, u % PT) for u in range(2 * PT)]

        def groups(u):
            i, first = u % PT, (u // PT) * 12 + (u % PT if u % PT < 4 else 2 * (u % PT) - 4)
            return [(first + g, 4 * g, min(4, i + 1 - 4 * g)) for g in range(1 if i < 4 else 2)]

        def w3(ap, c0, width=512):
            return ap.rearrange("(k p) n -> p k n", p=P)[:, :, c0:c0 + width]

        LOADS = {"cc": (w3(t["w_in"], O_CC), None), "cx": (w3(t["w_in"], O_CX), None),
                 "cb": (w3(t["w_in"], O_CB), ("cc", KC - 1, COLS - 1)), "q": (w3(t["w_in"], O_Q), ("cx", KC - 1, COLS - 1)),
                 "k": (w3(t["w_in"], O_K), ("cb", KC - 1, COLS - 1)), "v": (w3(t["w_in"], O_V), ("q", KC - 1, COLS - 1)),
                 "xk": (w3(t["w_xk"], 0), ("k", KC - 1, COLS - 1)), "xv": (w3(t["w_xv"], 0), ("v", TILES - 1)),
                 "ga0": (w3(t["w_in"], O_GA), None), "gb0": (w3(t["w_in"], O_GB), None),
                 "ga1": (w3(t["w_in"], O_GA + 512), ("ga", 3, COLS - 1)), "gb1": (w3(t["w_in"], O_GB + 512), ("gb", 3, COLS - 1)),
                 "mo0": (w3(t["w_mix_out"], 0), ("ga", 7, COLS - 1)), "mo1": (w3(t["w_mix_out"], 512), ("gb", 7, COLS - 1)),
                 "xq": (w3(t["w_xq"], 0), ("mo", TILES - 1, 0)), "xo": (w3(t["w_xo"], 0, D), ("mo", TILES - 1, 1))}

        def ring_load(sp, name):
            n = RING_ORDER.index(name)
            src, after = LOADS[name]
            if after is not None:
                R.made(sp, *after)
            dst = ring[n % 2] if src.shape[1] == KD else ring_xo
            sp.dma_start(dst, src).then_inc(ring_in[n % 2], 16)

        def ring_slot(pe, name):
            n = RING_ORDER.index(name)
            pe.wait_ge(ring_in[n % 2], 16 * (n // 2 + 1))
            return ring[n % 2]

        def samples(row):
            return row[:, HALO + SEQ:UW].rearrange("p (b s) -> p b s", b=DB)

        def apart(eng):
            eng.sem_inc(passed, 1)

        block = ctx.enter_context(nc.Block())

        @block.sync
        def _(sp):
            sp.dma_start(consts, t["consts"]).then_inc(consts_in, 16)
            sp.dma_start(convp, t["convp"]).then_inc(consts_in, 16)
            sp.dma_start(pages, t["pages"]).then_inc(consts_in, 16)
            with nc.allow_non_contiguous_dma("page numbers, one per partition"):
                sp.dma_start(pgi, t["pages"].rearrange("a (g p) -> p (a g)", g=2)).then_inc(pgi_in, 16)
            sp.dma_start(gain, t["norm_mix"].to_broadcast([P, D])).then_inc(gain_in, 16)
            for i in range(TILES):
                sp.dma_start(resid[0:rows_of(i), i, :], t["x"][i * P:i * P + rows_of(i), :]).then_inc(x_in[i], 16)
            for name in ("cc", "cx"):
                ring_load(sp, name)
            sp.dma_start(halo, t["state_conv"]).then_inc(halo_in, 16)
            with nc.allow_non_contiguous_dma("8 columns of w_in"):
                sp.dma_start(wfz, w3(t["w_in"], O_FZ, H)).then_inc(wfz_in, 16)
            sp.dma_start(mem, t["mem_prompt"].rearrange("(i p) d -> p i d", p=P)).then_inc(mem_in, 16)
            sp.wait_ge(gain_used, 1)
            sp.dma_start(gain, t["norm_mem"].to_broadcast([P, D])).then_inc(gain_in, 16)
            for name in ("cb", "q", "k", "v", "xk", "xv"):
                ring_load(sp, name)
            sp.wait_ge(neg_stored, 16)
            R.read(sp, "mv", 1)
            sp.wait_ge(stage_stored[0], 16 * 6), sp.wait_ge(stage_stored[1], 16 * 5)
            for p in range(2):
                sp.dma_start(negk[p], neg_d[p:p + 1, 0:SEQ].to_broadcast([P, SEQ])).then_inc(negk_in[p], 16)
            with sp.Fori(1, H // 2) as hp:
                for p in range(2):
                    sp.wait_ge(fs_max, hp * 16 - 8 + 8 * p)
                    sp.dma_start(negk[p], neg_d[ds(hp * 2 + p, 1), 0:SEQ].to_broadcast([P, SEQ])
                                 ).then_inc(negk_in[p], 16)
            sp.wait_ge(fp_full, 1 + H // 2)
            sp.wait_ge(rev_stored, 16 * 2 * DB)
            for q in range(DS):
                sp.dma_start(nd[q * H:(q + 1) * H, :], neg_d[:, SEQ:NT]).then_inc(nd_in, 16)
            sp.dma_start(gain[:, 0:8 * QH], t["revsel"]).then_inc(revsel_in, 16)
            with sp.Fori(0, DB) as b:
                for g in range(PAGES // 4):
                    if g == 2:
                        sp.wait_ge(rev_used, b + 1)
                        sp.dma_start(rev_f, rev_d[ds(b, 1)].rearrange("a x h (g s) -> (a x h g) s", g=8)
                                     ).then_inc(rev_in, 16)
                    sp.wait_ge(kt_full, b * 32 + g * 4 + 4)
                    for p in range(4):
                        page = sp.value_load(pages[0:1, ds(b * PAGES + (g * 4 + p), 1)], min_val=0, max_val=N_POOL - 1)
                        sp.dma_start(kpage[g % 2][:, p, :], t["cache_k"][ds(page, 1)].rearrange("a s d -> (a s) d")
                                     ).then_inc(k_in[g % 2], 16)

            sp.wait_ge(kt_full, DB * 32 + 8)
            sp.dma_start(upc, t["w_up_conv"].rearrange("(k p) n -> p k n", p=P)).then_inc(upc_in, 16)
            sp.wait_ge(v_used, 16 * (DB - 1) + 12 + 8)
            ring_load(sp, "ga0")
            sp.wait_ge(so_full, DB)
            ring_load(sp, "gb0")
            sp.dma_start(upa, t["w_up_attn"].rearrange("(k p) n -> p k n", p=P)).then_inc(upa_in, 16)
            sp.wait_ge(sx_read, DB + 2)
            for i in range(2):
                sp.dma_start(xr[i], t["x"][i * P:(i + 1) * P, :]).then_inc(xr_in[i], 16)
            sp.wait_ge(gain_used, 2)
            sp.dma_start(gain, t["norm_xattn"].to_broadcast([P, D])).then_inc(gain_in, 16)
            for name in ("ga1", "gb1", "mo0", "mo1"):
                ring_load(sp, name)
            for i in range(2, TILES):
                R.read(sp, "mo", i - 2, 1)
                sp.dma_start(xr[i % 2][0:rows_of(i), :], t["x"][i * P:i * P + rows_of(i), :]).then_inc(xr_in[i % 2], 16)
            for name in ("xq", "xo"):
                ring_load(sp, name)
            sp.dma_start(wr, t["w_router"].rearrange("(k p) n -> p k n", p=P)).then_inc(wr_in, 16)
            R.made(sp, "xq", KC - 1, COLS - 1)
            for b in range(CKS):
                sp.dma_start(ck[b], t["cache_mem_k"][b].rearrange("(i p) d -> p i d", p=P)).then_inc(ck_in[b], 16)
            sp.dma_start(cv, t["cache_mem_v"].rearrange("b (i p) d -> p b i d", p=P)).then_inc(cv_in, 16)
            sp.wait_ge(gain_used, 3)
            sp.dma_start(gain, t["norm_ffn"].to_broadcast([P, D])).then_inc(gain_in, 16)
            for b in range(CKS, DB):
                R.made(sp, "ckT", b - CKS, 1)
                sp.dma_start(ck[b % CKS], t["cache_mem_k"][b].rearrange("(i p) d -> p i d", p=P)).then_inc(ck_in[b % CKS], 16)
            sp.wait_ge(gain_used, 4)
            sp.dma_start(gain, t["norm_final"].to_broadcast([P, D])).then_inc(gain_in, 16)
            R.made(sp, "h2", TILES - 1, 1)
            sp.wait_ge(routed, 1)
            n = sp.value_load(nblk[0:1, 0:1], min_val=2, max_val=MAXB)

            def expert_load(b, which):
                src = t[which][ds(sp.value_load(blke[0:1, ds(b, 1)], min_val=0, max_val=NE - 1), 1)]
                return src.rearrange("a (k p) n -> p (a k) n", p=P)

            sp.dma_start(wg, expert_load(0, "w_expert_gate")).then_inc(wg_in, 16)
            sp.dma_start(wu, expert_load(0, "w_expert_up")).then_inc(wu_in, 16)
            sp.dma_start(wd, expert_load(0, "w_expert_down")).then_inc(wd_in, 16)
            sp.wait_ge(g_full, 1)
            sp.dma_start(wg, expert_load(1, "w_expert_gate")).then_inc(wg_in, 16)
            sp.wait_ge(u_full, 1)
            sp.dma_start(wu, expert_load(1, "w_expert_up")).then_inc(wu_in, 16)
            with sp.Fori(1, n - 1) as b:
                sp.wait_ge(g_full, b + 1)
                apart(sp)
                sp.dma_start(wg, expert_load(b + 1, "w_expert_gate")).then_inc(wg_in, 16)
                sp.wait_ge(u_full, b + 1)
                apart(sp)
                sp.dma_start(wu, expert_load(b + 1, "w_expert_up")).then_inc(wu_in, 16)
                sp.wait_ge(d_full, b * 2 + 2)
                apart(sp)
                sp.dma_start(wd, expert_load(b, "w_expert_down")).then_inc(wd_in, 16)
            sp.wait_ge(d_full, n * 2)
            apart(sp)
            sp.dma_start(wd, expert_load(n - 1, "w_expert_down")).then_inc(wd_in, 16)
            sp.wait_ge(y_stored, n * 16)
            apart(sp)
            for i in range(TILES):
                r = rows_of(i)
                if i >= PT:
                    sp.wait_ge(summed, i - PT + 1)
                for k in range(2):
                    sp.dma_start(yy[i % PT][0:r, k, :], y_d[k * NT + i * P:k * NT + i * P + r, :]).then_inc(x_in[i], 16)
            for i in range(TILES):
                sp.wait_ge(n_fin.scaled, i + 1)
                dst = t["y_prompt"][i * P:(i + 1) * P, :] if i < PT else t["y_sample"]
                sp.dma_start(dst, xf[i % 4][0:rows_of(i), :]).then_inc(y_out[i % 4], 16)
            for p in range(4):
                sp.wait_ge(y_out[p], 16 * (3 if p == 0 else 2))

        @block.tensor
        def _(pe):
            def product(tag, name, f, n):
                slot = ring_slot(pe, name)
                R.pe_free(pe, *tag)
                for k in range(KD):
                    last = nc.tensor.matmul(bank(R.bank(*tag))[:, 0:NC_], slot[:, k, f * P:(f + 1) * P],
                                            xnT[:, k, cols_of(n)], start=k == 0, stop=k == KD - 1)
                last.then_inc(R.full, 1)

            def rows_product(tag, name, src, i, r):
                slot = ring_slot(pe, name)
                R.pe_free(pe, *tag)
                for k in range(KD):
                    last = nc.tensor.matmul(bank(R.bank(*tag))[0:r, :], src[:, k, i * P:i * P + r], slot[:, k, :],
                                            start=k == 0, stop=k == KD - 1)
                last.then_inc(R.full, 1)

            def turn(tag, pieces):
                R.pe_free(pe, *tag)
                for dst, src in pieces(bank(R.bank(*tag))):
                    r = src.shape[0]
                    last = nc.tensor.transpose(dst, src, ident[0:r, 0:r])
                last.then_inc(R.full, 1)

            pe.wait_ge(consts_in, 48)
            n_mix.pe_turn(pe)
            pe.wait_ge(totals_ready, 1)
            for g in range(2):
                R.pe_free(pe, "later", g)
                nc.tensor.matmul(bank(R.bank("later", g))[:, 0:H], consts[:, C_PAGES:C_PAGES + P], ptot[:, g, :],
                                 start=True, stop=True).then_inc(R.full, 1)
            pe.wait_ge(halo_in, 16)
            turn(("halo",), lambda b: [(b[:, c * 2 * DB:(c + 1) * 2 * DB], halo[:, c * P:(c + 1) * P]) for c in range(KC)])
            R.read(pe, "nmix", TILES - 1, 1)
            for name in ("cc", "cx", "cb"):
                for f, n in FN:
                    product((name, f, n), name, f, n)
            pe.wait_ge(tail_got, 1)
            turn(("tail",), lambda b: [(b[0:2 + 2 * DB, c * P:(c + 1) * P], tailT[:, c, :]) for c in range(KC)])
            n_mem.pe_turn(pe)
            for name in "qk":
                for f, n in FN:
                    product((name, f, n), name, f, n)
            pe.wait_ge(wfz_in, 16)
            for n in range(COLS):
                R.pe_free(pe, "fz", n)
                for k in range(KD):
                    last = nc.tensor.matmul(bank(R.bank("fz", n))[0:H, 0:NC_], wfz[:, k, :], xnT[:, k, cols_of(n)],
                                            start=k == 0, stop=k == KD - 1)
                last.then_inc(R.full, 1)
            for i in range(TILES):
                rows_product(("v", i), "v", xnT, i, rows_of(i))
            for i in range(TILES):
                R.read(pe, "k", KC - 1, COLS - 1)
                turn(("kout", i), lambda b: [(b[0:rows_of(i), c * P:(c + 1) * P], kT[:, c, i * P:i * P + rows_of(i)])
                                             for c in range(KC)])
            pe.wait_ge(lf_ready, 1)
            turn(("lf",), lambda b: [(b[0:rows_of(i), i * H:(i + 1) * H], lf[:, 2, i * P:i * P + rows_of(i)])
                                     for i in range(TILES)])
            R.read(pe, "nmem", 1, 1)
            for i in range(2):
                rows_product(("mk", i), "xk", memT, i, P)
            for i in range(2):
                R.read(pe, "mk", i)
                turn(("mkT", i), lambda b: [(b[:, h * XD:(h + 1) * XD], stage[i][:, h * XD:(h + 1) * XD])
                                            for h in range(XH)])
            for i in range(2):
                rows_product(("mv", i), "xv", memT, i, P)

            R.read(pe, "mv", 1), R.read(pe, "lf")
            pe.sem_inc(fp_full, 1), pe.sem_inc(fp_read, 1)
            with pe.Fori(0, H // 2) as hp:
                def scores(u, p, i):
                    n = (i + 1) * P
                    if i == 0:
                        pe.wait_ge(qz_ready, hp * 2 + p + 1)
                    if u >= 2:
                        pe.wait_ge(fs_max, hp * 16 + u - 1)
                    for c0 in range(0, n, 512):
                        c1 = min(n, c0 + 512)
                        nc.tensor.matmul(ps[u % 2][:, c0:c1], qz[p][:, i * P:(i + 1) * P],
                                         kT.rearrange("p c n -> p (c n)")[:, ds(hp * NT + c0, c1 - c0)],
                                         start=True, stop=c1 < n)
                    nc.tensor.matmul(ps[u % 2][:, n - P:n], identb, causalb, start=False, stop=True).then_inc(fs_full, 1)

                def turn_probs(u):
                    pe.wait_ge(fs_exp, hp * 16 + u + 1)
                    for g, j0, nj in groups(u):
                        if g >= 2:
                            pe.wait_ge(ft_act if g % 2 == 0 else ft_dve, hp * 12 + g // 2)
                        for j in range(nj):
                            last = nc.tensor.transpose(bank(4 + g % 2)[:, j * P:(j + 1) * P],
                                                       prob[u % 2][:, (j0 + j) * P:(j0 + j + 1) * P], ident)
                        last.then_inc(ft_full, 1)

                def weigh(u, i):
                    done = groups(u)[-1][0] + 1
                    pe.wait_ge(ft_act, hp * 12 + (done + 1) // 2)
                    if done // 2:
                        pe.wait_ge(ft_dve, hp * 12 + done // 2)
                    if u >= 2:
                        pe.wait_ge(fo_read, hp * 16 + u - 1)
                    for j in range(i + 1):
                        last = nc.tensor.matmul(bank(6 + u % 2)[:, 0:P], probT[u % 2][:, j, :], vtok[:, j, ds(hp * P, P)],
                                                start=j == 0, stop=j == i)
                    last.then_inc(fo_full, 1)

                scores(*units()[0])
                pe.wait_ge(fp_read, hp + 1)
                for u, p, i in units():
                    if u + 1 < 2 * PT:
                        scores(*units()[u + 1])
                    turn_probs(u)
                    if u:
                        weigh(u - 1, (u - 1) % PT)
                weigh(2 * PT - 1, PT - 1)
                pe.wait_ge(fo_read, hp * 16 + 16)
                for i in range(PT):
                    last = nc.tensor.transpose(ps[2][:, i * P:(i + 1) * P], pair[:, i, :], ident)
                last.then_inc(fp_full, 1)

            pe.wait_ge(fp_read, H // 2 + 1)
            pe.sem_inc(kt_full, 8), pe.sem_inc(v_used, 8)

            def turn_keys(b, g):
                pe.wait_ge(k_in[g % 2], b * 256 + 64 * (g // 2 + 1))
                for c in range(KC):
                    if not (isinstance(b, int) and b + g == 0):
                        pe.wait_ge(kt_lo, b * 32 + 4 * (g - 1) + c + 1)
                    for p in range(4):
                        last = nc.tensor.transpose(bank(c)[:, p * PAGE:(p + 1) * PAGE],
                                                   kpage[g % 2][:, p, c * P:(c + 1) * P], ident)
                    last.then_inc(kt_full, 1)

            def sample_scores(b, g):
                pe.wait_ge(kt_lo, b * 32 + 4 * g + 4)
                if g >= 2:
                    pe.wait_ge(sc_read, b * 9 + g - 1)
                out = bank(4 + g % 2)[0:2 * QH, :]
                for c in range(KC):
                    for keys in (kpT_hi, kpT_lo):
                        last = nc.tensor.matmul(out, qb[:, c * 2 * QH:(c + 1) * 2 * QH], keys[g % 2][:, c, :],
                                                start=c == 0 and keys is kpT_hi, stop=c == KC - 1 and keys is kpT_lo)
                    if c == 0:
                        nc.tensor.matmul(out[0:QH, :], revsel[:, g * QH:(g + 1) * QH], rev, start=False, stop=False)
                last.then_inc(sc_full, 1)

            def new_scores(b):
                pe.wait_ge(sx_read, b + 1)
                for c in range(KC):
                    last = nc.tensor.matmul(bank(6)[0:2 * QH, 0:NS], qb_f[:, c * 2 * QH:(c + 1) * 2 * QH], ks[:, c, :],
                                            start=c == 0, stop=c == KC - 1)
                last.then_inc(sc_full, 1)

            def turn_sample_probs(b):
                for r in range(4):
                    pe.wait_ge(s_exp, b * 5 + r + 1)
                    if r >= 2:
                        pe.wait_ge(t2_lo, b * 5 + r - 1)
                    apart(pe)
                    for j in range(8):
                        last = nc.tensor.transpose(bank(4 + r % 2)[:, j * QH:(j + 1) * QH],
                                                   sprob[:, (r * 8 + j) * PAGE:(r * 8 + j + 1) * PAGE], ident[0:QH, 0:QH])
                    last.then_inc(t2_full, 1)
                pe.wait_ge(s_exp, b * 5 + 5)
                pe.wait_ge(sx_read, b + 2)
                apart(pe)
                nc.tensor.transpose(bank(6)[0:NS, 64:64 + QH], sprob[:, PAST:PAST + NS], ident[0:QH, 0:QH]
                                    ).then_inc(t2_full, 1)

            def weigh_pages(b, g):
                first = g == 0
                for half in range(2):
                    pe.wait_ge(v_split, b * 16 + 2 * g + half + 1)
                    for p in (2 * half, 2 * half + 1):
                        for values in (v_hi[half][:, p % 2, :], v_lo[g % 4][:, p, :]):
                            last = nc.tensor.matmul(bank(7)[0:2 * QH, :], sprobT[:, g * 4 + p, :], values, start=first,
                                                    stop=False)
                            first = False
                    last.then_inc(v_used, 1)

            def weigh_new():
                nc.tensor.matmul(bank(7)[0:2 * QH, :], snewT_f, vtok[0:NS, PT, :], start=False, stop=True
                                 ).then_inc(so_full, 1)

            def pick_own(b):
                pe.wait_ge(so_read, b + 1)
                apart(pe)
                for c in range(KC):
                    last = nc.tensor.matmul(bank(6)[:, 128 + c * DS:128 + (c + 1) * DS], own[:, c * P:(c + 1) * P],
                                            consts[0:2 * QH, C_SELQ:C_SELQ + DS], start=True, stop=True)
                last.then_inc(sx_full, 1)

            def sample_step(b, wb, more):
                pe.wait_ge(qb_ready, b + 1)
                if wb is not None:
                    pe.wait_ge(t2_lo, b * 5)
                for g in range(8):
                    sample_scores(b, g)
                    if g == 7:
                        new_scores(b)
                    if g < 6 or more:
                        turn_keys(b, g + 2)
                    if wb is not None:
                        weigh_pages(wb, g)
                if wb is not None:
                    weigh_new()
                    pick_own(wb)
                turn_sample_probs(b)

            turn_keys(0, 0), turn_keys(0, 1)
            sample_step(0, None, True)
            with pe.Fori(0, DB - 2) as b:
                sample_step(b + 1, b, True)
            sample_step(DB - 1, DB - 2, False)
            pe.wait_ge(t2_lo, DB * 5)
            for g in range(8):
                weigh_pages(DB - 1, g)
            weigh_new()
            pick_own(DB - 1)

            pe.wait_ge(sx_read, DB + 2)

            def up(tag, weight, arrived, src, f, n):
                pe.wait_ge(arrived, 16)
                R.pe_free(pe, *tag)
                for k in range(KC):
                    last = nc.tensor.matmul(bank(R.bank(*tag))[:, 0:NC_], weight[:, k, f * P:(f + 1) * P],
                                            src[:, k, cols_of(n)], start=k == 0, stop=k == KC - 1)
                last.then_inc(R.full, 1)

            for f, n in FN8:
                product(("ga", f, n), f"ga{f // 4}", f % 4, n)
                up(("yc", f, n), upc, upc_in, cyT, f, n)
                product(("gb", f, n), f"gb{f // 4}", f % 4, n)
                up(("ya", f, n), upa, upa_in, oT, f, n)
            pe.wait_ge(mixed, KD * COLS)
            for i in range(TILES):
                for half in range(2):
                    rows_product(("mo", i, half), f"mo{half}", mixT, i, rows_of(i))
            n_xat.pe_turn(pe)
            R.read(pe, "nxat", TILES - 1, 1)
            for f, n in FN:
                product(("xq", f, n), "xq", f, n)
            R.read(pe, "xq", KC - 1, COLS - 1)

            def cross_scores(i):
                for half in range(2):
                    R.pe_free(pe, "xs", i, half)
                    for h in (2 * half, 2 * half + 1):
                        last = nc.tensor.matmul(bank(R.bank("xs", i, half))[:, (h % 2) * NMEM:(h % 2 + 1) * NMEM],
                                                q2T[:, h, i * P:(i + 1) * P], memKT[:, h, :], start=True, stop=True)
                    last.then_inc(R.full, 1)

            def cross_weigh(i):
                R.read(pe, "xt", i, 0), R.read(pe, "xt", i, 1)
                R.pe_free(pe, "xo", i)
                for h in range(XH):
                    for m in range(2):
                        last = nc.tensor.matmul(bank(R.bank("xo", i))[:, h * P:(h + 1) * P], memV[:, m, h * XD:(h + 1) * XD],
                                                xpT[i % 2][:, 2 * h + m, :], start=m == 0, stop=m == 1)
                last.then_inc(R.full, 1)

            cross_scores(0)
            for i in range(PT):
                if i + 1 < PT:
                    cross_scores(i + 1)
                pe.wait_ge(x_norm, i + 1)
                for half in range(2):
                    turn(("xt", i, half), lambda b: [(b[:, j * P:(j + 1) * P], xp[i % 2][
                        :, (4 * half + j) // 2, (j % 2) * P:(j % 2 + 1) * P]) for j in range(4)])
                if i:
                    cross_weigh(i - 1)
            cross_weigh(PT - 1)
            pe.wait_ge(qp_ready, 1)
            for b in range(DB):
                pe.wait_ge(ck_in[b % CKS], 16 * (b // CKS + 1))
                for m in range(2):
                    turn(("ckT", b, m), lambda x: [(x[:, h * P:(h + 1) * P], ck[b % CKS][:, m, h * XD:(h + 1) * XD])
                                                   for h in range(XH)])
                if b % 2:
                    R.pe_free(pe, "ss", b // 2)
                    rows = slice(b // 2 * 32, b // 2 * 32 + 32)
                    for bb in (b - 1, b):
                        R.read(pe, "ckT", bb, 0), R.read(pe, "ckT", bb, 1)
                        for h in range(XH):
                            n = bb * XH + h
                            last = nc.tensor.matmul(bank(R.bank("ss", b // 2))[rows, 0:NMEM], qp[:, n * 32:(n + 1) * 32],
                                                    ckT[bb % 2][:, h, :], start=n % 8 == 0, stop=n % 8 == 7)
                    last.then_inc(R.full, 1)
            def output_product(i):
                for half in range(2):
                    r = rows_of(i)
                    R.pe_free(pe, "h2", i, half)
                    for k in range(XH):
                        last = nc.tensor.matmul(bank(R.bank("h2", i, half))[0:r, :], o2T[:, k, i * P:i * P + r],
                                                ring_xo[:, k, half * 512:(half + 1) * 512], start=k == 0, stop=k == XH - 1)
                    last.then_inc(R.full, 1)

            R.read(pe, "xo", PT - 1)
            ring_slot(pe, "xo")
            for i in range(PT):
                output_product(i)
            pe.wait_ge(sx_norm, 1)
            turn(("spT",), lambda b: [(b[:, m * P:(m + 1) * P], sp_[:, m * P:(m + 1) * P]) for m in range(2)])
            R.read(pe, "spT")
            pe.wait_ge(cv_in, 16)
            R.pe_free(pe, "so")
            for n in range(DB * XH):
                for m in range(2):
                    last = nc.tensor.matmul(bank(R.bank("so"))[:, n * DS:(n + 1) * DS], cv[:, n // XH, m, n % XH * XD:(n % XH + 1) * XD],
                                            spT[:, m, n * DS:(n + 1) * DS], start=m == 0, stop=m == 1)
            last.then_inc(R.full, 1)
            R.read(pe, "so")
            output_product(PT)
            n_ffn.pe_turn(pe)
            R.read(pe, "nffn", TILES - 1, 1)
            pe.wait_ge(wr_in, 16)
            for n in range(COLS):
                R.pe_free(pe, "lgT", n)
                for k in range(KD):
                    last = nc.tensor.matmul(bank(R.bank("lgT", n))[0:NG + NE, 0:NC_], wr[:, k, :], xnT[:, k, cols_of(n)],
                                            start=k == 0, stop=k == KD - 1)
                last.then_inc(R.full, 1)
            R.read(pe, "lgT", COLS - 1)
            turn(("lg",), lambda b: [(b[0:rows_of(i), i * 36:(i + 1) * 36], lgT[:, i * P:i * P + rows_of(i)])
                                     for i in range(TILES)])
            pe.wait_ge(hot_ready, 1)
            R.pe_free(pe, "rank")
            b = bank(R.bank("rank"))
            for i in range(TILES + 1):
                for j in range(min(i, TILES - 1) + 1):
                    last = nc.tensor.matmul(b[:, i * NE:(i + 1) * NE], beforeb if j == i else onesb, hot[:, j, :],
                                            start=j == 0, stop=j == min(i, TILES - 1))
            last.then_inc(R.full, 1)
            pe.wait_ge(routed, 1)
            n = pe.value_load(nblk[0:1, 0:1], min_val=2, max_val=MAXB)

            def turn_rows():
                for c in range(KD):
                    last = nc.tensor.transpose(ps[1][:, c * P:(c + 1) * P], xg[:, c * P:(c + 1) * P], ident)
                last.then_inc(xt_full, 1)

            def gate_product():
                for k in range(KD):
                    last = nc.tensor.matmul(bank(0), xgT[:, k, :], wg[:, k, :], start=k == 0, stop=k == KD - 1)
                last.then_inc(g_full, 1)

            def up_product():
                for k in range(KD):
                    last = nc.tensor.matmul(bank(1), xgT[:, k, :], wu[:, k, :], start=k == 0, stop=k == KD - 1)
                last.then_inc(u_full, 1)

            def turn_hidden():
                for c in range(DE // P):
                    last = nc.tensor.transpose(bank(4)[:, c * P:(c + 1) * P], hh[:, c * P:(c + 1) * P], ident)
                last.then_inc(ht_full, 1)

            def down_product():
                for half in range(2):
                    for k in range(DE // P):
                        last = nc.tensor.matmul(bank(6 + half), hT[:, k, :], wd[:, k, half * 512:(half + 1) * 512],
                                                start=k == 0, stop=k == DE // P - 1)
                    last.then_inc(d_full, 1)

            pe.sem_inc(d_full, 2)
            pe.wait_ge(xg_in, 16)
            turn_rows()
            pe.wait_ge(xt_read, 1)
            pe.wait_ge(wg_in, 16)
            gate_product()
            pe.wait_ge(wu_in, 16)
            up_product()
            pe.wait_ge(xg_in, 32)
            turn_rows()
            with pe.Fori(1, n) as b:
                pe.wait_ge(xt_read, b + 1)
                pe.wait_ge(wg_in, b * 16 + 16)
                pe.wait_ge(h_ready, b)
                gate_product()
                turn_hidden()
                pe.wait_ge(wu_in, b * 16 + 16)
                up_product()
                pe.wait_ge(xg_in, b * 16 + 32)
                turn_rows()
                pe.wait_ge(ht_read, b)
                pe.wait_ge(wd_in, b * 16)
                pe.wait_ge(d_read, b)
                down_product()
            pe.wait_ge(h_ready, n)
            apart(pe)
            turn_hidden()
            pe.wait_ge(ht_read, n)
            pe.wait_ge(wd_in, n * 16)
            pe.wait_ge(d_read, n)
            down_product()

        @block.scalar
        def _(act):
            def copy(tag, dst, src, scale=1.0, last=True):
                R.made(act, *tag)
                ins = nc.scalar.activation(dst, src(bank(R.bank(*tag))), ACT.Copy, scale=scale)
                if last:
                    ins.then_inc(R.by["act"], 1)

            act.wait_ge(made_up, 1)
            n_mix.act_stats(act, lambda i: resid[:, i, :], lambda i: act.wait_ge(x_in[i], 16))
            n_mix.act_copy(act, xnT)
            for f, n in FN:
                if n < COLS - 1:
                    copy(("cc", f, n), uT[:, f, HALO + n * NC_:HALO + (n + 1) * NC_], lambda b: b[:, 0:NC_])
                else:
                    copy(("cc", f, n), uT[:, f, HALO + n * NC_:HALO + SEQ], lambda b: b[:, 0:NC_ - NS], last=False)
                    copy(("cc", f, n), samples(uT[:, f, :])[:, :, HALO:], lambda b: b[:, NC_ - NS:NC_].rearrange(
                        "p (b s) -> p b s", b=DB))
            act.wait_ge(gain_used, 1)
            act.drain()
            n_mem.act_stats(act, lambda i: mem[:, i, :], lambda i: act.wait_ge(mem_in, 16))
            n_mem.act_copy(act, memT)
            act.wait_ge(rev_stored, 16 * 2 * DB)
            for f, n in FN:
                copy(("q", f, n), qT[:, f, cols_of(n)], lambda b: b[:, 0:NC_], scale=HD ** -0.5)
            for f, n in FN:
                copy(("k", f, n), kT[:, f, cols_of(n)], lambda b: b[:, 0:NC_])
            act.drain()
            nc.scalar.activation(qs, qT[:, :, SEQ:NT], ACT.Copy)
            nc.scalar.activation(ks, kT[:, :, SEQ:NT], ACT.Copy)
            act.wait_ge(abs_ready, 1)
            nc.scalar.activation(lf[:, 1, :], lf[:, 1, :], ACT.Exp, scale=-1.0)
            act.drain()
            nc.scalar.activation(lf[:, 1, :], lf[:, 1, :], ACT.Ln, bias=1.0).then_inc(ln_ready, 1)
            for i in range(TILES):
                copy(("v", i), vtok[0:rows_of(i), i, :], lambda b: b[0:rows_of(i), :])
            for i in range(TILES):
                if i >= 2:
                    act.wait_ge(stage_stored[i % 2], 16 * (i // 2))
                copy(("kout", i), stage[i % 2][0:rows_of(i), :], lambda b: b[0:rows_of(i), :])
            for i in range(2):
                act.wait_ge(stage_stored[i], 16 * (5 if i == 0 else 4))
                copy(("mk", i), stage[i], lambda b: b)
            for i in range(2):
                copy(("mkT", i), memKT[:, :, i * P:(i + 1) * P], lambda b: b.rearrange("p (h m) -> p h m", h=XH))
            for i in range(2):
                copy(("mv", i), memV[:, i, :], lambda b: b)

            act.wait_ge(qz_cleared, 2)

            def exp(hp, u):
                act.wait_ge(fs_max, hp * 16 + u + 1)
                n = (u % PT + 1) * P
                nc.scalar.activation(prob[u % 2][:, 0:n], prob[u % 2][:, 0:n], ACT.Exp, bias=fstat[:, 1, u % 4:u % 4 + 1],
                                     accum_out=fstat[:, 2, u % 4:u % 4 + 1]).then_inc(fs_exp, 1)

            def copy_pair(hp):
                act.wait_ge(fp_full, hp + 2)
                nc.scalar.activation(oT.rearrange("p c n -> p (c n)")[:, ds(hp * NT, SEQ)], ps[2][:, :], ACT.Copy
                                     ).then_inc(fp_read, 1)

            def pair_step(hp, before):
                for p in range(2):
                    nc.scalar.activation(qz[p][p * HD:(p + 1) * HD, :],
                                         qT.rearrange("p c n -> p (c n)")[p * HD:(p + 1) * HD, ds(hp * NT, SEQ)],
                                         ACT.Copy).then_inc(qz_ready, 1)
                if before is not None:
                    copy_pair(before)
                exp(hp, 0)
                for u, p, i in units():
                    for g, j0, nj in groups(u):
                        if g % 2 == 0:
                            act.wait_ge(ft_full, hp * 24 + g + 1)
                            if u >= 2:
                                act.wait_ge(fo_full, hp * 16 + u - 1)
                            nc.scalar.activation(probT[u % 2][:, j0:j0 + nj, :], bank(4)[:, 0:nj * P].rearrange(
                                "p (j x) -> p j x", j=nj), ACT.Copy).then_inc(ft_act, 1)
                    if u + 1 < 2 * PT:
                        exp(hp, u + 1)

            pair_step(0, None)
            with act.Fori(0, H // 2 - 1) as hp:
                pair_step(hp + 1, hp)
            copy_pair(H // 2 - 1)
            def round_keys(b, g):
                if g >= 2:
                    act.wait_ge(sc_full, b * 9 + g - 1)
                for c in range(KC):
                    act.wait_ge(kt_full, b * 32 + g * 4 + c + 9)
                    nc.scalar.activation(kpT_hi[g % 2][:, c, :], bank(c), ACT.Copy).then_inc(kt_hi, 1)

            def copy_low(b, g):
                act.wait_ge(sc_full, b * 9 + g + 1)
                nc.scalar.activation(sprob[:, g * 512:(g + 1) * 512], bank(4 + g % 2)[QH:2 * QH, :], ACT.Copy
                                     ).then_inc(sc_low, 1)

            def round_values(b, g):
                act.wait_ge(v_in[g % 4], b * 128 + 64 * (g // 4 + 1))
                for half in range(2):
                    act.wait_ge(v_used, b * 16 + 2 * g + half + 7)
                    nc.scalar.activation(v_hi[half], vpage[g % 4][:, 2 * half:2 * half + 2, :], ACT.Copy).then_inc(v_rounded, 1)

            def exp_pages(b):
                act.wait_ge(s_max, b + 2)
                for r in range(5):
                    x = sprob[:, r * 1024:(r + 1) * 1024] if r < 4 else sprob[:, PAST:PAST + NS]
                    nc.scalar.activation(x, x, ACT.Exp, bias=sstat[:, 10:11], accum_out=sstat[:, 12 + r:13 + r]
                                         ).then_inc(s_exp, 1)
                    if r:
                        round_probs(b, r - 1)

            def round_probs(b, r):
                act.wait_ge(t2_full, b * 5 + r + 1)
                if r < 4:
                    nc.scalar.activation(sprobT[:, r * 8:(r + 1) * 8, 0:QH], bank(4 + r % 2)[:, 0:8 * QH].rearrange(
                        "p (j x) -> p j x", j=8), ACT.Copy).then_inc(t2_hi, 1)
                else:
                    nc.scalar.activation(snewT[:, 0:QH], bank(6)[0:NS, 64:64 + QH], ACT.Copy).then_inc(t2_hi, 1)

            def sample_step(b, wb, more):
                for g in range(8):
                    if wb is not None:
                        round_values(wb, g)
                    copy_low(b, g)
                    if g < 6 or more:
                        round_keys(b, g + 2)
                exp_pages(b)
                round_probs(b, 4)

            round_keys(0, 0), round_keys(0, 1)
            sample_step(0, None, True)
            with act.Fori(0, DB - 2) as b:
                sample_step(b + 1, b, True)
            sample_step(DB - 1, DB - 2, False)
            for g in range(8):
                round_values(DB - 1, g)

            for x, (f, n) in enumerate(FN8):
                for m, name in enumerate(("ga", "gb")):
                    if x >= 2:
                        act.wait_ge(mixed, x - 1)
                    R.made(act, name, f, n)
                    nc.scalar.activation(gate[m][x % 2], bank(R.bank(name, f, n))[:, 0:NC_], ACT.Sigmoid
                                         ).then_inc(R.by["act"], 1)
            act.wait_ge(gain_used, 2)
            n_xat.act_stats(act, lambda i: resid[:, i, :], lambda i: R.read(act, "mo", i, 1))
            n_xat.act_copy(act, xnT)
            for f, n in FN:
                copy(("xq", f, n), q2T[:, f, cols_of(n)], lambda b: b[:, 0:NC_])
            XSCALE = XD ** -0.5

            def cross_exp(i):
                act.wait_ge(x_max, i + 1)
                for half in range(2):
                    for h in (2 * half, 2 * half + 1):
                        last = nc.scalar.activation(xp[i % 2][:, h, :], bank(R.bank("xs", i, half))[
                            :, (h % 2) * NMEM:(h % 2 + 1) * NMEM], ACT.Exp, bias=xstat[:, i % 2, 4 + h:5 + h],
                            scale=XSCALE, accum_out=xstat[:, i % 2, 8 + h:9 + h])
                    last.then_inc(R.by["act"], 1)
                act.drain()
                act.sem_inc(x_exp, 1)

            cross_exp(0)
            for i in range(PT):
                if i + 1 < PT:
                    if i + 1 >= 2:
                        R.made(act, "xt", i - 1, 1)
                    cross_exp(i + 1)
                R.made(act, "xt", i, 0)
                if i >= 2:
                    R.made(act, "xo", i - 2)
                copy(("xt", i, 0), xpT[i % 2][:, 0:4, :], lambda b: b.rearrange("p (j x) -> p j x", j=4))
            for b in range(DB):
                if b >= 2:
                    R.made(act, "ss", b // 2 - 1)
                copy(("ckT", b, 0), ckT[b % 2][:, :, 0:P], lambda x: x.rearrange("p (h m) -> p h m", h=XH))
            act.wait_ge(sx_max, 1)
            nc.scalar.activation(sp_, sp_, ACT.Exp, bias=sxstat[:, 1:2], scale=XSCALE, accum_out=sxstat[:, 2:3]
                                 ).then_inc(sx_exp, 1)
            copy(("spT",), spT, lambda b: b[:, 0:2 * P].rearrange("p (m x) -> p m x", m=2))
            R.made(act, "so")
            for b in range(DB):
                last = nc.scalar.activation(o2T[:, :, SEQ + b * DS:SEQ + (b + 1) * DS], bank(R.bank("so"))[
                    :, b * XH * DS:(b + 1) * XH * DS].rearrange("p (h s) -> p h s", h=XH), ACT.Copy)
            last.then_inc(R.by["act"], 1)
            n_ffn.act_stats(act, lambda i: resid[:, i, :], lambda i: R.read(act, "h2", i, 1))
            n_ffn.act_copy(act, xnT)
            for n in range(COLS):
                copy(("lgT", n), lgT[:, cols_of(n)], lambda b: b[0:NG + NE, 0:NC_])
            act.wait_ge(g_sub, 1)
            nc.scalar.activation(t4[1], t4[1], ACT.Exp).then_inc(g_exp, 1)
            act.wait_ge(e_sub, 1)
            nc.scalar.activation(t1[:, 5, :], t1[:, 5, :], ACT.Exp).then_inc(e_exp, 1)
            act.wait_ge(routed, 1)
            n = act.value_load(nblk[0:1, 0:1], min_val=2, max_val=MAXB)

            def copy_rows():
                nc.scalar.activation(xgT, ps[1][:, :].rearrange("p (c x) -> p c x", c=KD), ACT.Copy).then_inc(xt_read, 1)

            def sigmoid():
                nc.scalar.activation(sg, bank(0), ACT.Sigmoid).then_inc(sg_ready, 1)

            def copy_hidden():
                nc.scalar.activation(hT, bank(4).rearrange("p (c x) -> p c x", c=DE // P), ACT.Copy).then_inc(ht_read, 1)

            def copy_results():
                nc.scalar.activation(yb, ps[3][:, :], ACT.Copy).then_inc(d_read, 1)

            act.sem_inc(d_read, 1)
            act.wait_ge(xt_full, 1)
            copy_rows()
            act.wait_ge(g_full, 1)
            sigmoid()
            act.wait_ge(xt_full, 2)
            copy_rows()
            with act.Fori(1, n) as b:
                act.wait_ge(g_full, b + 1)
                sigmoid()
                act.wait_ge(ht_full, b)
                copy_hidden()
                act.wait_ge(xt_full, b + 2)
                copy_rows()
                act.wait_ge(y_free, b)
                act.wait_ge(d_full, b * 2 + 2)
                copy_results()
            act.wait_ge(ht_full, n)
            copy_hidden()
            act.wait_ge(y_free, n)
            act.wait_ge(d_full, n * 2 + 2)
            copy_results()
            n_fin.act_stats(act, lambda i: resid[:, i, :], lambda i: act.wait_ge(summed, i + 1))

        @block.vector
        def _(dve):
            nc.vector.memset(ss, 1.0)
            nc.vector.memset(ones, 1.0)
            dve.drain()
            dve.sem_inc(made_up, 1)
            n_mix.dve_scale(dve, lambda i: resid[:, i, :], 1)
            dve.wait_ge(consts_in, 48)
            nc.vector.tensor_copy(identb, ident)
            nc.vector.tensor_copy(causalb, consts[:, C_CAUSAL:C_CAUSAL + P])
            dve.wait_ge(past_in, 32)
            for g in range(2):
                nc.vector.tensor_reduce(ptot[:, g, :], past[:, g, :].rearrange("p (s h) -> p h s", h=H), AX, ALU.add)
            dve.drain()
            dve.sem_inc(totals_ready, 1)
            nc.vector.memset(after[:, :, :, PAGE - 1:PAGE], 0.0)
            for g in range(2):
                for h in range(H):
                    gates = past[:, g, :].rearrange("p (s h) -> p h s", h=H)[:, h, :]
                    nc.vector.tensor_tensor_scan(after[:, g, h, 0:PAGE - 1][:, ::-1],
                                                 ones[:, 0:1].to_broadcast([P, PAGE - 1]), gates[:, 1:PAGE][:, ::-1],
                                                 0.0, ALU.mult, ALU.add)
            dve.drain()
            for g in range(2):
                R.made(dve, "later", g)
                nc.vector.tensor_tensor(after[:, g], after[:, g], bank(R.bank("later", g))[:, 0:H].unsqueeze(2)
                                        .to_broadcast([P, H, PAGE]), ALU.add)
            dve.drain()
            dve.sem_inc(R.by["dve"], 2)
            nc.vector.tensor_copy(after_hi.bitcast(F32R), after)
            dve.drain()
            nc.vector.tensor_tensor(after.bitcast(F32R), after, after_hi, ALU.subtract).then_inc(after_ready, 1)
            R.made(dve, "halo")
            nc.vector.memset(uT[:, :, 0:HALO], 0.0)
            for c in range(KC):
                last = nc.vector.tensor_copy(samples(uT[:, c, :])[:, :, 0:HALO], bank(R.bank("halo"))[
                    :, c * 2 * DB:(c + 1) * 2 * DB].rearrange("p (b s) -> p b s", b=DB))
            last.then_inc(R.by["dve"], 1)
            for f, n in FN:
                R.made(dve, "cx", f, n)
                R.read(dve, "cc", f, n)
                b = bank(R.bank("cx", f, n))
                if n < COLS - 1:
                    u = uT[:, f, HALO + n * NC_:HALO + (n + 1) * NC_]
                    nc.vector.tensor_tensor(u, b[:, 0:NC_], u, ALU.mult).then_inc(R.by["dve"], 1)
                else:
                    u = uT[:, f, HALO + n * NC_:HALO + SEQ]
                    nc.vector.tensor_tensor(u, b[:, 0:NC_ - NS], u, ALU.mult)
                    u = samples(uT[:, f, :])[:, :, HALO:]
                    nc.vector.tensor_tensor(u, b[:, NC_ - NS:NC_].rearrange("p (b s) -> p b s", b=DB), u,
                                            ALU.mult).then_inc(R.by["dve"], 1)
            dve.drain()
            nc.vector.tensor_copy(tailT[:, :, 0:2], uT[:, :, HALO + SEQ - 2:HALO + SEQ])
            for c in range(KC):
                last = nc.vector.tensor_copy(tailT[:, c, 2:].rearrange("p (b s) -> p b s", b=DB),
                                             samples(uT[:, c, :])[:, :, DS:])
            last.then_inc(tail_got, 1)
            n_mem.dve_scale(dve, lambda i: mem[:, i, :], 2)
            for j in range(3):
                for c in range(KC):
                    tap = convp[:, j * KC + c:j * KC + c + 1]
                    for u, y in ((uT[:, c, j:j + SEQ], cyT[:, c, 0:SEQ]),
                                 (samples(uT[:, c, :])[:, :, j:j + DS],
                                  cyT[:, c, SEQ:NT].rearrange("p (b s) -> p b s", b=DB))):
                        if j == 0:
                            nc.vector.tensor_scalar(y, u, tap, convp[:, 3 * KC + c:3 * KC + c + 1], ALU.mult, ALU.add)
                        else:
                            nc.vector.scalar_tensor_tensor(y, u, tap, y, ALU.mult, ALU.add)
                dve.drain()
            for f, n in FN:
                R.made(dve, "cb", f, n)
                y = cyT[:, f, cols_of(n)]
                nc.vector.tensor_tensor(y, bank(R.bank("cb", f, n))[:, 0:NC_], y, ALU.mult).then_inc(R.by["dve"], 1)
            R.made(dve, "tail")
            nc.vector.tensor_copy(tail, bank(R.bank("tail"))[0:2 + 2 * DB, :]).then_inc(R.by["dve"], 1)
            for n in range(COLS):
                R.made(dve, "fz", n)
                nc.vector.tensor_scalar(lf[:, 0, cols_of(n)], bank(R.bank("fz", n))[0:H, 0:NC_], convp[0:H, 4 * KC:4 * KC + 1],
                                        None, ALU.add).then_inc(R.by["dve"], 1)
            dve.drain()
            nc.vector.scalar_tensor_tensor(lf[:, 1, :], lf[:, 0, :], -1.0, lf[:, 0, :], ALU.mult, ALU.max
                                           ).then_inc(abs_ready, 1)
            dve.wait_ge(ln_ready, 1)
            nc.vector.scalar_tensor_tensor(lf[:, 2, :], lf[:, 0, :], 0.0, lf[:, 1, :], ALU.min, ALU.subtract
                                           ).then_inc(lf_ready, 1)
            dve.drain()
            nc.vector.tensor_tensor_scan(lf[:, 1, 0:SEQ], ones[0:H, 0:1].to_broadcast([H, SEQ]), lf[:, 2, 0:SEQ], 0.0,
                                         ALU.mult, ALU.add)
            nc.vector.tensor_copy(lf[:, 1, SEQ:NT], lf[:, 2, SEQ:NT])
            dve.drain()
            new_sum = lf[:, 1, SEQ:NT].rearrange("p (b s) -> p b s", b=DB)
            for s in range(1, DS):
                nc.vector.tensor_tensor(new_sum[:, :, s:s + 1], new_sum[:, :, s:s + 1], new_sum[:, :, s - 1:s], ALU.add)
                dve.drain()
            nc.vector.tensor_scalar(lf[:, 3, :], lf[:, 1, :], -1.0, None, ALU.mult).then_inc(neg_ready, 1)
            R.made(dve, "lf")
            b = bank(R.bank("lf"))
            nc.vector.tensor_copy(lfo[:, 0:PT, :], b[:, 0:PT * H].rearrange("p (i h) -> p i h", i=PT))
            nc.vector.tensor_copy(lfo[0:NS, PT, :], b[0:NS, PT * H:TILES * H]).then_inc(R.by["dve"], 1)

            R.read(dve, "mv", 1)
            for p in range(2):
                nc.vector.memset(qz[p][(1 - p) * HD:(2 - p) * HD, :], 0.0).then_inc(qz_cleared, 1)
            with dve.Fori(0, H // 2) as hp:
                def biased(u, p, i):
                    n = (i + 1) * P
                    if i == 0:
                        dve.wait_ge(negk_in[p], hp * 16 + 16)
                    dve.wait_ge(fs_full, hp * 16 + u + 1)
                    if u >= 2:
                        dve.wait_ge(ft_full, hp * 24 + groups(u - 2)[-1][0] + 1)
                    apart(dve)
                    nc.vector.tensor_tensor_reduce(out=prob[u % 2][:, 0:n], in0=ps[u % 2][:, 0:n], in1=negk[p][:, 0:n],
                                                   scale=1.0, scalar=-3e38, op0=ALU.add, op1=ALU.max,
                                                   accum_out=fstat[:, 0, u % 4:u % 4 + 1])
                    dve.drain()
                    nc.vector.tensor_scalar(fstat[:, 1, u % 4:u % 4 + 1], fstat[:, 0, u % 4:u % 4 + 1], -1.0, None, ALU.mult
                                            ).then_inc(fs_max, 1)

                def divide(u, p, i):
                    dve.wait_ge(fo_full, hp * 16 + u + 1)
                    if u == 0:
                        dve.wait_ge(fp_full, hp + 1)
                    nc.vector.reciprocal(fstat[:, 3, u % 4:u % 4 + 1], fstat[:, 2, u % 4:u % 4 + 1])
                    dve.drain()
                    nc.vector.tensor_scalar(pair[:, i, p * HD:(p + 1) * HD], bank(6 + u % 2)[:, p * HD:(p + 1) * HD],
                                            fstat[:, 3, u % 4:u % 4 + 1], None, ALU.mult).then_inc(fo_read, 1)

                biased(*units()[0])
                for u, p, i in units():
                    if u + 1 < 2 * PT:
                        biased(*units()[u + 1])
                    for g, j0, nj in groups(u):
                        if g % 2:
                            dve.wait_ge(ft_full, hp * 24 + g + 1)
                            if u >= 2:
                                dve.wait_ge(fo_full, hp * 16 + u - 1)
                            nc.vector.tensor_copy(probT[u % 2][:, j0:j0 + nj, :], bank(5)[:, 0:nj * P].rearrange(
                                "p (j x) -> p j x", j=nj)).then_inc(ft_dve, 1)
                    if u:
                        divide(*units()[u - 1])
                divide(*units()[2 * PT - 1])
            dve.wait_ge(fp_full, 1 + H // 2)
            nc.vector.tensor_scalar(qb, consts[:, 0:KC * (2 * QH + 2)], 0.0, None, ALU.mult)
            dve.wait_ge(revsel_in, 16)
            nc.vector.tensor_copy(revsel, gain[:, 0:8 * QH])
            dve.wait_ge(nd_in, 16 * DS)
            nc.vector.tensor_tensor(nbias, consts[0:QH, C_MASK:C_MASK + DB * NS].rearrange("p (b s) -> p b s", b=DB),
                                    nd.unsqueeze(1).to_broadcast([QH, DB, NS]), ALU.add)
            dve.drain()
            dve.sem_inc(s_max, 1), dve.sem_inc(sx_read, 1)

            def place_queries(b):
                for half in range(2):
                    r = slice(half * HD, (half + 1) * HD)
                    hi, lo = (qb[r, :].rearrange("p (c x) -> p c x", c=KC)[:, :, part * QH + half:part * QH + half + 25:H]
                              for part in range(2))
                    nc.vector.tensor_copy(hi, qs[r, :, ds(b * DS, DS)])
                    dve.drain()
                    nc.vector.tensor_tensor(lo, qs[r, :, ds(b * DS, DS)], hi, ALU.subtract)
                dve.wait_ge(rev_in, b * 16 + 16)
                apart(dve)
                nc.vector.tensor_copy(rev, rev_f)
                dve.drain()
                dve.sem_inc(qb_ready, 1), dve.sem_inc(rev_used, 1)

            def split_keys(b, g):
                for c in range(KC):
                    dve.wait_ge(kt_hi, b * 32 + g * 4 + c + 1)
                    nc.vector.tensor_tensor(kpT_lo[g % 2][:, c, :], bank(c), kpT_hi[g % 2][:, c, :], ALU.subtract
                                            ).then_inc(kt_lo, 1)

            def split_values(b, g):
                for half in range(2):
                    two = slice(2 * half, 2 * half + 2)
                    dve.wait_ge(v_rounded, b * 16 + 2 * g + half + 1)
                    nc.vector.tensor_tensor(v_lo[g % 4][:, two, :], vpage[g % 4][:, two, :], v_hi[half], ALU.subtract
                                            ).then_inc(v_split, 1)

            def join_scores(b, g):
                if g < 8:
                    dve.wait_ge(sc_low, b * 8 + g + 1)
                    apart(dve)
                    out, hi, lo = sprob[:, g * 512:(g + 1) * 512], bank(4 + g % 2)[0:QH, :], sprob[:, g * 512:(g + 1) * 512]
                else:
                    dve.wait_ge(sc_full, b * 9 + g + 1)
                    apart(dve)
                    out, hi, lo = sprob[:, PAST:PAST + NS], bank(6)[0:QH, 0:NS], nb[:, 1, :]
                    nc.vector.tensor_tensor(lo, bank(6)[QH:2 * QH, 0:NS], nb[:, 0, :], ALU.add)
                    dve.drain()
                nc.vector.tensor_tensor_reduce(out=out, in0=hi, in1=lo, scale=1.0, scalar=-3e38, op0=ALU.add,
                                               op1=ALU.max, accum_out=sstat[:, g:g + 1]).then_inc(sc_read, 1)

            def divide_own(b):
                dve.wait_ge(so_full, b + 1)
                nc.vector.scalar_tensor_tensor(own, bank(7)[0:2 * QH, :], srecip, consts[0:2 * QH, C_DIAG:C_DIAG + DA],
                                               ALU.mult, ALU.mult).then_inc(so_read, 1)

            def split_probs(b):
                for r in range(5):
                    dve.wait_ge(t2_hi, b * 5 + r + 1)
                    if r < 4:
                        nc.vector.tensor_tensor(sprobT[:, r * 8:(r + 1) * 8, QH:2 * QH], bank(4 + r % 2)[:, 0:8 * QH].rearrange(
                            "p (j x) -> p j x", j=8), sprobT[:, r * 8:(r + 1) * 8, 0:QH], ALU.subtract).then_inc(t2_lo, 1)
                    else:
                        nc.vector.tensor_tensor(snewT[:, QH:2 * QH], bank(6)[0:NS, 64:64 + QH], snewT[:, 0:QH], ALU.subtract
                                                ).then_inc(t2_lo, 1)
                nc.vector.tensor_reduce(sstat[:, 17:18], sstat[:, 12:17], AX, ALU.add)
                dve.drain()
                nc.vector.reciprocal(srecip[0:QH, :], sstat[:, 17:18])
                nc.vector.reciprocal(srecip[QH:2 * QH, :], sstat[:, 17:18])
                dve.drain()

            def take_output(b):
                dve.wait_ge(sx_full, b + 1)
                nc.vector.tensor_copy(oT[:, :, ds(b * DS + SEQ, DS)], bank(6)[:, 128:128 + KC * DS].rearrange(
                    "p (c s) -> p c s", c=KC)).then_inc(sx_read, 1)

            def sample_step(b, wb, more):
                for g in range(8):
                    if wb is not None:
                        split_values(wb, g)
                    join_scores(b, g)
                    if g < 6 or more:
                        split_keys(b, g + 2)
                nc.vector.tensor_copy(nb[:, 0, :], nbias.rearrange("p b s -> p (b s)")[:, ds(b * NS, NS)])
                dve.drain()
                join_scores(b, 8)
                dve.drain()
                nc.vector.tensor_reduce(sstat[:, 9:10], sstat[:, 0:9], AX, ALU.max)
                dve.drain()
                nc.vector.tensor_scalar(sstat[:, 10:11], sstat[:, 9:10], -1.0, None, ALU.mult).then_inc(s_max, 1)
                if wb is not None:
                    divide_own(wb)
                if more:
                    place_queries(b + 1)
                if wb is not None:
                    take_output(wb)
                else:
                    dve.sem_inc(sx_read, 1)
                split_probs(b)

            dve.sem_inc(rev_used, 1)
            split_keys(0, 0), split_keys(0, 1)
            place_queries(0)
            sample_step(0, None, True)
            with dve.Fori(0, DB - 2) as b:
                sample_step(b + 1, b, True)
            sample_step(DB - 1, DB - 2, False)
            for g in range(8):
                split_values(DB - 1, g)
            divide_own(DB - 1)
            take_output(DB - 1)

            for x, (f, n) in enumerate(FN8):
                for m, (name, y) in enumerate((("ga", "yc"), ("gb", "ya"))):
                    R.read(dve, name, f, n)
                    R.made(dve, y, f, n)
                    nc.vector.tensor_tensor(gate[m][x % 2], bank(R.bank(y, f, n))[:, 0:NC_], gate[m][x % 2], ALU.mult
                                            ).then_inc(R.by["dve"], 1)
                dve.drain()
                nc.vector.tensor_tensor(mixT[:, f, cols_of(n)], gate[0][x % 2], gate[1][x % 2], ALU.add).then_inc(mixed, 1)
            for i in range(TILES):
                r = rows_of(i)
                dve.wait_ge(xr_in[i % 2], 16 * (i // 2 + 1))
                for half in range(2):
                    R.made(dve, "mo", i, half)
                    c = slice(half * 512, (half + 1) * 512)
                    nc.vector.tensor_tensor(resid[0:r, i, c], bank(R.bank("mo", i, half))[0:r, :], xr[i % 2][0:r, c],
                                            ALU.add).then_inc(R.by["dve"], 1)
            n_xat.dve_scale(dve, lambda i: resid[:, i, :], 3)
            nc.vector.memset(qp, 0.0)
            R.read(dve, "xq", KC - 1, COLS - 1)
            dve.drain()
            for b in range(DB):
                cols = qp[:, b * 128:(b + 1) * 128].rearrange("p (h x) -> p h x", h=XH)
                for h in range(XH):
                    at_ = (b % 2) * 16 + h * DS
                    last = nc.vector.tensor_copy(cols[:, h, at_:at_ + DS], q2T[:, h, SEQ + b * DS:SEQ + (b + 1) * DS])
            last.then_inc(qp_ready, 1)

            def cross_max(i):
                st = xstat[:, i % 2, :]
                for half in range(2):
                    R.made(dve, "xs", i, half)
                    nc.vector.tensor_reduce(st[:, 2 * half:2 * half + 2], bank(R.bank("xs", i, half)).rearrange(
                        "p (h m) -> p h m", h=2), AX, ALU.max)
                dve.drain()
                nc.vector.tensor_scalar(st[:, 4:8], st[:, 0:4], -(XD ** -0.5), None, ALU.mult).then_inc(x_max, 1)

            def cross_out(i):
                R.made(dve, "xo", i)
                nc.vector.tensor_copy(o2T[:, :, i * P:(i + 1) * P], bank(R.bank("xo", i)).rearrange("p (h x) -> p h x", h=XH)
                                      ).then_inc(R.by["dve"], 1)

            cross_max(0)
            for i in range(PT):
                dve.wait_ge(x_exp, i + 1)
                st = xstat[:, i % 2, :]
                nc.vector.reciprocal(st[:, 12:16], st[:, 8:12])
                dve.drain()
                nc.vector.tensor_tensor(xp[i % 2], xp[i % 2], st[:, 12:16].unsqueeze(2).to_broadcast([P, XH, NMEM]),
                                        ALU.mult).then_inc(x_norm, 1)
                if i + 1 < PT:
                    cross_max(i + 1)
                R.made(dve, "xt", i, 1)
                nc.vector.tensor_copy(xpT[i % 2][:, 4:8, :], bank(R.bank("xt", i, 1)).rearrange("p (j x) -> p j x", j=4)
                                      ).then_inc(R.by["dve"], 1)
                if i:
                    cross_out(i - 1)
            cross_out(PT - 1)
            for b in range(DB):
                R.made(dve, "ckT", b, 1)
                nc.vector.tensor_copy(ckT[b % 2][:, :, P:2 * P], bank(R.bank("ckT", b, 1)).rearrange("p (h m) -> p h m", h=XH)
                                      ).then_inc(R.by["dve"], 1)
                if b % 2:
                    R.made(dve, "ss", b // 2)
                    rows = slice(b // 2 * 32, b // 2 * 32 + 32)
                    nc.vector.tensor_copy(sp_[rows, :], bank(R.bank("ss", b // 2))[rows, 0:NMEM]).then_inc(R.by["dve"], 1)
            dve.drain()
            nc.vector.tensor_reduce(sxstat[:, 0:1], sp_, AX, ALU.max)
            dve.drain()
            nc.vector.tensor_scalar(sxstat[:, 1:2], sxstat[:, 0:1], -(XD ** -0.5), None, ALU.mult).then_inc(sx_max, 1)
            dve.wait_ge(sx_exp, 1)
            nc.vector.reciprocal(sxstat[:, 3:4], sxstat[:, 2:3])
            dve.drain()
            nc.vector.tensor_scalar(sp_, sp_, sxstat[:, 3:4], None, ALU.mult).then_inc(sx_norm, 1)
            for i in range(TILES):
                r = rows_of(i)
                for half in range(2):
                    R.made(dve, "h2", i, half)
                    c = slice(half * 512, (half + 1) * 512)
                    nc.vector.tensor_tensor(resid[0:r, i, c], bank(R.bank("h2", i, half))[0:r, :], resid[0:r, i, c],
                                            ALU.add).then_inc(R.by["dve"], 1)

            def ffn_free(i):
                R.made(dve, "nffn", i, 1)
                dve.wait_ge(x3_stored[i % 4], 16 * (i // 4 + 1))

            n_ffn.dve_scale(dve, lambda i: resid[:, i, :], 4, ffn_free)
            nc.vector.memset(lg, 0.0)
            nc.vector.tensor_copy(beforeb, consts[:, C_BEFORE:C_BEFORE + P])
            nc.vector.memset(onesb, 1.0)
            for k in range(2):
                for a in range(2):
                    nc.vector.tensor_scalar(pairs[:, k, :, a], consts[:, C_TOK:C_TOK + TILES], float(k * a * NT), None, ALU.add)
            nc.vector.memset(empty[:, :, 0:1], 0)
            nc.vector.memset(empty[:, :, 1:2], 2 * NT)
            dve.drain()
            dve.sem_inc(empty_ready, 1)
            R.made(dve, "lg")
            b = bank(R.bank("lg"))
            nc.vector.tensor_copy(lg[:, 0:PT, :], b[:, 0:PT * 36].rearrange("p (i e) -> p i e", i=PT))
            nc.vector.tensor_copy(lg[0:NS, PT, :], b[0:NS, PT * 36:TILES * 36]).then_inc(R.by["dve"], 1)
            dve.drain()
            for p in range(4):
                dve.wait_ge(x3_stored[p], 16 * (3 if p == 0 else 2))
            TT, TS_, RED = nc.vector.tensor_tensor, nc.vector.tensor_scalar, nc.vector.tensor_reduce
            gl, el = lg[:, :, 0:NG], lg[:, :, NG:]

            def over(col, width):
                return t1[:, col, :].unsqueeze(2).to_broadcast([P, TILES, width])

            def row(c0, width):
                return consts[:, c0:c0 + width].unsqueeze(1).to_broadcast([P, TILES, width])

            RED(t1[:, 0, :], gl, AX, ALU.max)
            dve.drain()
            TT(t4[1], gl, over(0, NG), ALU.subtract).then_inc(g_sub, 1)
            TT(t4[0], gl, over(0, NG), ALU.is_lt)
            dve.drain()
            nc.vector.scalar_tensor_tensor(t4[2], t4[0], 1000.0, row(C_EXP, NG), ALU.mult, ALU.add)
            dve.drain()
            RED(t1[:, 1, :], t4[2], AX, ALU.min)
            dve.drain()
            m, le, hot1, hot2, le2, tmp, tmp2 = t32
            TT(m, row(C_GRP, NE), over(1, NE), ALU.is_equal)
            dve.drain()
            TS_(tmp, m, -NEG, NEG, ALU.mult, ALU.add)
            TT(le, el, m, ALU.mult)
            dve.drain()
            TT(le, le, tmp, ALU.add)
            dve.drain()
            for k, (src, one) in enumerate(((le, hot1), (le2, hot2))):
                if k:
                    nc.vector.scalar_tensor_tensor(le2, hot1, 2 * NEG, le, ALU.mult, ALU.add)
                    dve.drain()
                RED(t1[:, 2 + k, :], src, AX, ALU.max)
                dve.drain()
                TT(tmp, src, over(2 + k, NE), ALU.is_lt)
                dve.drain()
                nc.vector.scalar_tensor_tensor(tmp2, tmp, 1000.0, row(C_EXP, NE), ALU.mult, ALU.add)
                dve.drain()
                RED(t1[:, 4, :], tmp2, AX, ALU.min)
                dve.drain()
                TT(one, row(C_EXP, NE), over(4, NE), ALU.is_equal)
                dve.drain()
            TT(tmp, hot1, hot2, ALU.add)
            TS_(t1[:, 6, :], consts[:, C_TOK:C_TOK + TILES], float(NT), None, ALU.is_lt)
            TT(t1[:, 5, :], t1[:, 3, :], t1[:, 2, :], ALU.subtract).then_inc(e_sub, 1)
            dve.drain()
            TT(hot, tmp, over(6, NE), ALU.mult)
            dve.drain()
            dve.sem_inc(hot_ready, 1)
            dve.wait_ge(g_exp, 1)
            RED(t1[:, 7, :], t4[1], AX, ALU.add)
            dve.wait_ge(e_exp, 1)
            TS_(t1[:, 8, :], t1[:, 5, :], 1.0, None, ALU.add)
            dve.drain()
            TT(t1[:, 9, :], t1[:, 7, :], t1[:, 8, :], ALU.mult)
            dve.drain()
            nc.vector.reciprocal(wgt[:, 0, :], t1[:, 9, :])
            dve.drain()
            TT(wgt[:, 1, :], wgt[:, 0, :], t1[:, 5, :], ALU.mult)
            R.made(dve, "rank")
            b = bank(R.bank("rank"))
            TS_(cnti, b[:, TILES * NE:(TILES + 1) * NE], float(BLK - 1), None, ALU.add)
            dve.drain()
            TS_(cnti, cnti, BLK.bit_length() - 1, None, ALU.logical_shift_right)
            dve.drain()
            nc.vector.tensor_copy(cnt[:, 0, :], cnti)
            dve.drain()
            nc.vector.tensor_tensor_scan(cnt[:, 1, :], ones[:, 0:1].to_broadcast([P, NE]), cnt[:, 0, :], 0.0, ALU.mult, ALU.add)
            dve.drain()
            TT(cnt[:, 2, :], cnt[:, 1, :], cnt[:, 0, :], ALU.subtract)
            dve.drain()
            TS_(cnt[:, 3, :], cnt[:, 2, :], float(BLK), None, ALU.mult)
            dve.drain()
            TT(tmp, b[:, 0:TILES * NE].rearrange("p (i e) -> p i e", i=TILES), cnt[:, 3, :].unsqueeze(1).to_broadcast(
                [P, TILES, NE]), ALU.add).then_inc(R.by["dve"], 1)
            dve.drain()
            TT(le, tmp, hot1, ALU.mult)
            TT(le2, tmp, hot2, ALU.mult)
            dve.drain()
            RED(t1[:, 10, :], le, AX, ALU.add)
            RED(t1[:, 11, :], le2, AX, ALU.add)
            dve.drain()
            nc.vector.tensor_copy(dest, t1[:, 10:12, :]).then_inc(dest_ready, 1)
            TT(bcmp, cnt[0:1, 1, :].unsqueeze(1).to_broadcast([1, MAXB, NE]),
               consts[0:1, C_BLK:C_BLK + MAXB].unsqueeze(2).to_broadcast([1, MAXB, NE]), ALU.is_le)
            dve.drain()
            RED(bsum, bcmp, AX, ALU.add)
            dve.drain()
            TS_(blke[0:1, 0:MAXB], bsum, float(NE - 1), None, ALU.min)
            nc.vector.tensor_copy(nblk, cnt[0:1, 1, NE - 1:NE])
            dve.drain()
            dve.sem_inc(routed, 1)
            n = dve.value_load(nblk[0:1, 0:1], min_val=2, max_val=MAXB)
            dve.wait_ge(sg_ready, 1)
            TT(sg, bank(0), sg, ALU.mult)
            dve.wait_ge(u_full, 1)
            dve.drain()
            TT(hh, bank(1), sg, ALU.mult).then_inc(h_ready, 1)
            with dve.Fori(1, n) as b:
                dve.wait_ge(sg_ready, b + 1)
                TT(sg, bank(0), sg, ALU.mult)
                dve.wait_ge(ht_full, b)
                dve.wait_ge(u_full, b + 1)
                apart(dve)
                dve.drain()
                TT(hh, bank(1), sg, ALU.mult).then_inc(h_ready, 1)
            for i in range(TILES):
                r = rows_of(i)
                dve.wait_ge(x_in[i], 16 + 32)
                for k in range(2):
                    last = nc.vector.scalar_tensor_tensor(resid[0:r, i, :], yy[i % PT][0:r, k, :], wgt[0:r, k, i:i + 1],
                                                          resid[0:r, i, :], ALU.mult, ALU.add)
                    if k == 0:
                        dve.drain()
                last.then_inc(summed, 1)
            n_fin.dve_scale(dve, lambda i: resid[:, i, :], 5, lambda i: dve.wait_ge(y_out[i % 4], 16 * (i // 4 + 1)))

        @block.gpsimd
        def _(pool):
            n_stored = 0

            def store(dst, src):
                nonlocal n_stored
                n_stored += 1
                pool.dma_start(dst, src).then_inc(stored, 16)

            pool.wait_ge(pgi_in, 16)
            for g in range(2):
                pool.indirect_dma_start(past[:, g, :], None, t["cache_logf"],
                                        bass.IndirectOffsetOnAxis(ap=pgi[:, g:g + 1].bitcast(U32), axis=0)).then_inc(past_in, 16)
            pool.wait_ge(after_ready, 1)
            for b in range(DB):
                for part, split in enumerate((after_hi, after)):
                    pool.dma_start(rev_d[b, part].rearrange("h (j s) -> j h s", j=PAGES),
                                   split[b % 4 * PAGES:(b % 4 + 1) * PAGES, b // 4]).then_inc(rev_stored, 16)
            R.read(pool, "tail")
            store(t["conv_prompt"], tail[0:2, :])
            store(t["conv_sample"], tail[2:2 + 2 * DB, :])
            R.read(pool, "v", TILES - 1)
            store(t["v_prompt"].rearrange("(i p) d -> p i d", p=P), vtok[:, 0:PT, :])
            store(t["v_sample"], vtok[0:NS, PT, :])
            for i in range(TILES):
                R.read(pool, "kout", i)
                dst = t["k_prompt"][i * P:(i + 1) * P, :] if i < PT else t["k_sample"]
                pool.dma_start(dst, stage[i % 2][0:rows_of(i), :]).then_inc(stage_stored[i % 2], 16)
            pool.wait_ge(neg_ready, 1)
            pool.dma_start(neg_d, lf[:, 3, :]).then_inc(neg_stored, 16)
            R.read(pool, "lf")
            store(t["lf_prompt"].rearrange("(i p) h -> p i h", p=P), lfo[:, 0:PT, :])
            store(t["lf_sample"], lfo[0:NS, PT, :])
            for i in range(2):
                R.read(pool, "mk", i)
                pool.dma_start(t["mk_prompt"][i * P:(i + 1) * P, :], stage[i]).then_inc(stage_stored[i], 16)
            R.read(pool, "mv", 1)
            store(t["mv_prompt"].rearrange("(i p) d -> p i d", p=P), memV)
            pool.wait_ge(consts_in, 48)
            with pool.Fori(0, DB) as b:
                for g in range(PAGES // 4):
                    pool.wait_ge(v_used, b * 16 + 2 * g + 2)
                    for p in range(4):
                        page = pool.value_load(pages[0:1, ds(b * PAGES + (g * 4 + p), 1)], min_val=0, max_val=N_POOL - 1)
                        pool.dma_start(vpage[g % 4][:, p, :], t["cache_v"][ds(page, 1)].rearrange("a s d -> (a s) d")
                                       ).then_inc(v_in[g % 4], 16)
            pool.wait_ge(sx_read, DB + 2)
            for i in range(TILES):
                pool.wait_ge(n_ffn.scaled, i + 1)
                pool.dma_start(x3_d[i * P:i * P + rows_of(i), :], xf[i % 4][0:rows_of(i), :]).then_inc(x3_stored[i % 4], 16)
            pool.wait_ge(empty_ready, 1)
            pool.dma_start(row_d.rearrange("(p n) a -> p (n a)", p=P), empty.rearrange("p n a -> p (n a)")
                           ).then_inc(empty_stored, 16)
            pool.wait_ge(dest_ready, 1)
            pool.wait_ge(empty_stored, 16)
            for i in range(TILES):
                for k in range(2):
                    r = rows_of(i)
                    pool.indirect_dma_start(row_d, bass.IndirectOffsetOnAxis(ap=dest[0:r, k, i:i + 1].bitcast(U32), axis=0),
                                            pairs[0:r, k, i, :], None).then_inc(rows_stored, 16)
            pool.wait_ge(rows_stored, 16 * 2 * TILES)
            pool.wait_ge(routed, 1)
            for p in range(4):
                pool.wait_ge(x3_stored[p], 16 * (3 if p == 0 else 2))
            n = pool.value_load(nblk[0:1, 0:1], min_val=2, max_val=MAXB)
            R.read(pool, "rank")

            def row_column(b, a):
                return row_d[ds(b * BLK, BLK), a:a + 1]

            with nc.allow_non_contiguous_dma("one number of a row for each partition"):
                def gather_rows():
                    pool.indirect_dma_start(xg, None, x3_d, bass.IndirectOffsetOnAxis(ap=rowi[:, 0:1].bitcast(U32), axis=0)
                                            ).then_inc(xg_in, 16)

                def scatter_results():
                    pool.indirect_dma_start(y_d, bass.IndirectOffsetOnAxis(ap=outi[:, 0:1].bitcast(U32), axis=0), yb, None
                                            ).then_inc(y_stored, 16)

                for b in range(3):
                    pool.dma_start(rowi, row_column(b, 0)).then_inc(rowi_in, 16)
                    pool.wait_ge(rowi_in, b * 16 + 16)
                    if b:
                        pool.wait_ge(xt_full, b)
                    gather_rows()
                    pool.wait_ge(xg_in, b * 16 + 16)
                pool.dma_start(rowi, row_column(3, 0)).then_inc(rowi_in, 16)
                pool.dma_start(outi, row_column(0, 1)).then_inc(outi_in, 16)
                pool.sem_inc(y_free, 1)
                with pool.Fori(1, n) as b:
                    pool.wait_ge(xt_full, b + 2)
                    pool.wait_ge(rowi_in, b * 16 + 48)
                    apart(pool)
                    gather_rows()
                    pool.wait_ge(outi_in, b * 16)
                    pool.wait_ge(d_read, b + 1)
                    apart(pool)
                    scatter_results()
                    pool.wait_ge(xg_in, b * 16 + 48)
                    pool.dma_start(rowi, row_column(b + 3, 0)).then_inc(rowi_in, 16)
                    pool.wait_ge(y_stored, b * 16)
                    pool.sem_inc(y_free, 1)
                    pool.dma_start(outi, row_column(b, 1)).then_inc(outi_in, 16)
                pool.wait_ge(outi_in, n * 16)
                pool.wait_ge(d_read, n + 1)
                apart(pool)
                scatter_results()
            pool.wait_ge(rowi_in, n * 16 + 48)
            pool.wait_ge(xg_in, n * 16 + 32)
            pool.wait_ge(y_stored, n * 16)
            apart(pool)
            pool.wait_ge(stored, 16 * n_stored)
            pool.wait_ge(neg_stored, 16)
            for i in range(2):
                pool.wait_ge(stage_stored[i], 16 * (6 - i))


_OUTS = [("y_prompt", (SEQ, D), (1, SEQ, D)), ("y_sample", (NS, D), (DB, DS, D)),
         ("conv_prompt", (2, DC), (1, 1, 2, DC)), ("k_prompt", (SEQ, DA), (1, 1, SEQ, H, HD)),
         ("v_prompt", (SEQ, DA), (1, 1, SEQ, H, HD)), ("lf_prompt", (SEQ, H), (1, 1, SEQ, H)),
         ("mk_prompt", (NMEM, XH * XD), (1, 1, NMEM, XH, XD)), ("mv_prompt", (NMEM, XH * XD), (1, 1, NMEM, XH, XD)),
         ("conv_sample", (DB * 2, DC), (1, DB, 2, DC)), ("k_sample", (NS, DA), (1, DB, DS, H, HD)),
         ("v_sample", (NS, DA), (1, DB, DS, H, HD)), ("lf_sample", (NS, H), (1, DB, DS, H))]


def lay_out(a):
    a = {k: np.asarray(v) for k, v in a.items()}
    out = {"consts": constants(), "revsel": rev_selectors()}
    out["x"] = np.concatenate([a["x_prompt"].reshape(SEQ, D), a["x_sample"].reshape(NS, D)])
    for k in ("cache_k", "cache_v"):
        out[k] = a[k].reshape(-1, PAGE, H * HD)
    out["cache_logf"] = a["cache_logf"].reshape(-1, PAGE * H)
    for k in ("cache_mem_k", "cache_mem_v"):
        out[k] = a[k].reshape(DB, NMEM, XH * XD)
    out["state_conv"] = a["state_conv"].reshape(DB * 2, DC)
    out["pages"] = a["page_table"].reshape(1, DB * PAGES)
    out["mem_prompt"] = a["mem_prompt"].reshape(NMEM, D)
    for k in ("norm_mix", "norm_xattn", "norm_mem", "norm_ffn", "norm_final"):
        out[k] = a[k].reshape(1, D)
    for k in ("w_in", "w_up_conv", "w_up_attn", "w_mix_out", "w_xq", "w_xk", "w_xv", "w_xo"):
        out[k] = a[k][0]
    for k in ("w_expert_gate", "w_expert_up", "w_expert_down"):
        out[k] = a[k][0]
    convp = np.zeros((P, 4 * KC + 1), np.float32)
    convp[:, :3 * KC] = a["conv_w"][0].reshape(3, KC, P).transpose(2, 0, 1).reshape(P, 3 * KC)
    convp[:, 3 * KC:4 * KC] = a["conv_b"][0].reshape(KC, P).T
    convp[:H, 4 * KC] = a["b_forget"][0]
    out["convp"] = convp
    out["w_router"] = np.concatenate([a["w_router_group"][0], a["w_router_expert"][0].transpose(1, 0, 2).reshape(D, NE)], 1)
    return {k: np.ascontiguousarray(v) for k, v in out.items()}


def kernel(**inputs):
    import concourse.bacc as bacc
    from concourse.bass_utils import run_bass_kernel_spmd

    nc = bacc.Bacc("TRN2", target_bir_lowering=False, num_devices=1)
    arrays = lay_out(inputs)
    t = {k: nc.dram_tensor("in_" + k, v.shape, mybir.dt.from_np(v.dtype), kind="ExternalInput").ap()
         for k, v in arrays.items()}
    for name, shape, _ in _OUTS:
        t[name] = nc.dram_tensor("out_" + name, shape, F32, kind="ExternalOutput").ap()
    build_program(nc, t)
    r = run_bass_kernel_spmd(nc, [{"in_" + k: v for k, v in arrays.items()}], core_ids=[0])
    return tuple(r.results[0]["out_" + name].reshape(shape) for name, _, shape in _OUTS)
```
